# Optimizing a Trainium2 kernel written in Bass

```python
import jax, jax.numpy as jnp
from jax import lax
import numpy as np

D_MODEL = 1024
BATCH = 1
SEQ = 1024
DEPTH = 2
DEC_BATCH = 1
DEC_SEQ = 32
PAST_LEN = 256

CHUNK = 64
HEAD_DIM = 64
SWA_HEADS = 8
SWA_KV_HEADS = 2
SWA_GROUP = SWA_HEADS // SWA_KV_HEADS
WINDOW = 128
WIN_CHUNKS = WINDOW // CHUNK
FOX_HEADS = 8
FOX_QBLK = 128
D_FF = 4 * D_MODEL
ROPE_THETA = 10000.0
EPS = 1e-6
SCALE = HEAD_DIM ** -0.5
W_QS = SWA_HEADS * HEAD_DIM
W_KS = SWA_KV_HEADS * HEAD_DIM
W_QF = FOX_HEADS * HEAD_DIM
SPLITS = tuple(np.cumsum([W_QS, W_KS, W_KS, W_QF, W_QF, W_QF]).tolist())
N_IN = SPLITS[-1] + FOX_HEADS
MIX_WIDTH = W_QS + W_QF

kernel_name = "hymba_swa_sink_fox_stream_step"

def rms_norm(x, g):
    xf = x.astype(jnp.float32)
    r = lax.rsqrt(jnp.mean(xf * xf, axis=-1, keepdims=True) + EPS)
    return (xf * r).astype(x.dtype) * g

def rope(x, pos):
    half = HEAD_DIM // 2
    inv_freq = ROPE_THETA ** (-jnp.arange(half, dtype=jnp.float32) / half)
    ang = pos.astype(jnp.float32)[:, None] * inv_freq[None, :]
    cos = jnp.cos(ang)[:, None, :]
    sin = jnp.sin(ang)[:, None, :]
    xf = x.astype(jnp.float32)
    x1, x2 = xf[..., :half], xf[..., half:]
    return jnp.concatenate([x1 * cos - x2 * sin, x2 * cos + x1 * sin], axis=-1).astype(x.dtype)

def adaln(c, w_ada, b_ada):
    mod = jnp.dot(jax.nn.silu(c), w_ada) + b_ada
    return jnp.split(mod[:, None, :], 6, axis=-1)

def project(h, w_in, b_forget, pos):
    B, S = h.shape[0], h.shape[1]
    z = jnp.dot(h, w_in)
    q_s, k_s, v_s, q_f, k_f, v_f, fg = jnp.split(z, SPLITS, axis=-1)
    q_s = rope(q_s.reshape(B, S, SWA_HEADS, HEAD_DIM), pos)
    k_s = rope(k_s.reshape(B, S, SWA_KV_HEADS, HEAD_DIM), pos)
    v_s = v_s.reshape(B, S, SWA_KV_HEADS, HEAD_DIM)
    q_f = q_f.reshape(B, S, FOX_HEADS, HEAD_DIM)
    k_f = k_f.reshape(B, S, FOX_HEADS, HEAD_DIM)
    v_f = v_f.reshape(B, S, FOX_HEADS, HEAD_DIM)
    logf = jax.nn.log_sigmoid((fg + b_forget).astype(jnp.float32))
    return q_s, k_s, v_s, q_f, k_f, v_f, logf

def sink_softmax(s, sink):
    m = jnp.maximum(jnp.max(s, axis=-1, keepdims=True), sink)
    p = jnp.exp(s - m)
    return p / (jnp.sum(p, axis=-1, keepdims=True) + jnp.exp(sink - m))

def swa_prompt(q, k, v, sinks):
    B, S = q.shape[0], q.shape[1]
    n_c = S // CHUNK
    pad = WIN_CHUNKS * CHUNK
    qc = q.reshape(B, n_c, CHUNK, SWA_KV_HEADS, SWA_GROUP, HEAD_DIM)
    kp = jnp.pad(k, ((0, 0), (pad, 0), (0, 0), (0, 0))).reshape(B, n_c + WIN_CHUNKS, CHUNK, SWA_KV_HEADS, HEAD_DIM)
    vp = jnp.pad(v, ((0, 0), (pad, 0), (0, 0), (0, 0))).reshape(B, n_c + WIN_CHUNKS, CHUNK, SWA_KV_HEADS, HEAD_DIM)
    kb = jnp.concatenate([kp[:, j:j + n_c] for j in range(WIN_CHUNKS + 1)], axis=2)
    vb = jnp.concatenate([vp[:, j:j + n_c] for j in range(WIN_CHUNKS + 1)], axis=2)
    kpos = (jnp.arange(n_c) * CHUNK - pad)[:, None] + jnp.arange((WIN_CHUNKS + 1) * CHUNK)[None, :]
    valid = kpos >= 0
    s = jnp.einsum('bcqhgd,bckhd->bchgqk', qc, kb).astype(jnp.float32) * SCALE
    s = jnp.where(valid[None, :, None, None, None, :], s, -jnp.inf)
    sink = sinks.astype(jnp.float32).reshape(SWA_KV_HEADS, SWA_GROUP)[None, None, :, :, None, None]
    p = sink_softmax(s, sink)
    o = jnp.einsum('bchgqk,bckhd->bcqhgd', p.astype(v.dtype), vb)
    return o.reshape(B, S, SWA_HEADS * HEAD_DIM)

def swa_sample(q, kk, vv, sinks):
    B, T = q.shape[0], q.shape[1]
    qg = q.reshape(B, T, SWA_KV_HEADS, SWA_GROUP, HEAD_DIM)
    s = jnp.einsum('bqhgd,bkhd->bhgqk', qg, kk).astype(jnp.float32) * SCALE
    sink = sinks.astype(jnp.float32).reshape(SWA_KV_HEADS, SWA_GROUP)[None, :, :, None, None]
    p = sink_softmax(s, sink)
    o = jnp.einsum('bhgqk,bkhd->bqhgd', p.astype(vv.dtype), vv)
    return o.reshape(B, T, SWA_HEADS * HEAD_DIM)

def fox_prompt(q, k, v, logf):
    B, S = q.shape[0], q.shape[1]
    n_q = S // FOX_QBLK
    F = jnp.cumsum(logf, axis=1)
    qb = q.reshape(B, n_q, FOX_QBLK, FOX_HEADS, HEAD_DIM).transpose(1, 0, 2, 3, 4)
    Fb = F.reshape(B, n_q, FOX_QBLK, FOX_HEADS).transpose(1, 0, 3, 2)
    Fk = F.transpose(0, 2, 1)
    kpos = jnp.arange(S)

    def block(args):
        qi, Fi, i = args
        s = jnp.einsum('bqhd,bkhd->bhqk', qi, k).astype(jnp.float32) * SCALE
        s = s + Fi[..., None] - Fk[:, :, None, :]
        qpos = i * FOX_QBLK + jnp.arange(FOX_QBLK)
        s = jnp.where(kpos[None, :] <= qpos[:, None], s, -jnp.inf)
        p = jax.nn.softmax(s, axis=-1)
        return jnp.einsum('bhqk,bkhd->bqhd', p.astype(v.dtype), v)

    o = lax.map(block, (qb, Fb, jnp.arange(n_q)))
    return o.transpose(1, 0, 2, 3, 4).reshape(B, S, FOX_HEADS * HEAD_DIM)

def fox_sample(q, kk, vv, lf):
    B, T = q.shape[0], q.shape[1]
    L = kk.shape[1]
    P = L - T
    F = jnp.cumsum(lf, axis=1).transpose(0, 2, 1)
    s = jnp.einsum('bqhd,bkhd->bhqk', q, kk).astype(jnp.float32) * SCALE
    s = s + F[:, :, P:, None] - F[:, :, None, :]
    mask = jnp.arange(L)[None, :] <= (P + jnp.arange(T))[:, None]
    s = jnp.where(mask, s, -jnp.inf)
    p = jax.nn.softmax(s, axis=-1)
    o = jnp.einsum('bhqk,bkhd->bqhd', p.astype(vv.dtype), vv)
    return o.reshape(B, T, FOX_HEADS * HEAD_DIM)

def mlp_sublayer(x, shift, scale, gate, g_pre, g_post, w_up, w_down):
    h = rms_norm(x, g_pre) * (1 + scale) + shift
    u = jnp.square(jax.nn.relu(jnp.dot(h, w_up)))
    return x + gate * rms_norm(jnp.dot(u, w_down), g_post)

def setup_inputs(seed: int = 0) -> dict:
    key = jax.random.key(seed)
    ks = jax.random.split(key, 24)
    f32 = jnp.float32
    keep = min(WINDOW, PAST_LEN)
    nrm = lambda k, shape, s=1.0: (jax.random.normal(k, shape, f32) * s).astype(f32)
    return {
        "x_prompt": nrm(ks[0], (BATCH, SEQ, D_MODEL)),
        "x_sample": nrm(ks[1], (DEC_BATCH, DEC_SEQ, D_MODEL)),
        "c_prompt": nrm(ks[2], (BATCH, D_MODEL)),
        "c_sample": nrm(ks[3], (DEC_BATCH, D_MODEL)),
        "cache_swa_k": nrm(ks[4], (DEPTH, DEC_BATCH, keep, SWA_KV_HEADS, HEAD_DIM)),
        "cache_swa_v": nrm(ks[5], (DEPTH, DEC_BATCH, keep, SWA_KV_HEADS, HEAD_DIM)),
        "cache_fox_k": nrm(ks[6], (DEPTH, DEC_BATCH, PAST_LEN, FOX_HEADS, HEAD_DIM)),
        "cache_fox_v": nrm(ks[7], (DEPTH, DEC_BATCH, PAST_LEN, FOX_HEADS, HEAD_DIM)),
        "cache_fox_logf": jax.nn.log_sigmoid(nrm(ks[8], (DEPTH, DEC_BATCH, PAST_LEN, FOX_HEADS)) + 2.0),
        "w_in": nrm(ks[9], (DEPTH, D_MODEL, N_IN), D_MODEL ** -0.5),
        "b_forget": 2.0 + nrm(ks[10], (DEPTH, FOX_HEADS), 0.5),
        "sinks": nrm(ks[11], (DEPTH, SWA_HEADS), 0.5),
        "w_out": nrm(ks[12], (DEPTH, MIX_WIDTH, D_MODEL), MIX_WIDTH ** -0.5),
        "w_up": nrm(ks[13], (DEPTH, D_MODEL, D_FF), D_MODEL ** -0.5),
        "w_down": nrm(ks[14], (DEPTH, D_FF, D_MODEL), D_FF ** -0.5),
        "w_ada": nrm(ks[15], (DEPTH, D_MODEL, 6 * D_MODEL), D_MODEL ** -0.5),
        "b_ada": nrm(ks[16], (DEPTH, 6 * D_MODEL), 0.01),
        "g_pre_mix": 1.0 + nrm(ks[17], (DEPTH, D_MODEL), 0.05),
        "g_post_mix": 1.0 + nrm(ks[18], (DEPTH, D_MODEL), 0.05),
        "g_pre_mlp": 1.0 + nrm(ks[19], (DEPTH, D_MODEL), 0.05),
        "g_post_mlp": 1.0 + nrm(ks[20], (DEPTH, D_MODEL), 0.05),
    }

def reference(x_prompt, x_sample, c_prompt, c_sample, cache_swa_k, cache_swa_v, cache_fox_k, cache_fox_v,
              cache_fox_logf, w_in, b_forget, sinks, w_out, w_up, w_down, w_ada, b_ada,
              g_pre_mix, g_post_mix, g_pre_mlp, g_post_mlp):
    S = x_prompt.shape[1]
    T = x_sample.shape[1]
    P = cache_fox_k.shape[2]
    keep = cache_swa_k.shape[2]
    pos_p = jnp.arange(S)
    pos_s = P + jnp.arange(T)
    xp, xs = x_prompt, x_sample
    p_sk, p_sv, p_fk, p_fv, p_fl = [], [], [], [], []
    s_sk, s_sv, s_fk, s_fv, s_fl = [], [], [], [], []
    for l in range(DEPTH):
        sh1, sc1, gt1, sh2, sc2, gt2 = adaln(c_prompt, w_ada[l], b_ada[l])
        h = rms_norm(xp, g_pre_mix[l]) * (1 + sc1) + sh1
        qs, kswa, vswa, qf, kf, vf, lf = project(h, w_in[l], b_forget[l], pos_p)
        o = jnp.concatenate([swa_prompt(qs, kswa, vswa, sinks[l]), fox_prompt(qf, kf, vf, lf)], axis=-1)
        xp = xp + gt1 * rms_norm(jnp.dot(o, w_out[l]), g_post_mix[l])
        xp = mlp_sublayer(xp, sh2, sc2, gt2, g_pre_mlp[l], g_post_mlp[l], w_up[l], w_down[l])
        p_sk.append(kswa[:, S - keep:])
        p_sv.append(vswa[:, S - keep:])
        p_fk.append(kf)
        p_fv.append(vf)
        p_fl.append(lf)
        sh1, sc1, gt1, sh2, sc2, gt2 = adaln(c_sample, w_ada[l], b_ada[l])
        h = rms_norm(xs, g_pre_mix[l]) * (1 + sc1) + sh1
        qs, kswa, vswa, qf, kf, vf, lf = project(h, w_in[l], b_forget[l], pos_s)
        kk_s = jnp.concatenate([cache_swa_k[l].astype(kswa.dtype), kswa], axis=1)
        vv_s = jnp.concatenate([cache_swa_v[l].astype(vswa.dtype), vswa], axis=1)
        kk_f = jnp.concatenate([cache_fox_k[l].astype(kf.dtype), kf], axis=1)
        vv_f = jnp.concatenate([cache_fox_v[l].astype(vf.dtype), vf], axis=1)
        lf_all = jnp.concatenate([cache_fox_logf[l].astype(jnp.float32), lf], axis=1)
        o = jnp.concatenate([swa_sample(qs, kk_s, vv_s, sinks[l]), fox_sample(qf, kk_f, vv_f, lf_all)], axis=-1)
        xs = xs + gt1 * rms_norm(jnp.dot(o, w_out[l]), g_post_mix[l])
        xs = mlp_sublayer(xs, sh2, sc2, gt2, g_pre_mlp[l], g_post_mlp[l], w_up[l], w_down[l])
        s_sk.append(kk_s[:, T:])
        s_sv.append(vv_s[:, T:])
        s_fk.append(kf)
        s_fv.append(vf)
        s_fl.append(lf)
    return (xp, xs,
            jnp.stack(p_sk), jnp.stack(p_sv), jnp.stack(p_fk), jnp.stack(p_fv), jnp.stack(p_fl),
            jnp.stack(s_sk), jnp.stack(s_sv), jnp.stack(s_fk), jnp.stack(s_fv), jnp.stack(s_fl))


_drawn_inputs = setup_inputs


def setup_inputs(seed=0):
    import zlib

    import numpy as np

    out = dict(_drawn_inputs(seed))
    spreads = {}
    factors = {'sinks': 8.0, 'b_ada': 2.828}
    for name, (base, spread) in spreads.items():
        noise = np.random.default_rng([zlib.crc32(name.encode()), seed]).standard_normal(out[name].shape)
        drawn = base * np.exp(spread * noise) if base else spread * noise
        out[name] = __import__('jax').numpy.asarray(drawn.astype(out[name].dtype))
    for name, factor in factors.items():
        out[name] = (out[name] * factor).astype(out[name].dtype)
    return out
```

```python
from contextlib import ExitStack

import numpy as np

import concourse.bass as bass
from concourse import mybir

ALU = mybir.AluOpType
ACT = mybir.ActivationFunctionType
AX = mybir.AxisListType
F32 = mybir.dt.float32
F32R = mybir.dt.float32r
BF16 = mybir.dt.bfloat16

P = 128
D = 1024
KT = D // P
SEQ, NEW = 1024, 32
TOK = SEQ + NEW
NCH = 3
CH = TOK // NCH
TT = SEQ // P
TAIL = TOK - P
NEWP = P - NEW
DEPTH = 2
HD = 64
NH_S, NKV, NH_F = 8, 2, 8
PAST, WIN = 256, 128
N_IN = 2312
SCALE = HD ** -0.5
EPS = 1e-6
NEG = -1e30
C_QS, C_KS, C_QF, C_KF, C_VF = 0, 512, 768, 1280, 1792
D_FF = 4 * D
HG = 4
MSTEPS = D_FF // (HG * P)
N_ADA = 6 * D // 256

N_TM, N_FM, N_WO, N_MLP = 5, 4, 4, 4
W_FM0, W_WO0 = N_TM, N_TM + N_FM
W_MLP0 = W_WO0 + N_WO
NW = W_MLP0 + N_MLP * MSTEPS
TM_COLS = [(C_KS, 256), (C_QS, 256), (C_QS + 256, 256), (C_VF, 256), (C_VF + 256, 264)]
SLOTW = KT * 264

FOX_ORDER = [6, 7, 4, 5, 2, 3, 0, 1]
NPRE1, NPOST1, NPRE2, NPOST2 = range(4)


def stream_pieces(c):
    a, b = c * CH, (c + 1) * CH
    out = [(a, min(b, SEQ), 0)]
    if b > SEQ:
        out.append((SEQ, b, 1))
    return out


def build(nc, a):
    ctx = ExitStack()
    with ctx:
        base = 16512

        def at(name, shape, dt, off):
            return nc.alloc_sbuf_tensor_at(name, shape, dt, offset=base + off)

        def sem(name):
            return ctx.enter_context(nc.semaphore(name))

        FM = KT * TOK * 4
        hh = at("hh", [P, KT, TOK], F32R, 0)
        hl = at("hl", [P, KT, TOK], F32R, FM)
        sq = at("sq", [P, KT, TOK], F32, 0)
        th = at("th", [P, KT, TOK], F32, FM)
        o = 2 * FM
        y = at("y", [P, KT, TOK], F32, o)
        xf = at("xf", [P, KT, TOK], F32, o + FM)
        uh = at("uh", [P, HG, TOK], F32R, o + FM)
        ul = at("ul", [P, HG, TOK], F32R, o + FM + FM // 2)
        mt = o + 2 * FM
        r_t = [at(f"r_t{i}", [P, CH], F32, mt + i * CH * 4) for i in range(2)]
        u_t = [at(f"u_t{i}", [P, CH], F32, mt + (2 + i) * CH * 4) for i in range(2)]
        rb = [at(f"rb{i}", [P, CH], F32, mt + 5632 + i * CH * 4) for i in range(2)]
        qs = at("qs", [P, 4, TOK], F32, o)
        ks = at("ks", [P, TOK], F32, o + 16896)
        vs = at("vs", [P, TT + 1, P], F32, o + 21120)
        qf = at("qf", [P, 4, TOK], F32, o + 25728)
        kf = at("kf", [P, 4, TOK], F32, o + 42624)
        vf = at("vf", [P, TT + 1, 512], F32, o + 59520)
        dz = o + 77952
        raw = [at(f"raw{i}", [P, SLOTW], F32, dz + i * SLOTW * 4) for i in range(2)]
        wh = [at(f"wh{i}", [P, SLOTW], F32R, dz + (2 + i) * SLOTW * 4) for i in range(2)]
        wl = [at(f"wl{i}", [P, SLOTW], F32R, dz + (4 + i) * SLOTW * 4) for i in range(2)]
        sz = dz + 6 * SLOTW * 4
        ro = [at(f"ro{i}", [P, 256], F32, sz + i * 1024) for i in range(2)]
        rt1 = at("rt1", [P, 256], F32, sz + 2048)
        rt2 = at("rt2", [P, 256], F32, sz + 3072)
        costab = at("costab", [P, TT + 1, 32], F32, sz + 4096)
        sintab = at("sintab", [P, TT + 1, 32], F32, sz + 5248)
        ko = [at(f"ko{i}", [P, 512], F32, sz + i * 2048) for i in range(2)]
        frow = at("frow", [NH_F, 2, SEQ], F32R, sz)
        pbuf = [at(f"pbuf{i}", [P, SEQ], F32, sz + i * 4096) for i in range(2)]
        sk1 = [at(f"sk1{i}", [P, SEQ], F32R, dz + i * 8192) for i in range(2)]
        sk2 = [at(f"sk2{i}", [P, SEQ], F32R, dz + 4096 + i * 8192) for i in range(2)]
        sq1 = [at(f"sq1{i}", [P, 4, P], F32R, dz + 16384 + i * 2048) for i in range(2)]
        spth = [at(f"spth{i}", [P, 2, 4, P], F32R, dz + 20480 + i * 8192) for i in range(2)]
        sptl = [at(f"sptl{i}", [P, 2, 4, P], F32R, dz + 24576 + i * 8192) for i in range(2)]
        svh = at("svh", [P, TT, 192], F32R, dz + 36864)
        svl = at("svl", [P, TT, 192], F32R, dz + 43008)
        fvh = at("fvh", [P, TT, 192], F32R, o)
        fvl = at("fvl", [P, TT, 192], F32R, o + 6144)
        q1 = [at("q1a", [P, SEQ], F32R, o + 12288), at("q1b", [P, SEQ], F32R, dz)]
        q2 = [at("q2a", [P, SEQ], F32R, o + 16384), at("q2b", [P, SEQ], F32R, dz + 4096)]
        k1 = [at("k1a", [P, SEQ], F32R, o + 20480), at("k1b", [P, SEQ], F32R, dz + 8192)]
        k2 = [at("k2a", [P, SEQ], F32R, dz + 12288), at("k2b", [P, SEQ], F32R, dz + 16384)]
        pth = [at(f"pth{i}", [P, 8 - 2 * i, 256], F32R, dz + 20480 + i * 16384) for i in range(2)]
        ptl = [at(f"ptl{i}", [P, 8 - 2 * i, 256], F32R, dz + 28672 + i * 14336) for i in range(2)]
        ckf = at("ckf", [P, 2, 512], F32, o)
        cvf = at("cvf", [P, 2, 512], F32, o + 4096)
        kft = at("kft", [P, 4, PAST + NEW], F32, o + 8192)
        cks = at("cks", [P, NKV, 2, HD], F32, o + 12800)
        cvs = at("cvs", [P, P], F32, o + 13824)
        kst = at("kst", [P, NKV, WIN + NEW], F32, o + 14336)
        aqs = at("aqs", [P, 8, NEW], F32, o + 15616)
        ap = at("ap", [P, PAST + NEW], F32, o + 16640)
        apt = at("apt", [P, 3, P], F32, o + 17792)
        fs = at("fs", [NH_F, PAST + NEW], F32, o + 19328)
        fsn = at("fsn", [NH_F, PAST + NEW], F32, o + 20480)
        cz = sz + 8192
        cpos = [cz]

        def small(name, shape, dt):
            n = int(np.prod(shape[1:])) * (2 if dt == BF16 else 4)
            t = nc.alloc_sbuf_tensor_at(name, shape, dt, offset=base + cpos[0])
            cpos[0] += (n + 31) // 32 * 32
            assert base + cpos[0] <= 229344, (name, cpos[0])
            return t

        ident = small("ident", [P, P], F32)
        onesd = small("onesd", [P, P], F32)
        tri = small("tri", [P, P], F32)
        cb = small("cb", [P, 512], BF16)
        identb = cb[:, 0:P]
        causb = cb[:, P:2 * P]
        winb = cb[:, 2 * P:4 * P]
        zerob = small("zerob", [P, P], BF16)
        vt = small("vt", [P, 80], F32)
        mod = small("mod", [P, 48, 2], F32)
        coef = small("coef", [P, 4, KT, 2], F32)
        sc = small("sc", [P, 2, KT], F32)
        sct = small("sct", [P, 3, 16], F32)
        snk = small("snk", [P, NH_S], F32)
        nsnk = small("nsnk", [P, NH_S], F32)
        ssnk = small("ssnk", [P, 2, 2], F32)
        bfg = small("bfg", [P, NH_F], F32)
        fg = small("fg", [P, TT + 1, NH_F], F32)
        fga = small("fga", [P, TT + 1, NH_F], F32)
        logf = small("logf", [P, TT + 1, NH_F], F32)
        lcum = small("lcum", [P, TT, NH_F], F32)
        lc = small("lc", [P, 2, NH_F], F32)
        lcs = small("lcs", [P, 2, NH_F], F32)
        qs_new = small("qs_new", [P, 4, NEW], F32)
        ks_new = small("ks_new", [P, NEW], F32)
        vs_new = small("vs_new", [P, P], F32)
        st = small("st", [P, 4, 20], F32)
        epst = small("epst", [P, 1], F32)
        vrow = at("vrow", [80, P], F32, sz + 6400)
        crow = at("crow", [16, P], F32, sz + 6912)
        xrow = [at(f"xrow{i}", [P, D], F32, i * 4096) for i in range(2)]
        orow = [at(f"orow{i}", [P, D], F32, i * 4096) for i in range(2)]
        cload = at("cload", [P, 3 * P], F32, dz)

        ps = nc.alloc_psum_tensor("ps", [P, 8, 512], F32)

        xd = nc.dram_tensor("x_kept", [P, KT, TOK], F32, kind="Internal").ap()
        fd = nc.dram_tensor("f_rows", [NH_F, 2, SEQ], F32, kind="Internal").ap()

        S = {}

        def sm(name):
            if name not in S:
                S[name] = sem(name)
            return S[name]

        def wait_apart(e, held, *waits):
            values = [e.to_reg(v) for _, v in waits]
            e.wait_ge(sm(held[0]), held[1])
            for (name, _), v in zip(waits, values):
                e.wait_ge(sm(name), v)

        for i in range(2):
            sm(f"xrow_in{i}"), sm(f"ada_in{i}"), sm(f"raw_in{i}"), sm(f"frow_in{i}"), sm(f"ko_out{i}"), sm(f"fin_out{i}")

        PJ = [("t", u, i) for u in range(N_TM) for i in range(TT + 1)] + \
             [("f", b, j, c) for b in range(N_FM) for j in range(2) for c in range(NCH)]
        NPJ = len(PJ)

        def by_act(it):
            return it[0] == "f" or it[1] in (0, 3, 4)

        def by_dve(it):
            return it[0] == "t" and it[1] != 3

        def n_act(q):
            return sum(by_act(x) for x in PJ[:q])

        def n_dve(q):
            return sum(by_dve(x) for x in PJ[:q])

        ROPES = [(u, i) for u in range(3) for i in range(TT + 1)]
        NR = len(ROPES)

        def w_view(t, n):
            if n < N_TM:
                w = TM_COLS[n][1]
                return t[:, 0:KT * w].rearrange("p (k n) -> p k n", k=KT)
            if n < W_MLP0 or (n - W_MLP0) % 4 < 2:
                return t[:, 0:KT * 256].rearrange("p (k n) -> p k n", k=KT)
            return t[:, 0:HG * 512].rearrange("p (k n) -> p k n", k=HG)

        def w_size(n):
            return KT * 264 if n == N_TM - 1 else KT * 256

        def slot_uses(n):
            return n // 2

        USES = [(NW + 1) // 2, NW // 2]

        NBT = [1 if FOX_ORDER[e % 8] < 4 else 2 for e in range(16)]
        BT = [sum(NBT[:e]) for e in range(17)]

        block = ctx.enter_context(nc.Block())

        @block.sync
        def _(sp):
            for n_, t in enumerate((ident, onesd, tri)):
                sp.dma_start(t[:, :], a["consts"][:, n_ * P:(n_ + 1) * P]).then_inc(sm("const_in"), 16)
            sp.dma_start(cload[:, :], a["consts"][:, 3 * P:6 * P]).then_inc(sm("const_in"), 16)
            sp.dma_start(crow[:, :], a["c_rows"]).then_inc(sm("c_in"), 16)
            for i in range(TT + 1):
                if i >= 2:
                    sp.wait_ge(sm("x_tr"), 2 * (i - 1))
                if i < TT:
                    sp.dma_start(xrow[i % 2][:, :], a["x_prompt"][i * P:(i + 1) * P, :]).then_inc(sm(f"xrow_in{i % 2}"), 16)
                else:
                    sp.dma_start(xrow[i % 2][0:NEW, :], a["x_sample"]).then_inc(sm(f"xrow_in{i % 2}"), 16)

            def load_w(l, n, src, wbase=None):
                wait_apart(sp, ("const_in", 64), ("w_lo", (l * NW + max(0, n - 1)) if wbase is None else wbase - 1))
                sp.dma_start(w_view(raw[n % 2], n), src).then_inc(sm(f"raw_in{n % 2}"), 16)

            with sp.Fori(0, DEPTH) as l:
                l1 = bass.ds(l, 1)
                sp.wait_ge(sm("x_ready"), l * 6 + 3)
                for t, n in ((vrow[0:48, :], "b_ada"), (vrow[48:80, :], "gains")):
                    sp.dma_start(t, a[n][l1, :, :].rearrange("l t p -> (l t) p")).then_inc(sm("vrow_in"), 16)
                for t, n in ((snk, "sinks_rows"), (bfg, "bf_rows")):
                    sp.dma_start(t[:, :], a[n][l1, :, :].rearrange("l p h -> (l p) h")).then_inc(sm("small_in"), 16)
                sp.dma_start(ssnk[:, 0, :], a["sinks_sample"][l1, :, :].rearrange("l p g -> (l p) g")).then_inc(sm("small_in"), 16)
                for t, n in ((costab, "cos"), (sintab, "sin")):
                    sp.dma_start(t[:, :, :], a[n].rearrange("p (i f) -> p i f", f=32)).then_inc(sm("small_in"), 16)
                sp.dma_start(lc[:, :, :], a["cache_fox_logf"][l1, :, :].rearrange("l (c p) h -> p (l c) h", p=P)).then_inc(sm("lcache_in"), 16)
                for n_, c_ in (("s_swa_k", "cache_swa_k"), ("s_swa_v", "cache_swa_v")):
                    sp.dma_start(a[n_][l1, 0:WIN - NEW, :], a[c_][l1, NEW:WIN, :]).then_inc(sm("cache_copied"), 16)
                wait_apart(sp, ("cb_ok", 1), ("w_lo", l * NW))
                with sp.Fori(0, N_ADA // 2) as ab:
                    for s in range(2):
                        sp.wait_ge(sm("ada_mm"), l * N_ADA + ab * 2 + s)
                        sp.dma_start(raw[s][:, 0:2048].rearrange("p (k n) -> p k n", k=KT),
                                     a["w_ada"][l1, :, bass.ds((ab * 2 + s) * 256, 256)].rearrange("l (k p) n -> p (l k) n", p=P)
                                     ).then_inc(sm(f"ada_in{s}"), 16)
                sp.wait_ge(sm("x_ready"), l * 6 + 3)
                sp.dma_start(xd, xf[:, :, :]).then_inc(sm("x_saved"), 16)
                sp.wait_ge(sm("ada_mm"), (l + 1) * N_ADA + 1)
                for n in range(N_TM + N_FM):
                    c0, w = TM_COLS[n] if n < N_TM else ((C_QF, 256), (C_QF + 256, 256), (C_KF, 256), (C_KF + 256, 256))[n - N_TM]
                    load_w(l, n, a["w_in"][l1, :, c0:c0 + w].rearrange("l (k p) n -> p (l k) n", p=P))
                    if n == 1:
                        wait_apart(sp, ("const_in", 64), ("rope_ok", l * NR + TT), ("ev_act", l * n_act(NPJ) + TT))
                        sp.dma_start(a["p_swa_k"][l1, :, :].rearrange("l p n -> (l p) n"), ro[(TT - 1) % 2][:, 0:P]).then_inc(sm("out_ks"), 16)
                        sp.dma_start(a["p_swa_v"][l1, :, :].rearrange("l p n -> (l p) n"), vs[:, TT - 1, :]).then_inc(sm("out_v"), 16)
                        wait_apart(sp, ("const_in", 64), ("rope_ok", l * NR + TT + 1), ("ev_act", l * n_act(NPJ) + TT + 1))
                        sp.dma_start(a["s_swa_k"][l1, WIN - NEW:WIN, :].rearrange("l p n -> (l p) n"), ro[TT % 2][NEWP:P, 0:P]).then_inc(sm("out_ks"), 16)
                        sp.dma_start(a["s_swa_v"][l1, WIN - NEW:WIN, :].rearrange("l p n -> (l p) n"), vs[NEWP:P, TT, :]).then_inc(sm("out_v"), 16)
                sp.wait_ge(sm("ev_act"), l * n_act(NPJ) + n_act(45))
                sp.dma_start(a["p_fox_v"][l1, :, :].rearrange("l (i p) n -> p (l i) n", p=P), vf[:, 0:TT, :]).then_inc(sm("out_v"), 16)
                sp.dma_start(a["s_fox_v"][l1, :, :].rearrange("l p n -> (l p) n"), vf[NEWP:P, TT, :]).then_inc(sm("out_v"), 16)
                sp.wait_ge(sm("logf_ok"), l + 1)
                sp.dma_start(a["p_fox_logf"][l1, :, :].rearrange("l (i p) n -> p (l i) n", p=P), logf[:, 0:TT, :]).then_inc(sm("out_small"), 16)
                sp.dma_start(a["s_fox_logf"][l1, :, :].rearrange("l p n -> (l p) n"), logf[NEWP:P, TT, :]).then_inc(sm("out_small"), 16)
                for i in range(TT + 1):
                    sp.wait_ge(sm("ko_ev"), l * (TT + 1) + i + 1)
                    if i < TT:
                        sp.dma_start(a["p_fox_k"][l1, i * P:(i + 1) * P, :].rearrange("l p n -> (l p) n"), ko[i % 2][:, :]).then_inc(sm(f"ko_out{i % 2}"), 16)
                    else:
                        sp.dma_start(a["s_fox_k"][l1, :, :].rearrange("l p n -> (l p) n"), ko[i % 2][NEWP:P, :]).then_inc(sm(f"ko_out{i % 2}"), 16)
                sp.wait_ge(sm("f_lo"), 2 * (l + 1))
                sp.dma_start(fd, frow[:, :, :].bitcast(F32)).then_inc(sm("f_kept"), 16)
                wait_apart(sp, ("const_in", 64), ("f_kept", (l + 1) * 16), ("fz_ok", 5 * (l + 1)))
                with sp.Fori(0, 4) as t:
                    for h in range(2):
                        sp.wait_ge(sm("fs_mm"), (l * 4 + t) * 16)
                        row = fd[bass.ds(t * 2 + h, 1), :, :].rearrange("h s n -> (h s) n")
                        sp.dma_start(k2[h][64:66, :].bitcast(F32), row).then_inc(sm(f"frow_in{h}"), 16)
                        sp.dma_start(q2[h][66:68, :].bitcast(F32), row).then_inc(sm(f"frow_in{h}"), 16)
                sp.wait_ge(sm("pv_mm"), (l + 1) * 4 * 8)
                cs = (a["cache_fox_k"], a["cache_fox_v"])
                for t, c_ in zip((ckf, cvf), cs):
                    sp.dma_start(t[:, :, :], c_[l1, :, :].rearrange("l (c p) n -> p (l c) n", p=P)).then_inc(sm("cache_in"), 16)
                for d in range(2):
                    sp.dma_start(cks[:, :, d, :], a["cache_swa_k"][l1, :, :].rearrange("l p (g e) -> (l p) g e", g=NKV)).then_inc(sm("cache_in"), 16)
                sp.dma_start(cvs[:, :], a["cache_swa_v"][l1, :, :].rearrange("l p n -> (l p) n")).then_inc(sm("cache_in"), 16)
                wait_apart(sp, ("const_in", 64), ("fo_lo", (l + 1) * 8))
                with sp.Fori(0, 2) as r:
                    for b in range(2):
                        n = W_WO0 + b
                        wb = sp.snap(l * NW + W_WO0 + r * 2 + b)
                        load_w(l, n, a["w_out"][l1, :, bass.ds((r * 2 + b) * 256, 256)].rearrange("l (k p) n -> p (l k) n", p=P), wb)
                sp.wait_ge(sm("ao_lo"), 2 * (l + 1))
                sp.dma_start(xf[:, :, :], xd).then_inc(sm("x_loaded"), 16)
                sp.wait_ge(sm("x_ready"), l * 6 + 6)
                sp.dma_start(xd, xf[:, :, :]).then_inc(sm("x_saved"), 16)
                with sp.Fori(0, MSTEPS) as m:
                    for b in range(4):
                        n = W_MLP0 + b
                        wb = sp.snap(l * NW + W_MLP0 + m * 4 + b)
                        if b < 2:
                            src = a["w_up"][l1, :, bass.ds((m * 2 + b) * 256, 256)].rearrange("l (k p) n -> p (l k) n", p=P)
                        else:
                            src = a["w_down"][l1, bass.ds(m * HG * P, HG * P), (b - 2) * 512:(b - 1) * 512].rearrange("l (k p) n -> p (l k) n", p=P)
                        load_w(l, n, src, wb)
                wait_apart(sp, ("const_in", 64), ("w_used", (l + 1) * NW), ("x_saved", (l + 1) * 32))
                sp.dma_start(xf[:, :, :], xd).then_inc(sm("x_loaded"), 16)
            for i in range(TT + 1):
                sp.wait_ge(sm("fin_ev"), 2 * (i + 1))
                if i < TT:
                    sp.dma_start(a["y_prompt"][i * P:(i + 1) * P, :], orow[i % 2][:, :]).then_inc(sm(f"fin_out{i % 2}"), 16)
                else:
                    sp.dma_start(a["y_sample"], orow[i % 2][NEWP:P, :]).then_inc(sm(f"fin_out{i % 2}"), 16)
            sp.wait_ge(sm("fin_out0"), 16 * 5)
            sp.wait_ge(sm("fin_out1"), 16 * 4)
            sp.wait_ge(sm("ko_out0"), 16 * DEPTH * 5)
            sp.wait_ge(sm("ko_out1"), 16 * DEPTH * 4)
            sp.wait_ge(sm("out_v"), 16 * DEPTH * 4)
            sp.wait_ge(sm("out_ks"), 16 * DEPTH * 2)
            sp.wait_ge(sm("out_small"), 16 * DEPTH * 2)
            sp.wait_ge(sm("cache_copied"), 16 * DEPTH * 2)
            sp.wait_ge(sm("x_saved"), 16 * DEPTH * 2)
            sp.wait_ge(sm("f_kept"), 16 * DEPTH)

        @block.gpsimd
        def _(pool):
            pool.memset(zerob[:, :], 0.0).then_inc(sm("zero_ok"), 1)
            pool.memset(epst[:, :], EPS).then_inc(sm("eps_ok"), 1)
            with pool.Fori(0, DEPTH) as l:
                wait_apart(pool, ("zero_ok", 1), ("w_used", l * NW + W_WO0))
                pool.memset(svh[:, :, 64:128].bitcast(F32), 0.0).then_inc(sm("sz_ok"), 1)
                pool.memset(svl[:, :, 64:128].bitcast(F32), 0.0).then_inc(sm("sz_ok"), 1)
                wait_apart(pool, ("zero_ok", 1), ("so_lo", (l + 1) * 16))
                pool.memset(fvh[:, :, 64:128].bitcast(F32), 0.0)
                pool.memset(fvl[:, :, 64:128].bitcast(F32), 0.0).then_inc(sm("fz_ok"), 1)
                n = 1
                for h in range(2):
                    for stack, value in ((k2, 1.0), (q2, -1.0)):
                        wait_apart(pool, ("zero_ok", 1), ("fz_ok", l * 5 + n))
                        pool.memset(stack[h][64:68, :].bitcast(F32), value).then_inc(sm("fz_ok"), 1)
                        n += 1
                wait_apart(pool, ("zero_ok", 1), ("x_ready", l * 6 + 6))
                pool.memset(y[:, :, :], 0.0).then_inc(sm("y_zero"), 1)

        @block.scalar
        def _(act):
            def copy(out, in_, **kw):
                return act.activation(out, in_, ACT.Copy, **kw)

            act.wait_ge(sm("c_tr"), 1)
            act.activation(sct[:, 0, :], ps[:, 7, 0:16], ACT.Exp, scale=-1.0).then_inc(sm("silu_a"), 1)
            act.wait_ge(sm("eps_ok"), 1)
            for i in range(TT + 1):
                for hf in range(2):
                    q = 2 * i + hf
                    act.wait_ge(sm("x_tr"), q + 1)
                    w = P if i < TT else NEW
                    ins = copy(xf[:, 4 * hf:4 * hf + 4, i * P:i * P + w],
                               ps[:, q % 2, 0:4 * w].rearrange("p (t n) -> p t n", t=4))
                    ins.then_inc(*((sm("x_ready"), NCH) if q == 2 * TT + 1 else (sm("x_put"), 1)))

            def split_hi(l, n, wb=None):
                w = w_size(n)
                if wb is None:
                    act.wait_ge(sm("w_used"), l * NW + max(0, n - 1))
                    act.wait_ge(sm(f"raw_in{n % 2}"), (l * USES[n % 2] + slot_uses(n) + 1) * 16)
                else:
                    cnt, used = wb
                    act.wait_ge(sm("w_used"), used)
                    act.wait_ge(sm(f"raw_in{n % 2}"), cnt)
                copy(wh[n % 2][:, 0:w], raw[n % 2][:, 0:w]).then_inc(sm("w_hi"), 1)

            def norm_rb(idx, c):
                act.wait_ge(sm("mean_ok"), idx + 1)
                act.wait_ge(sm("nt_ok"), idx if c == 0 else idx - 1)
                act.activation(rb[c % 2][:, :], ps[:, 4 + c % 2, 0:CH], ACT.Ln, bias=epst[:, 0:1]).then_inc(sm("ln_ok"), 1)
                act.wait_ge(sm("ln_ok"), idx + 1)
                act.activation(rb[c % 2][:, :], rb[c % 2][:, :], ACT.Exp, scale=-0.5).then_inc(sm("rb_ok"), 1)

            def pre_norm(l, nu):
                pn = 0 if nu == NPRE1 else 1
                for c in range(NCH):
                    cs = slice(c * CH, (c + 1) * CH)
                    idx = l * 12 + nu * 3 + c
                    act.wait_ge(sm("x_ready"), l * 6 + 3 + (3 if pn else 0) - 2 + c)
                    act.activation(sq[:, :, cs], xf[:, :, cs], ACT.Square).then_inc(sm("sq_ok"), 1)
                    norm_rb(idx, c)
                    act.wait_ge(sm("h_full"), l * 6 + pn * 3 + c + 1)
                    copy(hh[:, :, cs], th[:, :, cs]).then_inc(sm("h_hi"), 1)

            with act.Fori(0, DEPTH) as l:
                pre_norm(l, NPRE1)
                split_hi(l, 0)
                split_hi(l, 1)
                act.wait_ge(sm("x_saved"), l * 32 + 16)
                nr = 0
                for q, it in enumerate(PJ):
                    if it[0] == "t":
                        _, u, i = it
                        b = q % 4
                        if by_act(it):
                            act.wait_ge(sm("pj_mm"), l * NPJ + q + 1)
                            if u == 0:
                                act.wait_ge(sm("rope_t"), l * NR + i + 1)
                            elif u == 4:
                                act.wait_ge(sm("fg_a"), l * 10 + i + 1)
                            if u == 0:
                                copy(vs[:, i, :], ps[:, b, P:256]).then_inc(sm("ev_act"), 1)
                            else:
                                copy(vf[:, i, (u - 3) * 256:(u - 2) * 256], ps[:, b, 0:256]).then_inc(sm("ev_act"), 1)
                        if u < 3:
                            act.wait_ge(sm("rtr_mm"), l * NR + nr + 1)
                            w0, w1 = (0, P) if i < TT else (NEWP, P)
                            n_ = 1 if u == 0 else 2
                            src = ps[:, 4 + nr % 2, 0:n_ * P].rearrange("p (t n) -> p t n", t=n_)[:, :, w0:w1]
                            dst = (ks[:, None, i * P:i * P + w1 - w0] if u == 0
                                   else qs[:, 2 * (u - 1):2 * u, i * P:i * P + w1 - w0])
                            copy(dst, src).then_inc(sm("rtr_ev"), 1)
                            nr += 1
                        if i == TT and u + 2 < N_TM + N_FM:
                            split_hi(l, u + 2)
                    else:
                        _, blk, j, c = it
                        act.wait_ge(sm("pj_mm"), l * NPJ + q + 1)
                        dst = (qf, kf)[blk // 2]
                        copy(dst[:, 2 * (blk % 2) + j, c * CH:(c + 1) * CH], ps[:, q % 4, 0:CH]).then_inc(sm("ev_act"), 1)
                        if j == 1 and c == NCH - 1 and N_TM + blk + 2 < W_WO0:
                            split_hi(l, N_TM + blk + 2)
                act.wait_ge(sm("fg_a"), l * 10 + 10)
                act.activation(fga[:, :, :], fga[:, :, :], ACT.Exp, scale=-1.0).then_inc(sm("fg_b"), 1)
                act.wait_ge(sm("fg_b"), 2 * l + 1)
                act.activation(fga[:, :, :], fga[:, :, :], ACT.Ln, bias=1.0).then_inc(sm("fg_b"), 1)
                for i in range(TT + 1):
                    act.wait_ge(sm("ko_mm"), l * (TT + 1) + i + 1)
                    if i == 0:
                        act.wait_ge(sm("rtr_mm"), (l + 1) * NR)
                        act.wait_ge(sm("out_ks"), (l + 1) * 32)
                        act.wait_ge(sm("rope_ok"), (l + 1) * NR)
                    if i >= 2:
                        act.wait_ge(sm(f"ko_out{i % 2}"), (l * (5 - i % 2) + i // 2) * 16)
                    copy(ko[i % 2][:, :], ps[:, 6 + i % 2, :]).then_inc(sm("ko_ev"), 1)
                act.wait_ge(sm("f_mm"), l + 1)
                act.wait_ge(sm("ko_out0"), (l + 1) * 5 * 16)
                act.wait_ge(sm("ko_out1"), (l + 1) * 4 * 16)
                for b in range(2):
                    copy(frow[:, 0, b * 512:(b + 1) * 512], ps[0:NH_F, b, :]).then_inc(sm("f_hi"), 1)
                act.wait_ge(sm("ev_act"), (l + 1) * n_act(NPJ))
                act.wait_ge(sm("rtr_ev"), (l + 1) * NR)
                copy(qs_new[:, :, :], qs[:, :, SEQ:TOK]).then_inc(sm("new_kept"), 1)
                copy(ks_new[:, :], ks[:, SEQ:TOK]).then_inc(sm("new_kept"), 1)
                copy(vs_new[:, :], vs[:, TT, :]).then_inc(sm("new_kept"), 1)

                def k_hi(g):
                    r = slice(64 * g, 64 * g + 64)
                    copy(sk1[g][0:64, :], ks[r, 0:SEQ]).then_inc(sm("sk_hi"), 1)
                    copy(sk1[g][64:128, :], ks[r, 0:SEQ]).then_inc(sm("sk_hi"), 1)

                def v_hi(g):
                    if g == 1:
                        act.wait_ge(sm("so_mm"), l * 16 + 8)
                    dst = svh[:, :, :].rearrange("p t (a n) -> p t a n", n=64)[:, :, 0:3:2, :]
                    src = vs[:, 0:TT, None, 64 * g:64 * g + 64].broadcast_to([P, TT, 2, 64])
                    copy(dst, src).then_inc(sm("sv_hi"), 1)

                def q_hi(w):
                    g, i = w // 8, w % 8
                    if w >= 2:
                        act.wait_ge(sm("s_mm"), l * 16 + w - 1)
                    for d in range(2):
                        r = slice(64 * d, 64 * d + 64)
                        copy(sq1[w % 2][r, d:4:2, :], qs[r, 2 * g:2 * g + 2, i * P:(i + 1) * P], scale=SCALE).then_inc(sm("sq_hi"), 1)

                def expo(w):
                    W = P if w % 8 == 0 else 256
                    s4 = st[:, w % 4, :]
                    act.wait_ge(sm("s_mn"), l * 16 + w + 1)
                    if w >= 2:
                        act.wait_ge(sm("st_mm"), l * 16 + w - 1)
                    else:
                        act.wait_ge(sm("f_kept"), (l + 1) * 16)
                    for x in range(4):
                        ins = act.activation(pbuf[w % 2][:, x * W:(x + 1) * W],
                                             ps[:, 2 * (w % 2) + x // 2, (x % 2) * 256:(x % 2) * 256 + W], ACT.Exp,
                                             bias=s4[:, 4 + x:5 + x], accum_out=s4[:, 8 + x:9 + x])
                    ins.then_inc(sm("s_exp"), 1)
                    act.wait_ge(sm("s_smx"), l * 16 + w + 1)
                    act.activation(s4[:, 12:16], s4[:, 12:16], ACT.Exp).then_inc(sm("s_es"), 1)

                def pt_hi(w):
                    nk = 1 if w % 8 == 0 else 2
                    act.wait_ge(sm("st_mm"), l * 16 + w + 1)
                    if w >= 2:
                        act.wait_ge(sm("so_mm"), l * 16 + w - 1)
                    copy(spth[w % 2][:, 0:nk, :, :],
                         ps[:, 4:4 + nk, :].rearrange("p k (h n) -> p k h n", h=4)).then_inc(sm("st_hi"), 1)

                def o_hi(w):
                    g, i = w // 8, w % 8
                    act.wait_ge(sm("so_mm"), l * 16 + w + 1)
                    copy(hh[:, 2 * g:2 * g + 2, i * P:(i + 1) * P],
                         ps[:, 6 + w % 2, 0:256].rearrange("p (t n) -> p t n", t=2)).then_inc(sm("so_hi"), 1)

                act.wait_ge(sm("w_used"), l * NW + W_WO0)
                k_hi(0)
                for w in range(-2, 17):
                    if 0 <= w + 2 < 16:
                        q_hi(w + 2)
                    if 0 <= w + 1 < 16:
                        expo(w + 1)
                    if 0 <= w < 16:
                        pt_hi(w)
                    if 0 <= w - 1 < 16:
                        o_hi(w - 1)
                    if w == -1:
                        v_hi(0)
                    if w == 0:
                        k_hi(1)
                    if w == 8:
                        v_hi(1)

                act.wait_ge(sm("so_lo"), (l + 1) * 16)
                act.wait_ge(sm("fz_ok"), 5 * (l + 1))
                with act.Fori(0, 4) as t:
                    pr = act.snap(l * 4 + t)

                    def stacks_hi(h):
                        r = slice(64 * h, 64 * h + 64)
                        t1 = bass.ds(t, 1)
                        qsrc = qf[r, t1, 0:SEQ].rearrange("p t n -> p (t n)")
                        ksrc = kf[r, t1, 0:SEQ].rearrange("p t n -> p (t n)")
                        act.wait_ge(sm("fs_mm"), pr * 16)
                        copy(q1[h][r, :], qsrc, scale=SCALE).then_inc(sm("fq_hi"), 1)
                        copy(q2[h][0:64, :], qsrc, scale=SCALE).then_inc(sm("fq_hi"), 1)
                        copy(k1[h][0:64, :], ksrc).then_inc(sm("fq_hi"), 1)
                        copy(k1[h][64:128, :], ksrc).then_inc(sm("fq_hi"), 1)

                    def expo(e):
                        i = FOX_ORDER[e % 8]
                        n, nb = (i + 1) * P, (1 if i < 4 else 2)
                        s4 = st[:, e % 4, :]
                        act.wait_ge(sm("fs_nm"), pr * 16 + e + 1)
                        act.wait_ge(sm("ft_mm"), pr * 24 + BT[max(0, e - 1)])
                        act.activation(pbuf[e % 2][:, 0:n].rearrange("p (c n) -> p c n", c=nb),
                                       ps[:, 2 * (e % 2):2 * (e % 2) + nb, 0:n // nb], ACT.Exp,
                                       bias=s4[:, 0:1], accum_out=s4[:, 1:2]).then_inc(sm("fs_exp"), 1)

                    def pt_hi(e):
                        i = FOX_ORDER[e % 8]
                        jb = (e // 2) % 2
                        act.wait_ge(sm("pv_mm"), pr * 8 + max(0, e // 2 - 1))
                        for bb in range(NBT[e]):
                            g = BT[e] + bb
                            k0, k1_ = 4 * bb, min(4 * bb + 4, i + 1)
                            act.wait_ge(sm("ft_mm"), pr * 24 + g + 1)
                            copy(pth[jb][:, k0:k1_, (i % 2) * P:(i % 2 + 1) * P],
                                 ps[:, 4 + g % 2, 0:(k1_ - k0) * P].rearrange("p (k n) -> p k n", n=P)).then_inc(sm("ft_hi"), 1)

                    def o_hi(b):
                        act.wait_ge(sm("pv_mm"), pr * 8 + (6, 8)[b])
                        c0 = (512, 0)[b]
                        copy(hh[:, bass.ds(t + 4, 1), c0:c0 + 512].rearrange("p t n -> p (t n)"),
                             ps[:, 6 + b, :]).then_inc(sm("fo_hi"), 1)

                    stacks_hi(0)
                    act.wait_ge(sm("pv_mm"), pr * 8)
                    vdst = fvh[:, :, :].rearrange("p t (a n) -> p t a n", n=64)[:, :, 0:3:2, :]
                    vsrc = vf[:, 0:TT, bass.ds(t * P, P)].rearrange("p t (a n) -> p t a n", n=64)
                    copy(vdst, vsrc).then_inc(sm("fv_hi"), 1)
                    for e in range(-1, 16):
                        if e + 1 < 16:
                            expo(e + 1)
                        if e == 1:
                            stacks_hi(1)
                        if e >= 0:
                            pt_hi(e)
                        if e == 13:
                            o_hi(0)
                    o_hi(1)

                act.wait_ge(sm("ck_tr"), l + 1)
                act.wait_ge(sm("new_kept"), 3 * (l + 1))
                for c in range(2):
                    copy(kft[:, :, c * P:(c + 1) * P], ps[:, c, :].rearrange("p (t n) -> p t n", t=4))
                copy(kft[:, :, PAST:], kf[:, :, SEQ:TOK])
                copy(kst[:, :, 0:WIN], ps[:, 2, 0:256].rearrange("p (g n) -> p g n", g=2))
                for g in range(2):
                    for d in range(2):
                        copy(kst[64 * d:64 * d + 64, g, WIN:], ks_new[64 * g:64 * g + 64, :])
                copy(fs[:, :], ps[0:NH_F, 3, 0:PAST + NEW])
                copy(fsn[:, :], ps[0:NH_F, 3, 0:PAST + NEW], scale=-1.0).then_inc(sm("ck_ev"), 1)
                copy(aqs[:, 0:4, :], qs_new[:, :, :], scale=SCALE).then_inc(sm("aq_ok"), 1)
                copy(aqs[:, 4:8, :], qf[:, :, SEQ:TOK], scale=SCALE).then_inc(sm("aq_ok"), 1)
                for w in range(4):
                    W = WIN + NEW if w < 2 else PAST + NEW
                    s4 = st[:, w, :]
                    act.wait_ge(sm("a_mn"), l * 4 + w + 1)
                    if w >= 1:
                        act.wait_ge(sm("at_mm"), l * 4 + w)
                    act.activation(ap[:, 0:W], ps[:, w % 2, 0:W], ACT.Exp, bias=s4[:, 1:2], accum_out=s4[:, 2:3]).then_inc(sm("a_exp"), 1)
                    if w < 2:
                        act.wait_ge(sm("a_smx"), l * 2 + w + 1)
                        act.activation(s4[:, 3:4], s4[:, 3:4], ACT.Exp).then_inc(sm("a_es"), 1)
                    act.wait_ge(sm("at_mm"), l * 4 + w + 1)
                    if w >= 1:
                        act.wait_ge(sm("ao_mm"), l * 4 + w)
                    copy(apt[:, 0:2 if w < 2 else 3, :],
                         ps[:, 2, 0:P * (2 if w < 2 else 3)].rearrange("p (k n) -> p k n", n=P)).then_inc(sm("at_ev"), 1)
                    if w % 2:
                        act.wait_ge(sm("ao_mm"), l * 4 + w + 1)
                        t0 = 0 if w < 2 else 4
                        copy(hh[:, t0:t0 + 4, SEQ:TOK], ps[:, 3, 0:P].rearrange("p (t n) -> p t n", t=4)).then_inc(sm("ao_hi"), 1)

                act.wait_ge(sm("ao_lo"), 2 * (l + 1))
                with act.Fori(0, 2) as r:
                    n0 = act.snap(l * NW + W_WO0 + r * 2)
                    split_hi(l, W_WO0, ((l * USES[W_WO0 % 2] + slot_uses(W_WO0) + r + 1) * 16, n0 - 1))
                    split_hi(l, W_WO0 + 1, ((l * USES[1 - W_WO0 % 2] + slot_uses(W_WO0 + 1) + r + 1) * 16, n0))
                    for b in range(2):
                        for j in range(2):
                            for c in range(NCH):
                                q = b * 6 + j * 3 + c
                                act.wait_ge(sm("y_mm"), l * 24 + r * 12 + q + 1)
                                copy(y[:, bass.ds(r * 4 + b * 2 + j, 1), c * CH:(c + 1) * CH].rearrange("p t n -> p (t n)"),
                                     ps[:, q % 6, 0:CH]).then_inc(sm("y_ev"), 1)

                def post_norm_act(nu, ready, value):
                    for c in range(NCH):
                        cs = slice(c * CH, (c + 1) * CH)
                        idx = l * 12 + nu * 3 + c
                        act.wait_ge(sm(ready), value)
                        if c == 0 and nu == NPOST1:
                            act.wait_ge(sm("w_used"), l * NW + W_MLP0)
                        act.activation(sq[:, :, cs], y[:, :, cs], ACT.Square).then_inc(sm("sq_ok"), 1)
                        norm_rb(idx, c)

                post_norm_act(NPOST1, "y_ev", (l + 1) * 24)
                pre_norm(l, NPRE2)
                act.wait_ge(sm("x_saved"), (l + 1) * 32)
                with act.Fori(0, MSTEPS) as m:
                    mm = act.snap(l * MSTEPS + m)
                    n0 = act.snap(l * NW + W_MLP0 + m * 4)
                    sl = [act.snap(l * USES[(W_MLP0 + s_) % 2] + slot_uses(W_MLP0 + s_) + m * 2) for s_ in range(2)]

                    def split(b):
                        split_hi(l, W_MLP0 + b, ((sl[b % 2] + (b // 2 + 1)) * 16, n0 + (b - 1)))

                    def u_hi(q):
                        c = q % 3
                        act.wait_ge(sm("u_sq"), mm * 12 + q + 1)
                        if q == 0:
                            act.wait_ge(sm("w_used"), n0)
                        copy(uh[:, q // 3, c * CH:(c + 1) * CH], u_t[q % 2][:, :]).then_inc(sm("u_hi"), 1)

                    split(0)
                    split(1)
                    for q in range(12):
                        if q == 6:
                            split(2)
                        act.wait_ge(sm("u_mm"), mm * 12 + q + 1)
                        act.wait_ge(sm("u_sq"), mm * 12 + max(0, q - 1))
                        act.activation(r_t[q % 2][:, :], ps[:, q % 4, 0:CH], ACT.Relu).then_inc(sm("u_relu"), 1)
                        if q >= 1:
                            u_hi(q - 1)
                    u_hi(11)
                    split(3)
                post_norm_act(NPOST2, "d_add", (l + 1) * MSTEPS * 24)

            for i in range(TT + 1):
                for hf in range(2):
                    q = 2 * i + hf
                    act.wait_ge(sm("fin_tr"), q + 1)
                    if i >= 2 and hf == 0:
                        act.wait_ge(sm(f"fin_out{i % 2}"), (i // 2) * 16)
                    copy(orow[i % 2][:, hf * 512:(hf + 1) * 512], ps[:, q % 2, :]).then_inc(sm("fin_ev"), 1)

        @block.vector
        def _(dve):
            dve.wait_ge(sm("const_in"), 64)
            dve.tensor_copy(cb[:, 0:P], ident[:, :])
            dve.tensor_copy(cb[:, P:4 * P], cload[:, :]).then_inc(sm("cb_ok"), 1)
            dve.wait_ge(sm("silu_a"), 1)
            dve.tensor_scalar(sct[:, 1, :], sct[:, 0, :], 1.0, None, ALU.add).then_inc(sm("silu_b"), 1)
            dve.wait_ge(sm("silu_b"), 1)
            dve.reciprocal(sct[:, 2, :], sct[:, 1, :]).then_inc(sm("silu_b"), 1)
            dve.wait_ge(sm("silu_b"), 2)
            dve.tensor_tensor(sc[:, :, :].rearrange("p s k -> p (s k)"), ps[:, 7, 0:16], sct[:, 2, :], ALU.mult).then_inc(sm("silu_b"), 1)

            def split_lo(l, n, n0=None):
                w = w_size(n)
                dve.wait_ge(sm("w_hi"), (l * NW + n + 1) if n0 is None else n0 + 1)
                dve.tensor_tensor(wl[n % 2][:, 0:w], raw[n % 2][:, 0:w], wh[n % 2][:, 0:w].bitcast(F32), ALU.subtract).then_inc(sm("w_lo"), 1)

            def pre_norm(l, nu):
                pn = 0 if nu == NPRE1 else 1
                b0 = 24 * pn
                for c in range(NCH):
                    cs = slice(c * CH, (c + 1) * CH)
                    idx = l * 12 + nu * 3 + c
                    dve.wait_ge(sm("rb_ok"), idx + 1)
                    dve.tensor_tensor(th[:, :, cs], xf[:, :, cs], rb[c % 2][:, None, :].broadcast_to([P, KT, CH]), ALU.mult).then_inc(sm("nt_ok"), 1)
                    dve.wait_ge(sm("nt_ok"), idx + 1)
                    for k in range(KT):
                        for (c0, c1, s_) in stream_pieces(c):
                            ins = dve.tensor_scalar(th[:, k, c0:c1], th[:, k, c0:c1], coef[:, 2 * pn, k, s_:s_ + 1],
                                                    mod[:, b0 + k, s_:s_ + 1], ALU.mult, ALU.add)
                    ins.then_inc(sm("h_full"), 1)
                    dve.wait_ge(sm("h_hi"), l * 6 + pn * 3 + c + 1)
                    dve.tensor_tensor(hl[:, :, cs], th[:, :, cs], hh[:, :, cs].bitcast(F32), ALU.subtract).then_inc(sm("h_ok"), 1)

            def post_norm(l, nu):
                pn = 0 if nu == NPOST1 else 1
                for c in range(NCH):
                    cs = slice(c * CH, (c + 1) * CH)
                    idx = l * 12 + nu * 3 + c
                    dve.wait_ge(sm("rb_ok"), idx + 1)
                    dve.tensor_tensor(y[:, :, cs], y[:, :, cs], rb[c % 2][:, None, :].broadcast_to([P, KT, CH]), ALU.mult).then_inc(sm("nt_ok"), 1)
                    dve.wait_ge(sm("nt_ok"), idx + 1)
                    dve.wait_ge(sm("x_loaded"), l * 32 + 16 * (pn + 1))
                    for k in range(KT):
                        for (c0, c1, s_) in stream_pieces(c):
                            ins = dve.scalar_tensor_tensor(out=xf[:, k, c0:c1], in0=y[:, k, c0:c1], scalar=coef[:, 2 * pn + 1, k, s_:s_ + 1],
                                                           in1=xf[:, k, c0:c1], op0=ALU.mult, op1=ALU.add)
                    ins.then_inc(sm("x_ready"), 1)

            with dve.Fori(0, DEPTH) as l:
                dve.wait_ge(sm("v_tr"), l + 1)
                dve.tensor_copy(vt[:, :], ps[:, 5, 0:80]).then_inc(sm("vt_ok"), 1)
                dve.wait_ge(sm("vt_ok"), l + 1)
                dve.wait_ge(sm("small_in"), (l + 1) * 80)
                dve.tensor_scalar(nsnk[:, :], snk[:, :], -1.0, None, ALU.mult)
                dve.tensor_scalar(ssnk[:, 1, :], ssnk[:, 0, :], -1.0, None, ALU.mult).then_inc(sm("nsnk_ok"), 1)
                dve.wait_ge(sm("lcache_in"), (l + 1) * 16)
                dve.tensor_scalar(lcs[:, 0, :], lc[:, 0, :], float(D), None, ALU.mult).then_inc(sm("lcs_ok"), 1)
                dve.wait_ge(sm("lcs_ok"), 2 * l + 1)
                dve.scalar_tensor_tensor(out=lcs[:, 1, :], in0=lc[:, 1, :], scalar=float(D), in1=lcs[:, 0, :], op0=ALU.mult, op1=ALU.add).then_inc(sm("lcs_ok"), 1)
                with dve.Fori(0, N_ADA // 2) as ab:
                    for s in range(2):
                        dve.wait_ge(sm("ada_mm"), l * N_ADA + ab * 2 + s + 2)
                        dve.tensor_tensor(mod[:, bass.ds(ab * 4 + 2 * s, 2), :], ps[:, 6 + s, 0:4].rearrange("p (j s) -> p j s", j=2),
                                          vt[:, bass.ds(ab * 4 + 2 * s, 2)][:, :, None].broadcast_to([P, 2, 2]), ALU.add).then_inc(sm("ada_ev"), 1)
                dve.wait_ge(sm("ada_ev"), (l + 1) * N_ADA)
                for n_, (m0, add) in enumerate(((8, 1.0), (16, 0.0), (32, 1.0), (40, 0.0))):
                    ins = dve.scalar_tensor_tensor(out=coef[:, n_, :, :], in0=mod[:, m0:m0 + KT, :], scalar=add,
                                                   in1=vt[:, 48 + 8 * n_:56 + 8 * n_][:, :, None].broadcast_to([P, KT, 2]), op0=ALU.add, op1=ALU.mult)
                ins.then_inc(sm("coef_ok"), 1)
                dve.wait_ge(sm("coef_ok"), l + 1)
                pre_norm(l, NPRE1)

                split_lo(l, 0)
                split_lo(l, 1)
                nr = 0
                for q, it in enumerate(PJ):
                    if it[0] == "f":
                        _, blk, j, c = it
                        if j == 1 and c == NCH - 1 and N_TM + blk + 2 < W_WO0:
                            split_lo(l, N_TM + blk + 2)
                        continue
                    _, u, i = it
                    b = q % 4
                    if u < 3:
                        nh = 2 if u == 0 else 4
                        src = ps[:, b, 0:nh * HD].rearrange("p (h s f) -> p h s f", h=nh, s=2)
                        t1 = rt1[:, 0:nh * HD].rearrange("p (h s f) -> p h s f", h=nh, s=2)
                        t2 = rt2[:, 0:nh * HD].rearrange("p (h s f) -> p h s f", h=nh, s=2)
                        dst = ro[nr % 2][:, 0:nh * HD].rearrange("p (h s f) -> p h s f", h=nh, s=2)
                        cos2 = costab[:, i, None, :].broadcast_to([P, nh * 2, 32])
                        sin1 = sintab[:, i, None, :].broadcast_to([P, nh, 32])
                        dve.wait_ge(sm("pj_mm"), l * NPJ + q + 1)
                        dve.wait_ge(sm("rope_ok"), l * NR + nr)
                        dve.tensor_tensor(rt1[:, 0:nh * HD].rearrange("p (h f) -> p h f", f=32),
                                          ps[:, b, 0:nh * HD].rearrange("p (h f) -> p h f", f=32), cos2, ALU.mult)
                        dve.tensor_tensor(t2[:, :, 0, :], src[:, :, 1, :], sin1, ALU.mult)
                        dve.tensor_tensor(t2[:, :, 1, :], src[:, :, 0, :], sin1, ALU.mult).then_inc(sm("rope_t"), 1)
                        n_wait = l * NR + nr + 1
                        dve.wait_ge(sm("rope_t"), n_wait)
                        if nr >= 2:
                            dve.wait_ge(sm("rtr_mm"), l * NR + nr - 1)
                        if u == 1 and i < 2:
                            dve.wait_ge(sm("out_ks"), (l + 1) * 32)
                        dve.tensor_tensor(dst[:, :, 0, :], t1[:, :, 0, :], t2[:, :, 0, :], ALU.subtract)
                        dve.tensor_tensor(dst[:, :, 1, :], t1[:, :, 1, :], t2[:, :, 1, :], ALU.add).then_inc(sm("rope_ok"), 1)
                        nr += 1
                    if u == 4:
                        dve.wait_ge(sm("pj_mm"), l * NPJ + q + 1)
                        dve.tensor_tensor(fg[:, i, :], ps[:, b, 256:264], bfg[:, :], ALU.add).then_inc(sm("fg_a"), 1)
                    if i == TT and u + 2 < N_TM + N_FM:
                        split_lo(l, u + 2)
                    if u == 4 and i == TT:
                        dve.wait_ge(sm("fg_a"), l * 10 + 9)
                        dve.scalar_tensor_tensor(out=fga[:, :, :].rearrange("p i h -> p (i h)"), in0=fg[:, :, :].rearrange("p i h -> p (i h)"),
                                                 scalar=-1.0, in1=fg[:, :, :].rearrange("p i h -> p (i h)"), op0=ALU.mult, op1=ALU.max).then_inc(sm("fg_a"), 1)
                dve.wait_ge(sm("fg_b"), 2 * l + 2)
                dve.scalar_tensor_tensor(out=logf[:, :, :].rearrange("p i h -> p (i h)"), in0=fg[:, :, :].rearrange("p i h -> p (i h)"),
                                         scalar=0.0, in1=fga[:, :, :].rearrange("p i h -> p (i h)"), op0=ALU.min, op1=ALU.subtract).then_inc(sm("logf_ok"), 1)
                dve.memset(lcum[:, 0, :], 0.0).then_inc(sm("lcum_ok"), 1)
                dve.wait_ge(sm("logf_ok"), l + 1)
                for i in range(1, TT):
                    dve.wait_ge(sm("lcum_ok"), l * TT + i)
                    dve.scalar_tensor_tensor(out=lcum[:, i, :], in0=logf[:, i - 1, :], scalar=float(D), in1=lcum[:, i - 1, :],
                                             op0=ALU.mult, op1=ALU.add).then_inc(sm("lcum_ok"), 1)
                for b in range(2):
                    dve.wait_ge(sm("f_hi"), 2 * l + b + 1)
                    dve.tensor_tensor(frow[:, 1, b * 512:(b + 1) * 512], ps[0:NH_F, b, :], frow[:, 0, b * 512:(b + 1) * 512].bitcast(F32),
                                      ALU.subtract).then_inc(sm("f_lo"), 1)

                def k_lo(g):
                    r = slice(64 * g, 64 * g + 64)
                    dve.wait_ge(sm("sk_hi"), l * 4 + 2 * g + 2)
                    for d in range(2):
                        ins = dve.tensor_tensor(sk2[g][64 * d:64 * d + 64, :], ks[r, 0:SEQ], sk1[g][r, :].bitcast(F32), ALU.subtract)
                    ins.then_inc(sm("sk_lo"), 1)

                def v_lo(g):
                    dve.wait_ge(sm("sv_hi"), l * 2 + g + 1)
                    half = lambda t: t[:, :, :].rearrange("p t (a n) -> p t a n", n=64)[:, :, 0:3:2, :]
                    dve.tensor_tensor(half(svl), vs[:, 0:TT, None, 64 * g:64 * g + 64].broadcast_to([P, TT, 2, 64]),
                                      half(svh).bitcast(F32), ALU.subtract).then_inc(sm("sv_lo"), 1)

                def q_lo(w):
                    g, i = w // 8, w % 8
                    for d in range(2):
                        r, ro_ = slice(64 * d, 64 * d + 64), slice(64 - 64 * d, 128 - 64 * d)
                        dve.wait_ge(sm("sq_hi"), l * 32 + 2 * w + d + 1)
                        ins = dve.scalar_tensor_tensor(out=sq1[w % 2][ro_, d:4:2, :], in0=qs[r, 2 * g:2 * g + 2, i * P:(i + 1) * P], scalar=SCALE,
                                                       in1=sq1[w % 2][r, d:4:2, :].bitcast(F32), op0=ALU.mult, op1=ALU.subtract)
                    ins.then_inc(sm("sq_lo"), 1)

                def row_max(w):
                    g = w // 8
                    W = P if w % 8 == 0 else 256
                    s4 = st[:, w % 4, :]
                    b = 2 * (w % 2)
                    dve.wait_ge(sm("s_mm"), l * 16 + w + 1)
                    dve.tensor_reduce(s4[:, 0:4], ps[:, b:b + 2, :].rearrange("p b (h n) -> p (b h) n", h=2)[:, :, 0:W], AX.X, ALU.max,
                                      negate=True).then_inc(sm("s_nm"), 1)
                    dve.wait_ge(sm("s_nm"), l * 16 + w + 1)
                    dve.tensor_tensor(s4[:, 4:8], s4[:, 0:4], nsnk[:, 4 * g:4 * g + 4], ALU.min).then_inc(sm("s_mn"), 1)
                    dve.wait_ge(sm("s_mn"), l * 16 + w + 1)
                    dve.tensor_tensor(s4[:, 12:16], s4[:, 4:8], snk[:, 4 * g:4 * g + 4], ALU.add).then_inc(sm("s_smx"), 1)

                def normalize(w):
                    W = P if w % 8 == 0 else 256
                    s4 = st[:, w % 4, :]
                    dve.wait_ge(sm("s_exp"), l * 16 + w + 1)
                    dve.wait_ge(sm("s_es"), l * 16 + w + 1)
                    dve.tensor_tensor(s4[:, 16:20], s4[:, 8:12], s4[:, 12:16], ALU.add).then_inc(sm("s_den"), 1)
                    dve.wait_ge(sm("s_den"), l * 16 + w + 1)
                    dve.reciprocal(s4[:, 16:20], s4[:, 16:20]).then_inc(sm("s_rd"), 1)
                    dve.wait_ge(sm("s_rd"), l * 16 + w + 1)
                    pv = pbuf[w % 2][:, 0:4 * W].rearrange("p (h n) -> p h n", h=4)
                    dve.tensor_tensor(pv, pv, s4[:, 16:20][:, :, None].broadcast_to([P, 4, W]), ALU.mult).then_inc(sm("s_norm"), 1)

                def pt_lo(w):
                    nk = 1 if w % 8 == 0 else 2
                    dve.wait_ge(sm("st_hi"), l * 16 + w + 1)
                    dve.tensor_tensor(sptl[w % 2][:, 0:nk, :, :].rearrange("p k h n -> p k (h n)"), ps[:, 4:4 + nk, :],
                                      spth[w % 2][:, 0:nk, :, :].rearrange("p k h n -> p k (h n)").bitcast(F32), ALU.subtract).then_inc(sm("st_lo"), 1)

                def o_lo(w):
                    g, i = w // 8, w % 8
                    dve.wait_ge(sm("so_hi"), l * 16 + w + 1)
                    dve.tensor_tensor(hl[:, 2 * g:2 * g + 2, i * P:(i + 1) * P], ps[:, 6 + w % 2, 0:256].rearrange("p (t n) -> p t n", t=2),
                                      hh[:, 2 * g:2 * g + 2, i * P:(i + 1) * P].bitcast(F32), ALU.subtract).then_inc(sm("so_lo"), 1)

                dve.wait_ge(sm("nsnk_ok"), l + 1)
                k_lo(0)
                for w in range(-2, 17):
                    if 0 <= w + 2 < 16:
                        q_lo(w + 2)
                    if 0 <= w + 1 < 16:
                        row_max(w + 1)
                    if 0 <= w < 16:
                        pt_lo(w)
                    if 0 <= w - 1 < 16:
                        o_lo(w - 1)
                    if 0 <= w + 1 < 16:
                        normalize(w + 1)
                    if w == -1:
                        v_lo(0)
                    if w == 0:
                        k_lo(1)
                    if w == 8:
                        v_lo(1)

                with dve.Fori(0, 4) as t:
                    pr = dve.snap(l * 4 + t)

                    def stacks_lo(h):
                        r, ro_ = slice(64 * h, 64 * h + 64), slice(64 - 64 * h, 128 - 64 * h)
                        t1 = bass.ds(t, 1)
                        dve.wait_ge(sm("fq_hi"), pr * 8 + 4 * h + 4)
                        dve.scalar_tensor_tensor(out=q1[h][ro_, :], in0=qf[r, t1, 0:SEQ].rearrange("p t n -> p (t n)"), scalar=SCALE,
                                                 in1=q1[h][r, :].bitcast(F32), op0=ALU.mult, op1=ALU.subtract).then_inc(sm("fq_lo"), 1)
                        dve.tensor_tensor(k2[h][0:64, :], kf[r, t1, 0:SEQ].rearrange("p t n -> p (t n)"), k1[h][r, :].bitcast(F32),
                                          ALU.subtract).then_inc(sm("fq_lo"), 1)

                    def row_max(e):
                        i = FOX_ORDER[e % 8]
                        n, nb = (i + 1) * P, (1 if i < 4 else 2)
                        b = 2 * (e % 2)
                        dve.wait_ge(sm("fs_mm"), pr * 16 + e + 1)
                        dve.tensor_reduce(st[:, e % 4, 0:1], ps[:, b:b + nb, 0:n // nb], AX.XY, ALU.max, negate=True).then_inc(sm("fs_nm"), 1)

                    def normalize(e):
                        i = FOX_ORDER[e % 8]
                        n = (i + 1) * P
                        s4 = st[:, e % 4, :]
                        dve.wait_ge(sm("fs_exp"), pr * 16 + e + 1)
                        dve.reciprocal(s4[:, 2:3], s4[:, 1:2]).then_inc(sm("fs_rd"), 1)
                        dve.wait_ge(sm("fs_rd"), pr * 16 + e + 1)
                        dve.tensor_scalar(pbuf[e % 2][:, 0:n], pbuf[e % 2][:, 0:n], s4[:, 2:3], None, ALU.mult).then_inc(sm("fs_norm"), 1)

                    def pt_lo(e):
                        i = FOX_ORDER[e % 8]
                        jb = (e // 2) % 2
                        for bb in range(NBT[e]):
                            g = BT[e] + bb
                            k0, k1_ = 4 * bb, min(4 * bb + 4, i + 1)
                            dve.wait_ge(sm("ft_hi"), pr * 24 + g + 1)
                            dve.tensor_tensor(ptl[jb][:, k0:k1_, (i % 2) * P:(i % 2 + 1) * P],
                                              ps[:, 4 + g % 2, 0:(k1_ - k0) * P].rearrange("p (k n) -> p k n", n=P),
                                              pth[jb][:, k0:k1_, (i % 2) * P:(i % 2 + 1) * P].bitcast(F32), ALU.subtract).then_inc(sm("ft_lo"), 1)

                    def o_lo(b):
                        dve.wait_ge(sm("fo_hi"), pr * 2 + b + 1)
                        c0 = (512, 0)[b]
                        t4 = bass.ds(t + 4, 1)
                        dve.tensor_tensor(hl[:, t4, c0:c0 + 512].rearrange("p t n -> p (t n)"), ps[:, 6 + b, :],
                                          hh[:, t4, c0:c0 + 512].rearrange("p t n -> p (t n)").bitcast(F32), ALU.subtract).then_inc(sm("fo_lo"), 1)

                    stacks_lo(0)
                    dve.wait_ge(sm("fv_hi"), pr + 1)
                    half = lambda t_: t_[:, :, :].rearrange("p t (a n) -> p t a n", n=64)[:, :, 0:3:2, :]
                    dve.tensor_tensor(half(fvl), vf[:, 0:TT, bass.ds(t * P, P)].rearrange("p t (a n) -> p t a n", n=64),
                                      half(fvh).bitcast(F32), ALU.subtract).then_inc(sm("fv_lo"), 1)
                    for e in range(-1, 16):
                        if e + 1 < 16:
                            row_max(e + 1)
                        if e == 1:
                            stacks_lo(1)
                        if e >= 0:
                            pt_lo(e)
                        if e + 1 < 16:
                            normalize(e + 1)
                        if e == 13:
                            o_lo(0)
                    o_lo(1)

                for w in range(4):
                    W = WIN + NEW if w < 2 else PAST + NEW
                    s4 = st[:, w, :]
                    dve.wait_ge(sm("a_mm"), l * 4 + w + 1)
                    if w < 2:
                        dve.tensor_reduce(s4[:, 0:1], ps[:, w % 2, 0:W], AX.X, ALU.max, negate=True).then_inc(sm("a_nm"), 1)
                        dve.wait_ge(sm("a_nm"), l * 2 + w + 1)
                        dve.tensor_tensor(s4[:, 1:2], s4[:, 0:1], ssnk[:, 1, w:w + 1], ALU.min).then_inc(sm("a_mn"), 1)
                        dve.wait_ge(sm("a_mn"), l * 4 + w + 1)
                        dve.tensor_tensor(s4[:, 3:4], s4[:, 1:2], ssnk[:, 0, w:w + 1], ALU.add).then_inc(sm("a_smx"), 1)
                        dve.wait_ge(sm("a_es"), l * 2 + w + 1)
                        dve.wait_ge(sm("a_exp"), l * 4 + w + 1)
                        dve.tensor_tensor(s4[:, 4:5], s4[:, 2:3], s4[:, 3:4], ALU.add).then_inc(sm("a_den"), 1)
                        dve.wait_ge(sm("a_den"), l * 2 + w + 1)
                        dve.reciprocal(s4[:, 5:6], s4[:, 4:5]).then_inc(sm("a_rd"), 1)
                    else:
                        dve.tensor_reduce(s4[:, 1:2], ps[:, w % 2, 0:W], AX.X, ALU.max, negate=True).then_inc(sm("a_mn"), 1)
                        dve.wait_ge(sm("a_exp"), l * 4 + w + 1)
                        dve.reciprocal(s4[:, 5:6], s4[:, 2:3]).then_inc(sm("a_rd"), 1)
                    dve.wait_ge(sm("a_rd"), l * 4 + w + 1)
                    dve.tensor_scalar(ap[:, 0:W], ap[:, 0:W], s4[:, 5:6], None, ALU.mult).then_inc(sm("a_norm"), 1)
                    if w % 2:
                        t0 = 0 if w < 2 else 4
                        dve.wait_ge(sm("ao_hi"), 2 * l + w // 2 + 1)
                        dve.tensor_tensor(hl[:, t0:t0 + 4, SEQ:TOK], ps[:, 3, 0:P].rearrange("p (t n) -> p t n", t=4),
                                          hh[:, t0:t0 + 4, SEQ:TOK].bitcast(F32), ALU.subtract).then_inc(sm("ao_lo"), 1)

                with dve.Fori(0, 2) as r:
                    n0 = dve.snap(l * NW + W_WO0 + r * 2)
                    for b in range(2):
                        split_lo(l, W_WO0 + b, n0 + b)
                post_norm(l, NPOST1)
                pre_norm(l, NPRE2)
                wait_apart(dve, ("const_in", 64), ("y_zero", l + 1))
                with dve.Fori(0, MSTEPS) as m:
                    mm = dve.snap(l * MSTEPS + m)
                    n0 = dve.snap(l * NW + W_MLP0 + m * 4)

                    def u_square(q):
                        dve.wait_ge(sm("u_relu"), mm * 12 + q + 1)
                        dve.wait_ge(sm("u_ok"), mm * 12 + max(0, q - 1))
                        dve.tensor_tensor(u_t[q % 2][:, :], r_t[q % 2][:, :], r_t[q % 2][:, :], ALU.mult).then_inc(sm("u_sq"), 1)

                    def u_lo(q):
                        c = q % 3
                        cs = slice(c * CH, (c + 1) * CH)
                        dve.wait_ge(sm("u_hi"), mm * 12 + q + 1)
                        dve.tensor_tensor(ul[:, q // 3, cs], u_t[q % 2][:, :], uh[:, q // 3, cs].bitcast(F32), ALU.subtract).then_inc(sm("u_ok"), 1)

                    split_lo(l, W_MLP0, n0)
                    split_lo(l, W_MLP0 + 1, n0 + 1)
                    for q in range(12):
                        if q == 6:
                            split_lo(l, W_MLP0 + 2, n0 + 2)
                        u_square(q)
                        if q >= 1:
                            u_lo(q - 1)
                    u_lo(11)
                    dve.wait_ge(sm("d_add"), mm * 24)
                    for q in range(24):
                        if q == 0:
                            split_lo(l, W_MLP0 + 3, n0 + 3)
                        kt, c = q // 3, q % 3
                        cs = slice(c * CH, (c + 1) * CH)
                        dve.wait_ge(sm("d_mm"), mm * 24 + q + 1)
                        dve.tensor_tensor(y[:, kt, cs], ps[:, 4 + q % 4, 0:CH], y[:, kt, cs], ALU.add).then_inc(sm("d_add"), 1)
                post_norm(l, NPOST2)

        @block.tensor
        def _(pe):
            def three(out, w_hi, w_lo, m_hi, m_lo, k, nk, start=True, stop=True):
                pe.matmul(out, w_hi, m_hi, start=start and k == 0, stop=False)
                pe.matmul(out, w_hi, m_lo, start=False, stop=False)
                return pe.matmul(out, w_lo, m_hi, start=False, stop=stop and k == nk - 1)

            pe.wait_ge(sm("const_in"), 64)
            pe.wait_ge(sm("c_in"), 16)
            pe.transpose(ps[:, 7, 0:16], crow[:, :], ident[0:16, 0:16]).then_inc(sm("c_tr"), 1)
            for i in range(TT + 1):
                pe.wait_ge(sm(f"xrow_in{i % 2}"), 16 * (i // 2 + 1))
                w = P if i < TT else NEW
                for hf in range(2):
                    q = 2 * i + hf
                    if q >= 2:
                        pe.wait_ge(sm("x_put"), q - 1)
                    for k in range(4):
                        ins = pe.transpose(ps[:, q % 2, k * w:(k + 1) * w], xrow[i % 2][0:w, (4 * hf + k) * P:(4 * hf + k + 1) * P], ident[0:w, 0:w])
                    ins.then_inc(sm("x_tr"), 1)
            pe.wait_ge(sm("zero_ok"), 1)
            pe.wait_ge(sm("cb_ok"), 1)
            pe.wait_ge(sm("silu_b"), 3)
            pe.matmul(ps[:, 7, 0:P], zerob[:, :], identb, start=True, stop=True).then_inc(sm("ada_mm"), 1)

            def means(l, nu):
                for c in range(NCH):
                    idx = l * 12 + nu * 3 + c
                    pe.wait_ge(sm("sq_ok"), idx + 1)
                    pe.wait_ge(sm("ln_ok"), idx)
                    for k in range(KT):
                        ins = pe.matmul(ps[:, 4 + c % 2, 0:CH], onesd[:, :], sq[:, k, c * CH:(c + 1) * CH], start=(k == 0), stop=(k == KT - 1))
                    ins.then_inc(sm("mean_ok"), 1)

            with pe.Fori(0, DEPTH) as l:
                pe.wait_ge(sm("vrow_in"), (l + 1) * 32)
                pe.wait_ge(sm("ln_ok"), l * 12)
                pe.transpose(ps[:, 5, 0:80], vrow[:, :], ident[0:80, 0:80]).then_inc(sm("v_tr"), 1)
                wait_apart(pe, ("zero_ok", 1), ("d_add", l * MSTEPS * 24))
                with pe.Fori(0, N_ADA // 2) as ab:
                    for s in range(2):
                        pe.wait_ge(sm(f"ada_in{s}"), (l * (N_ADA // 2) + ab + 1) * 16)
                        pe.wait_ge(sm("ada_ev"), l * N_ADA + ab * 2)
                        for j in range(2):
                            for k in range(KT):
                                ins = pe.matmul(ps[:, 6 + s, 2 * j:2 * j + 2], raw[s][:, k * 256 + j * P:k * 256 + (j + 1) * P], sc[:, :, k],
                                                start=(k == 0), stop=(k == KT - 1))
                        ins.then_inc(sm("ada_mm"), 1)
                means(l, NPRE1)

                pe.wait_ge(sm("h_ok"), l * 6 + 3)

                def transposes(nr):
                    u = ROPES[nr][0]
                    pe.wait_ge(sm("rope_ok"), l * NR + nr + 1)
                    if nr >= 2:
                        pe.wait_ge(sm("rtr_ev"), l * NR + nr - 1)
                    for j in range(1 if u == 0 else 2):
                        ins = pe.transpose(ps[:, 4 + nr % 2, j * P:(j + 1) * P], ro[nr % 2][:, j * P:(j + 1) * P], ident[:, :])
                    ins.then_inc(sm("rtr_mm"), 1)

                pending = None
                for q, it in enumerate(PJ):
                    b = q % 4
                    n = it[1] if it[0] == "t" else N_TM + it[1]
                    if q >= 4:
                        if n_act(q - 3):
                            pe.wait_ge(sm("ev_act"), l * n_act(NPJ) + n_act(q - 3))
                        if by_dve(PJ[q - 4]):
                            it4 = PJ[q - 4]
                            if it4[1] < 3:
                                pe.wait_ge(sm("rope_t"), l * NR + it4[1] * (TT + 1) + it4[2] + 1)
                            else:
                                pe.wait_ge(sm("fg_a"), l * 10 + it4[2] + 1)
                    pe.wait_ge(sm("w_lo"), l * NW + n + 1)
                    if it[0] == "t":
                        _, u, i = it
                        w = TM_COLS[u][1]
                        t0 = i * P if i < TT else TAIL
                        ts = slice(t0, t0 + P)
                        whv, wlv = w_view(wh[n % 2], n), w_view(wl[n % 2], n)
                        for k in range(KT):
                            ins = three(ps[:, b, 0:w], hh[:, k, ts], hl[:, k, ts], whv[:, k, :], wlv[:, k, :], k, KT)
                        ins.then_inc(sm("pj_mm"), 1)
                        last = i == TT
                    else:
                        _, blk, j, c = it
                        cs = slice(c * CH, (c + 1) * CH)
                        whv, wlv = w_view(wh[n % 2], n), w_view(wl[n % 2], n)
                        for k in range(KT):
                            ins = three(ps[:, b, 0:CH], whv[:, k, j * P:(j + 1) * P], wlv[:, k, j * P:(j + 1) * P],
                                        hh[:, k, cs], hl[:, k, cs], k, KT)
                        ins.then_inc(sm("pj_mm"), 1)
                        last = j == 1 and c == NCH - 1
                    if last:
                        pe.matmul(ps[:, 7, 0:32], zerob[:, :], identb[:, 0:32], start=True, stop=True).then_inc(sm("w_used"), 1)
                    if pending is not None:
                        transposes(pending)
                        pending = None
                    if it[0] == "t" and it[1] < 3:
                        pending = it[1] * (TT + 1) + it[2]
                pe.wait_ge(sm("ev_act"), (l + 1) * n_act(NPJ))
                for i in range(TT + 1):
                    if i >= 2:
                        pe.wait_ge(sm("ko_ev"), l * (TT + 1) + i - 1)
                    t0 = i * P if i < TT else TAIL
                    for t in range(4):
                        ins = pe.transpose(ps[:, 6 + i % 2, t * P:(t + 1) * P], kf[:, t, t0:t0 + P], ident[:, :])
                    ins.then_inc(sm("ko_mm"), 1)
                pe.wait_ge(sm("logf_ok"), l + 1)
                pe.wait_ge(sm("lcum_ok"), (l + 1) * TT)
                for i in range(TT):
                    out = ps[0:NH_F, i // 4, (i % 4) * P:(i % 4 + 1) * P]
                    pe.matmul(out, logf[:, i, :], tri[:, :], start=(i % 4 == 0), stop=False, skip_group_check=True)
                    ins = pe.matmul(out, lcum[:, i, :], onesd[:, :], start=False, stop=(i % 4 == 3), skip_group_check=True)
                ins.then_inc(sm("f_mm"), 1)

                def scores(w):
                    g, i = w // 8, w % 8
                    W = P if i == 0 else 256
                    k0 = 0 if i == 0 else (i - 1) * P
                    pe.wait_ge(sm("sq_lo"), l * 16 + w + 1)
                    pe.wait_ge(sm("sk_lo"), l * 2 + g + 1)
                    if w >= 2:
                        pe.wait_ge(sm("s_exp"), l * 16 + w - 1)
                    for bb in range(2):
                        bank = 2 * (w % 2) + bb
                        view = ps[:, bank, :].rearrange("p (h n) -> p h n", h=2)
                        msk = winb[:, 256 - W:256]
                        for h in range(2):
                            pe.matmul(view[:, h, 0:W], identb, msk, start=(h == 0), stop=False, skip_group_check=True)
                        for h in range(2):
                            hd = 2 * h + bb
                            r = slice(64 * bb, 64 * bb + 64)
                            pe.matmul(view[:, h, 0:W], sq1[w % 2][:, hd, :], sk1[g][:, k0:k0 + W], start=False, stop=False, skip_group_check=True)
                            ins = pe.matmul(view[:, h, 0:W], sq1[w % 2][r, hd, :], sk2[g][r, k0:k0 + W], start=False, stop=(h == 1), skip_group_check=True)
                    ins.then_inc(sm("s_mm"), 1)

                def p_transposes(w):
                    W = P if w % 8 == 0 else 256
                    pe.wait_ge(sm("s_norm"), l * 16 + w + 1)
                    pe.wait_ge(sm("st_lo"), l * 16 + w)
                    for kb in range(W // P):
                        for hd in range(4):
                            ins = pe.transpose(ps[:, 4 + kb, hd * P:(hd + 1) * P], pbuf[w % 2][:, hd * W + kb * P:hd * W + (kb + 1) * P], ident[:, :])
                    ins.then_inc(sm("st_mm"), 1)

                def products(w):
                    g, i = w // 8, w % 8
                    pe.wait_ge(sm("st_lo"), l * 16 + w + 1)
                    pe.wait_ge(sm("sv_lo"), l * 2 + g + 1)
                    if w >= 2:
                        pe.wait_ge(sm("so_lo"), l * 16 + w - 1)
                    kbs = [0] if i == 0 else [i - 1, i]
                    todo = [(kb, d) for kb in range(len(kbs)) for d in range(2)]
                    for x, (kb, d) in enumerate(todo):
                        vsl = slice(64 * d, 64 * d + P)
                        out = ps[:, 6 + w % 2, 0:256]
                        ins = three(out, svh[:, kbs[kb], vsl], svl[:, kbs[kb], vsl],
                                    spth[w % 2][:, kb, 2 * d:2 * d + 2, :], sptl[w % 2][:, kb, 2 * d:2 * d + 2, :], x, len(todo))
                    ins.then_inc(sm("so_mm"), 1)

                pe.wait_ge(sm("sz_ok"), 2 * (l + 1))
                pe.wait_ge(sm("f_lo"), 2 * (l + 1))
                pe.wait_ge(sm("ko_ev"), (l + 1) * (TT + 1))
                pe.wait_ge(sm("rtr_ev"), (l + 1) * NR)
                for w in range(-1, 17):
                    if 0 <= w + 1 < 16:
                        scores(w + 1)
                    if 0 <= w < 16:
                        p_transposes(w)
                    if 0 <= w - 1 < 16:
                        products(w - 1)

                wait_apart(pe, ("zero_ok", 1), ("so_lo", (l + 1) * 16), ("fz_ok", 5 * (l + 1)))
                with pe.Fori(0, 4) as t:
                    pr = pe.snap(l * 4 + t)

                    def scores(e):
                        h, i = e // 8, FOX_ORDER[e % 8]
                        n, nb = (i + 1) * P, (1 if i < 4 else 2)
                        w = n // nb
                        if e % 8 == 0:
                            pe.wait_ge(sm("fq_lo"), pr * 4 + 2 * h + 2)
                            pe.wait_ge(sm(f"frow_in{h}"), (pr + 1) * 32)
                        pe.wait_ge(sm("fs_exp"), pr * 16 + max(0, e - 1))
                        qb = slice(i * P, (i + 1) * P)
                        for c in range(nb):
                            out = ps[:, 2 * (e % 2) + c, 0:w]
                            pe.matmul(out, q1[h][:, qb], k1[h][:, c * w:(c + 1) * w], start=True, stop=False)
                            ins = pe.matmul(out, q2[h][0:68, qb], k2[h][0:68, c * w:(c + 1) * w], start=False, stop=(c < nb - 1))
                        ins = pe.matmul(ps[:, 2 * (e % 2) + nb - 1, w - P:w], identb, causb, start=False, stop=True)
                        ins.then_inc(sm("fs_mm"), 1)

                    def p_transposes(e):
                        i = FOX_ORDER[e % 8]
                        pe.wait_ge(sm("fs_norm"), pr * 16 + e + 1)
                        for bb in range(NBT[e]):
                            g = BT[e] + bb
                            pe.wait_ge(sm("ft_lo"), pr * 24 + max(0, g - 1))
                            k0, k1_ = 4 * bb, min(4 * bb + 4, i + 1)
                            for kb in range(k0, k1_):
                                ins = pe.transpose(ps[:, 4 + g % 2, (kb - k0) * P:(kb - k0 + 1) * P], pbuf[e % 2][:, kb * P:(kb + 1) * P], ident[:, :])
                            ins.then_inc(sm("ft_mm"), 1)

                    def products(jj):
                        h, J, jb = jj // 4, 3 - jj % 4, jj % 2
                        bank, half = (6, J - 2) if J >= 2 else (7, J)
                        if h == 0 and J in (3, 1):
                            pe.wait_ge(sm("fo_lo"), pr * 2)
                            pe.matmul(ps[:, bank, :], zerob[:, :], cb[:, :], start=True, stop=False, skip_group_check=True)
                        pe.wait_ge(sm("ft_lo"), pr * 24 + BT[2 * jj + 2])
                        if jj == 0:
                            pe.wait_ge(sm("fv_lo"), pr + 1)
                        vsl = slice(64 * h, 64 * h + P)
                        for kb in range(2 * J + 2):
                            q0 = P if kb == 2 * J + 1 else 0
                            out = ps[:, bank, half * 256 + q0:half * 256 + 256]
                            mh, ml = pth[jb][:, kb, q0:256], ptl[jb][:, kb, q0:256]
                            for wv, mv in ((fvh, mh), (fvh, ml), (fvl, mh)):
                                ins = pe.matmul(out, wv[:, kb, vsl], mv, start=False, stop=(kb == 2 * J + 1 and wv is fvl), skip_group_check=True)
                        ins.then_inc(sm("pv_mm"), 1)

                    for e in range(-1, 16):
                        if e + 1 < 16:
                            scores(e + 1)
                        if e >= 0:
                            p_transposes(e)
                        if e >= 2 and e % 2 == 0:
                            products(e // 2 - 1)
                    products(7)

                pe.wait_ge(sm("cache_in"), (l + 1) * 80)
                pe.wait_ge(sm("lcs_ok"), 2 * (l + 1))
                pe.wait_ge(sm("ft_lo"), (l + 1) * 96)
                pe.wait_ge(sm("fo_lo"), (l + 1) * 8)
                for c in range(2):
                    for t in range(4):
                        pe.transpose(ps[:, c, t * P:(t + 1) * P], ckf[:, c, t * P:(t + 1) * P], ident[:, :])
                for g in range(2):
                    pe.transpose(ps[:, 2, g * P:(g + 1) * P], cks[:, g, :, :].rearrange("p d e -> p (d e)"), ident[:, :])
                pe.matmul(ps[0:NH_F, 3, 0:P], lc[:, 0, :], tri[:, :], start=True, stop=False, skip_group_check=True)
                pe.matmul(ps[0:NH_F, 3, P:2 * P], lc[:, 1, :], tri[:, :], start=False, stop=False, skip_group_check=True)
                pe.matmul(ps[0:NH_F, 3, P:2 * P], lcs[:, 0, :], onesd[:, :], start=False, stop=False, skip_group_check=True)
                pe.matmul(ps[0:NH_F, 3, 2 * P:2 * P + NEW], logf[NEWP:P, TT, :], tri[NEWP:P, NEWP:P], start=False, stop=False, skip_group_check=True)
                pe.matmul(ps[0:NH_F, 3, 2 * P:2 * P + NEW], lcs[:, 1, :], onesd[:, 0:NEW], start=False, stop=True,
                          skip_group_check=True).then_inc(sm("ck_tr"), 1)
                for w in range(4):
                    pe.wait_ge(sm("zero_ok"), 1)
                    pe.wait_ge(sm("ck_ev"), l + 1)
                    pe.wait_ge(sm("aq_ok"), 2 * (l + 1))
                    W = WIN + NEW if w < 2 else PAST + NEW
                    if w >= 2:
                        pe.wait_ge(sm("a_exp"), l * 4 + w - 1)
                    for hd in range(4):
                        h = 4 * (w % 2) + hd
                        r = slice(64 * (h % 2), 64 * (h % 2) + 64)
                        out = ps[32 * hd:32 * hd + 32, w % 2, 0:W]
                        qn = aqs[r, (0 if w < 2 else 4) + h // 2, :]
                        if w < 2:
                            ins = pe.matmul(out, qn, kst[r, w, :], start=True, stop=True)
                            continue
                        pe.matmul(out, qn, kft[r, h // 2, :], start=True, stop=False)
                        pe.matmul(out, ident[0:NH_F, h:h + 1].broadcast_to([NH_F, NEW]), fsn[:, :], start=False, stop=False)
                        pe.matmul(out, fs[:, PAST:], ident[0:NH_F, h:h + 1].broadcast_to([NH_F, W]), start=False, stop=False)
                        ins = pe.matmul(out[:, PAST:W], identb[0:NEW, 0:NEW], causb[0:NEW, 0:NEW], start=False, stop=True)
                    ins.then_inc(sm("a_mm"), 1)
                    pe.wait_ge(sm("a_norm"), l * 4 + w + 1)
                    if w >= 1:
                        pe.wait_ge(sm("at_ev"), l * 4 + w)
                    starts = [0, NEW] if w < 2 else [0, P, PAST + NEW - P]
                    for kb, c0 in enumerate(starts):
                        ins = pe.transpose(ps[:, 2, kb * P:(kb + 1) * P], ap[:, c0:c0 + P], ident[:, :])
                    ins.then_inc(sm("at_mm"), 1)
                    pe.wait_ge(sm("at_ev"), l * 4 + w + 1)
                    if w == 2:
                        pe.wait_ge(sm("ao_lo"), 2 * l + 1)
                    for hd in range(4):
                        h = 4 * (w % 2) + hd
                        out = ps[64 * (h % 2):64 * (h % 2) + 64, 3, (h // 2) * NEW:(h // 2 + 1) * NEW]
                        pc = slice(hd * NEW, (hd + 1) * NEW)
                        if w < 2:
                            pe.matmul(out, cvs[:, 64 * w:64 * w + 64], apt[:, 0, pc], start=True, stop=False)
                            ins = pe.matmul(out, vs_new[NEWP:P, 64 * w:64 * w + 64], apt[NEWP:P, 1, pc], start=False, stop=True)
                        else:
                            for kb in range(2):
                                pe.matmul(out, cvf[:, kb, h * HD:(h + 1) * HD], apt[:, kb, pc], start=(kb == 0), stop=False)
                            ins = pe.matmul(out, vf[NEWP:P, TT, h * HD:(h + 1) * HD], apt[NEWP:P, 2, pc], start=False, stop=True)
                    ins.then_inc(sm("ao_mm"), 1)

                def step(n, out, b, j, cs, k, nk, m_hi, m_lo):
                    whv, wlv = w_view(wh[n % 2], n), w_view(wl[n % 2], n)
                    js = slice(j * P, (j + 1) * P)
                    return three(out, whv[:, k, js], wlv[:, k, js], m_hi[:, k, cs], m_lo[:, k, cs], k, nk)

                wait_apart(pe, ("zero_ok", 1), ("ao_lo", 2 * (l + 1)))
                with pe.Fori(0, 2) as r:
                    n0 = pe.snap(l * NW + W_WO0 + r * 2)
                    yb = pe.snap(l * 24 + r * 12)
                    for q in range(12):
                        b, j, c = q // 6, (q // 3) % 2, q % 3
                        if q % 6 == 0:
                            pe.wait_ge(sm("w_lo"), n0 + b + 1)
                        pe.wait_ge(sm("y_ev"), yb + max(0, q - 5))
                        for k in range(KT):
                            ins = step(W_WO0 + b, ps[:, q % 6, 0:CH], b, j, slice(c * CH, (c + 1) * CH), k, KT, hh, hl)
                        ins.then_inc(sm("y_mm"), 1)
                        if q % 6 == 5:
                            pe.matmul(ps[:, 7, 0:32], zerob[:, :], identb[:, 0:32], start=True, stop=True).then_inc(sm("w_used"), 1)
                pe.wait_ge(sm("y_ev"), (l + 1) * 24)
                means(l, NPOST1)
                means(l, NPRE2)

                with pe.Fori(0, MSTEPS) as m:
                    mm = pe.snap(l * MSTEPS + m)
                    n0 = pe.snap(l * NW + W_MLP0 + m * 4)
                    for q in range(12):
                        b, j, c = q // 6, (q // 3) % 2, q % 3
                        if q % 6 == 0:
                            pe.wait_ge(sm("w_lo"), n0 + b + 1)
                        if q < 3:
                            pe.wait_ge(sm("h_ok"), l * 6 + 4 + c)
                        pe.wait_ge(sm("u_relu"), mm * 12 + max(0, q - 3))
                        for k in range(KT):
                            ins = step(W_MLP0 + b, ps[:, q % 4, 0:CH], b, j, slice(c * CH, (c + 1) * CH), k, KT, hh, hl)
                        ins.then_inc(sm("u_mm"), 1)
                        if q % 6 == 5:
                            pe.matmul(ps[:, 7, 0:32], zerob[:, :], identb[:, 0:32], start=True, stop=True).then_inc(sm("w_used"), 1)
                    for q in range(24):
                        b, j, c = q // 12, (q // 3) % 4, q % 3
                        if q % 12 == 0:
                            pe.wait_ge(sm("w_lo"), n0 + b + 3)
                        if q < 3:
                            pe.wait_ge(sm("u_ok"), mm * 12 + 10 + c)
                        pe.wait_ge(sm("d_add"), mm * 24 + max(0, q - 3))
                        for k in range(HG):
                            ins = step(W_MLP0 + 2 + b, ps[:, 4 + q % 4, 0:CH], b, j, slice(c * CH, (c + 1) * CH), k, HG, uh, ul)
                        ins.then_inc(sm("d_mm"), 1)
                        if q % 12 == 11:
                            pe.matmul(ps[:, 0, 0:32], zerob[:, :], identb[:, 0:32], start=True, stop=True).then_inc(sm("w_used"), 1)
                pe.wait_ge(sm("d_add"), (l + 1) * MSTEPS * 24)
                means(l, NPOST2)

            pe.wait_ge(sm("x_ready"), DEPTH * 6 + 3)
            for i in range(TT + 1):
                t0 = i * P if i < TT else TAIL
                for hf in range(2):
                    q = 2 * i + hf
                    if q >= 2:
                        pe.wait_ge(sm("fin_ev"), q - 1)
                    for k in range(4):
                        ins = pe.transpose(ps[:, q % 2, k * P:(k + 1) * P], xf[:, 4 * hf + k, t0:t0 + P], ident[:, :])
                    ins.then_inc(sm("fin_tr"), 1)


def constants():
    k, q = np.arange(P)[:, None], np.arange(P)[None, :]
    caus = np.where(q > k, NEG, 0.0)
    w = np.arange(256)[None, :]
    win = np.where(((k < 64) & (w >= 192)) | ((k >= 64) & (w < 64)), NEG, 0.0)
    consts = np.concatenate([np.eye(P), np.full((P, P), 1.0 / D), (k <= q) * 1.0, caus, win], 1).astype(np.float32)
    half = HD // 2
    inv = np.float32(10000.0) ** (-np.arange(half, dtype=np.float32) / np.float32(half))
    pos = np.zeros((P, TT + 1), np.float32)
    pos[:, :TT] = np.arange(SEQ).reshape(TT, P).T
    pos[NEWP:, TT] = PAST + np.arange(NEW)
    ang = pos[:, :, None] * inv[None, None, :]
    return consts, np.cos(ang).astype(np.float32).reshape(P, -1), np.sin(ang).astype(np.float32).reshape(P, -1)


def kernel(x_prompt, x_sample, c_prompt, c_sample, cache_swa_k, cache_swa_v, cache_fox_k, cache_fox_v,
           cache_fox_logf, w_in, b_forget, sinks, w_out, w_up, w_down, w_ada, b_ada,
           g_pre_mix, g_post_mix, g_pre_mlp, g_post_mlp):
    import concourse.bacc as bacc
    from concourse.bass_utils import run_bass_kernel_spmd as run

    consts, cos, sin = constants()
    A = lambda x: np.ascontiguousarray(np.asarray(x))
    rows = lambda g: A(g).reshape(DEPTH, KT, P)
    sk = A(sinks)
    ins = {
        "x_prompt": A(x_prompt).reshape(SEQ, D), "x_sample": A(x_sample).reshape(NEW, D),
        "c_rows": np.concatenate([A(c_prompt).reshape(KT, P), A(c_sample).reshape(KT, P)]),
        "cache_swa_k": A(cache_swa_k).reshape(DEPTH, WIN, P), "cache_swa_v": A(cache_swa_v).reshape(DEPTH, WIN, P),
        "cache_fox_k": A(cache_fox_k).reshape(DEPTH, PAST, 512), "cache_fox_v": A(cache_fox_v).reshape(DEPTH, PAST, 512),
        "cache_fox_logf": A(cache_fox_logf).reshape(DEPTH, PAST, NH_F),
        "w_in": A(w_in), "w_out": A(w_out), "w_up": A(w_up), "w_down": A(w_down), "w_ada": A(w_ada),
        "b_ada": A(b_ada).reshape(DEPTH, 48, P),
        "gains": np.concatenate([rows(g_pre_mix), rows(g_post_mix), rows(g_pre_mlp), rows(g_post_mlp)], 1),
        "sinks_rows": np.repeat(sk[:, None, [0, 2, 1, 3, 4, 6, 5, 7]], P, 1), "bf_rows": np.repeat(A(b_forget)[:, None, :], P, 1),
        "sinks_sample": np.repeat(sk.reshape(DEPTH, 2, 4).transpose(0, 2, 1), NEW, 1),
        "consts": consts, "cos": cos, "sin": sin,
    }
    outs = {
        "y_prompt": (SEQ, D), "y_sample": (NEW, D),
        "p_swa_k": (DEPTH, WIN, P), "p_swa_v": (DEPTH, WIN, P),
        "p_fox_k": (DEPTH, SEQ, 512), "p_fox_v": (DEPTH, SEQ, 512), "p_fox_logf": (DEPTH, SEQ, NH_F),
        "s_swa_k": (DEPTH, WIN, P), "s_swa_v": (DEPTH, WIN, P),
        "s_fox_k": (DEPTH, NEW, 512), "s_fox_v": (DEPTH, NEW, 512), "s_fox_logf": (DEPTH, NEW, NH_F),
    }
    nc = bacc.Bacc("TRN2", target_bir_lowering=False, num_devices=1)
    a = {n: nc.dram_tensor(n, v.shape, mybir.dt.from_np(v.dtype), kind="ExternalInput").ap() for n, v in ins.items()}
    a |= {n: nc.dram_tensor(n, s, F32, kind="ExternalOutput").ap() for n, s in outs.items()}
    build(nc, a)
    r = run(nc, [ins], core_ids=[0]).results[0]
    kv = lambda n, s, h: r[n].reshape(DEPTH, 1, s, h, HD)
    return (r["y_prompt"].reshape(1, SEQ, D), r["y_sample"].reshape(1, NEW, D),
            kv("p_swa_k", WIN, NKV), kv("p_swa_v", WIN, NKV), kv("p_fox_k", SEQ, NH_F), kv("p_fox_v", SEQ, NH_F),
            r["p_fox_logf"].reshape(DEPTH, 1, SEQ, NH_F),
            kv("s_swa_k", WIN, NKV), kv("s_swa_v", WIN, NKV), kv("s_fox_k", NEW, NH_F), kv("s_fox_v", NEW, NH_F),
            r["s_fox_logf"].reshape(DEPTH, 1, NEW, NH_F))
```

```python
from contextlib import ExitStack

import numpy as np

import concourse.bass as bass
from concourse import mybir

ALU = mybir.AluOpType
ACT = mybir.ActivationFunctionType
AX = mybir.AxisListType
F32 = mybir.dt.float32
F32R = mybir.dt.float32r
BF16 = mybir.dt.bfloat16

P = 128
D = 1024
KT = D // P
SEQ, NEW = 1024, 32
TOK = SEQ + NEW
NCH = 3
CH = TOK // NCH
TT = SEQ // P
TAIL = TOK - P
NEWP = P - NEW
DEPTH = 2
HD = 64
NH_S, NKV, NH_F = 8, 2, 8
PAST, WIN = 256, 128
N_IN = 2312
SCALE = HD ** -0.5
EPS = 1e-6
NEG = -1e30
C_QS, C_KS, C_QF, C_KF, C_VF = 0, 512, 768, 1280, 1792
D_FF = 4 * D
HG = 4
MSTEPS = D_FF // (HG * P)
N_ADA = 6 * D // 256
N_ADA1 = 2 * D // 256
ADA_SLOT = [0, 1, 2, 4, 3, 5, 0, 1]

N_FM, N_TM, N_WO, N_MLP = 4, 5, 4, 4
W_WO0 = N_FM + N_TM
W_MLP0 = W_WO0 + N_WO
NW = W_MLP0 + N_MLP * MSTEPS
FM_COLS = [C_QF, C_QF + 256, C_KF, C_KF + 256]
TM_COLS = [(C_VF, 256), (C_VF + 256, 264), (C_KS, 256), (C_QS, 256), (C_QS + 256, 256)]
U_GATE, U_KV = 1, 2
SLOTW = KT * 264

FOX_ORDER = [6, 7, 4, 5, 2, 3, 0, 1]
NPRE1, NPOST1, NPRE2, NPOST2 = range(4)


def stream_pieces(c):
    a, b = c * CH, (c + 1) * CH
    out = [(a, min(b, SEQ), 0)]
    if b > SEQ:
        out.append((SEQ, b, 1))
    return out


def build(nc, a):
    ctx = ExitStack()
    with ctx:
        base = 16512

        def at(name, shape, dt, off):
            return nc.alloc_sbuf_tensor_at(name, shape, dt, offset=base + off)

        def sem(name):
            return ctx.enter_context(nc.semaphore(name))

        FM = KT * TOK * 4
        hh = at("hh", [P, KT, TOK], F32R, 0)
        hl = at("hl", [P, KT, TOK], F32R, FM)
        sq = at("sq", [P, KT, TOK], F32, 0)
        th = at("th", [P, KT, TOK], F32, FM)
        o = 2 * FM
        y = at("y", [P, KT, TOK], F32, o)
        xr = at("xr", [P, KT, TOK], F32, FM)
        xf = at("xf", [P, KT, TOK], F32, o + FM)
        uh = at("uh", [P, HG, TOK], F32R, o + FM)
        ul = at("ul", [P, HG, TOK], F32R, o + FM + FM // 2)
        mt = o + 2 * FM
        r_t = [at(f"r_t{i}", [P, CH], F32, mt + i * CH * 4) for i in range(2)]
        u_t = [at(f"u_t{i}", [P, CH], F32, mt + (2 + i) * CH * 4) for i in range(2)]
        rb = [at(f"rb{i}", [P, CH], F32, mt + 5632 + i * CH * 4) for i in range(2)]
        qs = at("qs", [P, 4, TOK], F32, o)
        ks = at("ks", [P, TOK], F32, o + 16896)
        vs = at("vs", [P, TT + 1, P], F32, o + 21120)
        qf = at("qf", [P, 4, TOK], F32, o + 25728)
        kf = at("kf", [P, 4, TOK], F32, o + 42624)
        vf = at("vf", [P, TT + 1, 512], F32, o + 59520)
        dz = o + 77952
        raw = [at(f"raw{i}", [P, SLOTW], F32, dz + i * SLOTW * 4) for i in range(2)]
        wh = [at(f"wh{i}", [P, SLOTW], F32R, dz + (2 + i) * SLOTW * 4) for i in range(2)]
        wl = [at(f"wl{i}", [P, SLOTW], F32R, dz + (4 + i) * SLOTW * 4) for i in range(2)]
        sz = dz + 6 * SLOTW * 4
        ro = [at(f"ro{i}", [P, 256], F32, sz + i * 1024) for i in range(2)]
        rt1 = at("rt1", [P, 256], F32, sz + 2048)
        rt2 = at("rt2", [P, 256], F32, sz + 3072)
        costab = at("costab", [P, TT + 1, 32], F32, sz + 4096)
        sintab = at("sintab", [P, TT + 1, 32], F32, sz + 5248)
        rk = [at(f"rk{i}", [P, P], F32, sz + 6400 + i * 512) for i in range(2)]
        ko = [at(f"ko{i}", [P, 512], F32, dz + SLOTW * 4 + i * 2048) for i in range(3)]
        frow = at("frow", [NH_F, 2, SEQ], F32R, dz)
        pbuf = [at(f"pbuf{i}", [P, SEQ], F32, sz + i * 4096) for i in range(2)]
        sk1 = [at(f"sk1{i}", [P, SEQ], F32R, dz + i * 8192) for i in range(2)]
        sk2 = [at(f"sk2{i}", [P, SEQ], F32R, dz + 4096 + i * 8192) for i in range(2)]
        sq1 = [at(f"sq1{i}", [P, 4, P], F32R, dz + 16384 + i * 2048) for i in range(2)]
        spth = [at(f"spth{i}", [P, 2, 4, P], F32R, dz + 20480 + i * 8192) for i in range(2)]
        sptl = [at(f"sptl{i}", [P, 2, 4, P], F32R, dz + 24576 + i * 8192) for i in range(2)]
        svh = at("svh", [P, TT, 192], F32R, dz + 36864)
        svl = at("svl", [P, TT, 192], F32R, dz + 43008)
        fvh = at("fvh", [P, TT, 192], F32R, o)
        fvl = at("fvl", [P, TT, 192], F32R, o + 6144)
        q1 = [at("q1a", [P, SEQ], F32R, o + 12288), at("q1b", [P, SEQ], F32R, dz)]
        q2 = [at("q2a", [P, SEQ], F32R, o + 16384), at("q2b", [P, SEQ], F32R, dz + 4096)]
        k1 = [at("k1a", [P, SEQ], F32R, o + 20480), at("k1b", [P, SEQ], F32R, dz + 8192)]
        k2 = [at("k2a", [P, SEQ], F32R, dz + 12288), at("k2b", [P, SEQ], F32R, dz + 16384)]
        pth = [at(f"pth{i}", [P, 8 - 2 * i, 256], F32R, dz + 20480 + i * 16384) for i in range(2)]
        ptl = [at(f"ptl{i}", [P, 8 - 2 * i, 256], F32R, dz + 28672 + i * 14336) for i in range(2)]
        ckf = at("ckf", [P, 2, 512], F32, o + 25728)
        cvf = at("cvf", [P, 2, 512], F32, o + 42624)
        kft = at("kft", [P, 4, PAST + NEW], F32, o + 8192)
        cks = at("cks", [P, NKV, 2, HD], F32, o + 25728 + TOK * 4)
        cvs = at("cvs", [P, P], F32, o + 25728 + TOK * 4 + 1024)
        kst = at("kst", [P, NKV, WIN + NEW], F32, o + 14336)
        aqs = at("aqs", [P, 8, NEW], F32, o + 15616)
        ap = at("ap", [P, PAST + NEW], F32, o + 16640)
        apt = at("apt", [P, 3, P], F32, o + 17792)
        fs = at("fs", [NH_F, PAST + NEW], F32, o + 19328)
        fsn = at("fsn", [NH_F, PAST + NEW], F32, o + 20480)
        ada_w = [at(f"ada_w{i}", [P, 2048], F32, dz + i * SLOTW * 4) for i in range(6)]
        ada_v = [at(f"ada_v{i}", [P, 2048], F32, 6 * TOK * 4 + i * FM) for i in range(2)]
        cz = sz + 8192
        cpos = [cz]

        def small(name, shape, dt):
            n = int(np.prod(shape[1:])) * (2 if dt == BF16 else 4)
            t = nc.alloc_sbuf_tensor_at(name, shape, dt, offset=base + cpos[0])
            cpos[0] += (n + 31) // 32 * 32
            assert base + cpos[0] <= 229344, (name, cpos[0])
            return t

        ident = small("ident", [P, P], F32)
        onesd = small("onesd", [P, P], F32)
        tri = small("tri", [P, P], F32)
        cb = small("cb", [P, 512], BF16)
        identb = cb[:, 0:P]
        causb = cb[:, P:2 * P]
        winb = cb[:, 2 * P:4 * P]
        zerob = small("zerob", [P, P], BF16)
        vt = small("vt", [P, 80], F32)
        mod = small("mod", [P, 48, 2], F32)
        coef = small("coef", [P, 4, KT, 2], F32)
        sc = small("sc", [P, 2, KT], F32)
        sct = small("sct", [P, 3, 16], F32)
        snk = small("snk", [P, NH_S], F32)
        nsnk = small("nsnk", [P, NH_S], F32)
        ssnk = small("ssnk", [P, 2, 2], F32)
        bfg = small("bfg", [P, NH_F], F32)
        fg = small("fg", [P, TT + 1, NH_F], F32)
        fga = small("fga", [P, TT + 1, NH_F], F32)
        logf = small("logf", [P, TT + 1, NH_F], F32)
        lcum = small("lcum", [P, TT, NH_F], F32)
        lc = small("lc", [P, 2, NH_F], F32)
        lcs = small("lcs", [P, 2, NH_F], F32)
        qs_new = small("qs_new", [P, 4, NEW], F32)
        ks_new = small("ks_new", [P, NEW], F32)
        vs_new = small("vs_new", [P, P], F32)
        st = small("st", [P, 4, 20], F32)
        epst = small("epst", [P, 1], F32)
        vrow = at("vrow", [80, P], F32, sz + 6400)
        crow = at("crow", [16, P], F32, sz + 6912)
        xrow = [at(f"xrow{i}", [P, D], F32, i * 4096) for i in range(8)]
        orow = [at(f"orow{i}", [P, D], F32, i * 4096) for i in range(8)]
        mrow = [at(f"mrow{i}", [2, 2048], F32, 4 * TOK * 4 + i * FM) for i in range(2)]
        mrow4 = [at("mrow4a", [2, 1024], F32, sz), at("mrow4b", [2, 1024], F32, mt)]
        cload = at("cload", [P, 3 * P], F32, dz)

        ps = nc.alloc_psum_tensor("ps", [P, 8, 512], F32)

        xd = nc.dram_tensor("x_kept", [P, KT, TOK], F32, kind="Internal").ap()
        fd = nc.dram_tensor("f_rows", [NH_F, 2, SEQ], F32, kind="Internal").ap()

        S = {}

        def sm(name):
            if name not in S:
                S[name] = sem(name)
            return S[name]

        def wait_apart(e, held, *waits):
            values = [e.to_reg(v) for _, v in waits]
            e.wait_ge(sm(held[0]), held[1])
            for (name, _), v in zip(waits, values):
                e.wait_ge(sm(name), v)

        for i in range(2):
            sm(f"ada_v_in{i}"), sm(f"raw_in{i}"), sm(f"frow_in{i}")
        for i in range(8):
            sm(f"xrow_in{i}")

        for i in range(6):
            sm(f"ada_in{i}")
        for i in range(NCH):
            sm(f"x_saved{i}"), sm(f"ko_out{i}")

        PJ = [("f", 0, j, c) for c in range(NCH) for j in range(2)] + \
             [("f", b, j, c) for b in range(1, N_FM) for j in range(2) for c in range(NCH)] + \
             [("t", u, i) for u in range(N_TM) for i in range(TT + 1)]
        NPJ = len(PJ)

        def by_act(it):
            return it[0] == "f" or it[1] <= U_KV

        def by_dve(it):
            return it[0] == "t" and it[1] >= U_GATE

        def n_act(q):
            return sum(by_act(x) for x in PJ[:q])

        def n_dve(q):
            return sum(by_dve(x) for x in PJ[:q])

        def q_of(u, i):
            return PJ.index(("t", u, i))

        def n_of(it):
            return it[1] if it[0] == "f" else N_FM + it[1]

        def ends(q):
            return q == NPJ - 1 or n_of(PJ[q + 1]) != n_of(PJ[q])

        ROPES = [(u, i) for u in range(U_KV, N_TM) for i in range(TT + 1)]
        NR = len(ROPES)

        DB = {False: [4 + q % 4 for q in range(24)], True: [(6, 7, 2, 3)[q % 4] for q in range(24)]}

        def w_view(t, n):
            if N_FM <= n < W_WO0:
                w = TM_COLS[n - N_FM][1]
                return t[:, 0:KT * w].rearrange("p (k n) -> p k n", k=KT)
            if n < W_MLP0 or (n - W_MLP0) % 4 < 2:
                return t[:, 0:KT * 256].rearrange("p (k n) -> p k n", k=KT)
            return t[:, 0:HG * 512].rearrange("p (k n) -> p k n", k=HG)

        def w_size(n):
            return KT * 264 if n == N_FM + U_GATE else KT * 256

        def slot_uses(n):
            return n // 2

        USES = [(NW + 1) // 2, NW // 2]

        NBT = [1 if FOX_ORDER[e % 8] < 4 else 2 for e in range(16)]
        BT = [sum(NBT[:e]) for e in range(17)]

        block = ctx.enter_context(nc.Block())

        @block.sync
        def _(sp):
            for n_, t in enumerate((ident, onesd, tri)):
                sp.dma_start(t[:, :], a["consts"][:, n_ * P:(n_ + 1) * P]).then_inc(sm("const_in"), 16)
            sp.dma_start(cload[:, :], a["consts"][:, 3 * P:6 * P]).then_inc(sm("const_in"), 16)
            sp.dma_start(crow[:, :], a["c_rows"]).then_inc(sm("c_in"), 16)
            for i in range(TT + 1):
                if i >= 8:
                    sp.wait_ge(sm("x_tr"), 2 * (i - 7))
                if i < TT:
                    sp.dma_start(xrow[i % 8][:, :], a["x_prompt"][i * P:(i + 1) * P, :]).then_inc(sm(f"xrow_in{i % 8}"), 16)
                else:
                    sp.dma_start(xrow[i % 8][0:NEW, :], a["x_sample"]).then_inc(sm(f"xrow_in{i % 8}"), 16)

            def load_w(l, n, src, wbase=None):
                wait_apart(sp, ("const_in", 64), ("w_lo", (l * NW + max(0, n - 1)) if wbase is None else wbase - 1))
                sp.dma_start(w_view(raw[n % 2], n), src).then_inc(sm(f"raw_in{n % 2}"), 16)

            with sp.Fori(0, DEPTH) as l:
                l1 = bass.ds(l, 1)
                wait_apart(sp, ("const_in", 64), ("ao_lo", 2 * l), ("out_ks", l * 32))
                for t, n in ((vrow[0:48, :], "b_ada"), (vrow[48:80, :], "gains")):
                    sp.dma_start(t, a[n][l1, :, :].rearrange("l t p -> (l t) p")).then_inc(sm("vrow_in"), 16)
                for t, n in ((snk, "sinks_rows"), (bfg, "bf_rows")):
                    sp.dma_start(t[:, :], a[n][l1, :, :].rearrange("l p h -> (l p) h")).then_inc(sm("small_in"), 16)
                sp.dma_start(ssnk[:, 0, :], a["sinks_sample"][l1, :, :].rearrange("l p g -> (l p) g")).then_inc(sm("small_in"), 16)
                for t, n in ((costab, "cos"), (sintab, "sin")):
                    sp.dma_start(t[:, :, :], a[n].rearrange("p (i f) -> p i f", f=32)).then_inc(sm("small_in"), 16)
                sp.dma_start(lc[:, :, :], a["cache_fox_logf"][l1, :, :].rearrange("l (c p) h -> p (l c) h", p=P)).then_inc(sm("lcache_in"), 16)
                for n_, c_ in (("s_swa_k", "cache_swa_k"), ("s_swa_v", "cache_swa_v")):
                    sp.dma_start(a[n_][l1, 0:WIN - NEW, :], a[c_][l1, NEW:WIN, :]).then_inc(sm("cache_copied"), 16)
                wait_apart(sp, ("cb_ok", 1), ("w_lo", l * NW))
                for b in range(N_ADA1):
                    slot = ADA_SLOT[b]
                    if b == 2:
                        wait_apart(sp, ("cb_ok", 1), ("w_used", l * NW))
                    if b >= 6:
                        wait_apart(sp, ("cb_ok", 1), ("ada_mm", l * N_ADA + b - 5))
                    sp.dma_start(ada_w[slot][:, :].rearrange("p (k n) -> p k n", k=KT),
                                 a["w_ada"][l1, :, b * 256:(b + 1) * 256].rearrange("l (k p) n -> p (l k) n", p=P)).then_inc(sm(f"ada_in{slot}"), 16)
                for c in range(NCH):
                    sp.wait_ge(sm("x_ready"), l * 6 + 1 + c)
                    sp.dma_start(xd[:, :, c * CH:(c + 1) * CH], xr[:, :, c * CH:(c + 1) * CH]).then_inc(sm(f"x_saved{c}"), 16)
                sp.wait_ge(sm("ada_mm"), l * N_ADA + N_ADA1)
                for n in range(W_WO0):
                    c0, w = (FM_COLS[n], 256) if n < N_FM else TM_COLS[n - N_FM]
                    load_w(l, n, a["w_in"][l1, :, c0:c0 + w].rearrange("l (k p) n -> p (l k) n", p=P))
                sp.wait_ge(sm("ev_act"), l * n_act(NPJ) + n_act(q_of(U_GATE, TT) + 1))
                sp.dma_start(a["p_fox_v"][l1, :, :].rearrange("l (i p) n -> p (l i) n", p=P), vf[:, 0:TT, :]).then_inc(sm("out_v"), 16)
                sp.dma_start(a["s_fox_v"][l1, :, :].rearrange("l p n -> (l p) n"), vf[NEWP:P, TT, :]).then_inc(sm("out_v"), 16)
                sp.wait_ge(sm("logf_ok"), l + 1)
                sp.dma_start(a["p_fox_logf"][l1, :, :].rearrange("l (i p) n -> p (l i) n", p=P), logf[:, 0:TT, :]).then_inc(sm("out_small"), 16)
                sp.dma_start(a["s_fox_logf"][l1, :, :].rearrange("l p n -> (l p) n"), logf[NEWP:P, TT, :]).then_inc(sm("out_small"), 16)
                for i, n_ in ((TT - 1, "p"), (TT, "s")):
                    wait_apart(sp, ("const_in", 64), ("rope_ok", l * NR + i + 1), ("ev_act", l * n_act(NPJ) + n_act(q_of(U_KV, i) + 1)))
                    r0 = 0 if i < TT else NEWP
                    dst = lambda t: (a[t][l1, :, :] if r0 == 0 else a[t][l1, WIN - NEW:WIN, :]).rearrange("l p n -> (l p) n")
                    sp.dma_start(dst(n_ + "_swa_k"), rk[i - TT + 1][r0:P, :]).then_inc(sm("out_ks"), 16)
                    sp.dma_start(dst(n_ + "_swa_v"), vs[r0:P, i, :]).then_inc(sm("out_v"), 16)

                def load_ada(b):
                    sp.dma_start(ada_v[b % 2][:, :].rearrange("p (k n) -> p k n", k=KT),
                                 a["w_ada"][l1, :, (N_ADA1 + b) * 256:(N_ADA1 + b + 1) * 256].rearrange("l (k p) n -> p (l k) n", p=P)
                                 ).then_inc(sm(f"ada_v_in{b % 2}"), 16)

                sp.wait_ge(sm("f_lo"), 2 * (l + 1))
                sp.dma_start(fd, frow[:, :, :].bitcast(F32)).then_inc(sm("f_kept"), 16)
                for i in range(TT + 1):
                    if i == TT:
                        wait_apart(sp, ("cb_ok", 1), ("w_used", l * NW + W_WO0))
                        load_ada(0)
                        load_ada(1)
                    wait_apart(sp, ("cb_ok", 1), ("ko_ev", l * (TT + 1) + i + 1))
                    if i < TT:
                        sp.dma_start(a["p_fox_k"][l1, i * P:(i + 1) * P, :].rearrange("l p n -> (l p) n"), ko[i % 3][:, :]).then_inc(sm(f"ko_out{i % 3}"), 16)
                    else:
                        sp.dma_start(a["s_fox_k"][l1, :, :].rearrange("l p n -> (l p) n"), ko[i % 3][NEWP:P, :]).then_inc(sm(f"ko_out{i % 3}"), 16)
                for b in range(2, 16):
                    wait_apart(sp, ("cb_ok", 1), ("ada_mm", l * N_ADA + N_ADA1 + b - 1))
                    load_ada(b)
                wait_apart(sp, ("const_in", 64), ("f_kept", (l + 1) * 16), ("fz_ok", 5 * (l + 1)))
                def load_rows(t, h):
                    row = fd[bass.ds(t * 2 + h, 1), :, :].rearrange("h s n -> (h s) n")
                    sp.dma_start(k2[h][64:66, :].bitcast(F32), row).then_inc(sm(f"frow_in{h}"), 16)
                    sp.dma_start(q2[h][66:68, :].bitcast(F32), row).then_inc(sm(f"frow_in{h}"), 16)

                load_rows(0, 0)
                load_rows(0, 1)
                with sp.Fori(1, 4) as t:
                    for h in range(2):
                        sp.wait_ge(sm("fs_mm"), (l * 4 + t) * 16 - 8 + 8 * h)
                        load_rows(t, h)
                sp.wait_ge(sm("fs_mm"), (l * 4 + 3) * 16)
                cs = (a["cache_fox_k"], a["cache_fox_v"])
                for t, c_ in zip((ckf, cvf), cs):
                    sp.dma_start(t[:, :, :], c_[l1, :, :].rearrange("l (c p) n -> p (l c) n", p=P)).then_inc(sm("cache_in"), 16)
                for d in range(2):
                    sp.dma_start(cks[:, :, d, :], a["cache_swa_k"][l1, :, :].rearrange("l p (g e) -> (l p) g e", g=NKV)).then_inc(sm("cache_in"), 16)
                sp.dma_start(cvs[:, :], a["cache_swa_v"][l1, :, :].rearrange("l p n -> (l p) n")).then_inc(sm("cache_in"), 16)
                wait_apart(sp, ("const_in", 64), ("fo_lo", (l + 1) * 8))
                for b in range(2):
                    load_w(l, W_WO0 + b, a["w_out"][l1, :, b * 256:(b + 1) * 256].rearrange("l (k p) n -> p (l k) n", p=P))
                sp.wait_ge(sm("ao_lo"), 2 * (l + 1))
                for c in range(NCH):
                    sp.wait_ge(sm(f"x_saved{c}"), (l * 2 + 1) * 16)
                sp.dma_start(xf[:, :, :], xd).then_inc(sm("x_loaded"), 16)
                for b in range(2, 4):
                    load_w(l, W_WO0 + b, a["w_out"][l1, :, b * 256:(b + 1) * 256].rearrange("l (k p) n -> p (l k) n", p=P))

                def load_mlp(m, b):
                    if b < 2:
                        src = a["w_up"][l1, :, bass.ds((m * 2 + b) * 256, 256)].rearrange("l (k p) n -> p (l k) n", p=P)
                    else:
                        src = a["w_down"][l1, bass.ds(m * HG * P, HG * P), (b - 2) * 512:(b - 1) * 512].rearrange("l (k p) n -> p (l k) n", p=P)
                    load_w(l, W_MLP0 + b, src, l * NW + W_MLP0 + m * 4 + b)

                load_mlp(0, 0)
                load_mlp(0, 1)
                for c in range(NCH):
                    sp.wait_ge(sm("x_ready"), l * 6 + 4 + c)
                    sp.dma_start(xd[:, :, c * CH:(c + 1) * CH], xr[:, :, c * CH:(c + 1) * CH]).then_inc(sm(f"x_saved{c}"), 16)
                with sp.Fori(0, MSTEPS - 1) as m:
                    load_mlp(m, 2)
                    load_mlp(m, 3)
                    load_mlp(m + 1, 0)
                    load_mlp(m + 1, 1)
                load_mlp(MSTEPS - 1, 2)
                load_mlp(MSTEPS - 1, 3)
                wait_apart(sp, ("cb_ok", 1), ("w_used", l * NW + NW - 2))
                for c in range(NCH):
                    sp.wait_ge(sm(f"x_saved{c}"), (l * 2 + 2) * 16)
                sp.dma_start(xr[:, :, :], xd).then_inc(sm("x_loaded"), 16)
            for i in range(TT + 1):
                sp.wait_ge(sm("fin_ev0"), i + 1)
                sp.wait_ge(sm("fin_ev1"), i + 1)
                if i < TT:
                    sp.dma_start(a["y_prompt"][i * P:(i + 1) * P, :], orow[i % 8][:, :]).then_inc(sm("fin_out0" if i == 0 else "fin_out"), 16)
                else:
                    sp.dma_start(a["y_sample"], orow[i % 8][NEWP:P, :]).then_inc(sm("fin_out0" if i == 0 else "fin_out"), 16)
            sp.wait_ge(sm("fin_out0"), 16)
            sp.wait_ge(sm("fin_out"), 16 * TT)
            for i in range(3):
                sp.wait_ge(sm(f"ko_out{i}"), 16 * DEPTH * 3)
            sp.wait_ge(sm("out_v"), 16 * DEPTH * 4)
            sp.wait_ge(sm("out_ks"), 16 * DEPTH * 2)
            sp.wait_ge(sm("out_small"), 16 * DEPTH * 2)
            sp.wait_ge(sm("cache_copied"), 16 * DEPTH * 2)
            for c in range(NCH):
                sp.wait_ge(sm(f"x_saved{c}"), 16 * DEPTH * 2)
            sp.wait_ge(sm("f_kept"), 16 * DEPTH)

        @block.gpsimd
        def _(pool):
            pool.memset(zerob[:, :], 0.0).then_inc(sm("zero_ok"), 1)
            pool.memset(epst[:, :], EPS).then_inc(sm("eps_ok"), 1)
            with pool.Fori(0, DEPTH) as l:
                wait_apart(pool, ("zero_ok", 1), ("w_used", l * NW + W_WO0))
                pool.memset(svh[:, :, 64:128].bitcast(F32), 0.0).then_inc(sm("sz_ok"), 1)
                pool.memset(svl[:, :, 64:128].bitcast(F32), 0.0).then_inc(sm("sz_ok"), 1)
                wait_apart(pool, ("zero_ok", 1), ("so_lo", (l + 1) * 16))
                pool.memset(fvh[:, :, 64:128].bitcast(F32), 0.0)
                pool.memset(fvl[:, :, 64:128].bitcast(F32), 0.0).then_inc(sm("fz_ok"), 1)
                n = 1
                for h in range(2):
                    for stack, value in ((k2, 1.0), (q2, -1.0)):
                        wait_apart(pool, ("zero_ok", 1), ("fz_ok", l * 5 + n))
                        pool.memset(stack[h][64:68, :].bitcast(F32), value).then_inc(sm("fz_ok"), 1)
                        n += 1
                wait_apart(pool, ("zero_ok", 1), ("x_ready", l * 6 + 6))
                pool.memset(y[:, :, :], 0.0).then_inc(sm("y_zero"), 1)

        @block.scalar
        def _(act):
            def copy(out, in_, **kw):
                return act.activation(out, in_, ACT.Copy, **kw)

            act.wait_ge(sm("c_tr"), 1)
            act.activation(sct[:, 0, :], ps[:, 7, 0:16], ACT.Exp, scale=-1.0).then_inc(sm("silu_a"), 1)
            act.wait_ge(sm("eps_ok"), 1)
            for i in range(TT + 1):
                for hf in range(2):
                    q = 2 * i + hf
                    act.wait_ge(sm("x_tr"), q + 1)
                    w = P if i < TT else NEW
                    ins = copy(xr[:, 4 * hf:4 * hf + 4, i * P:i * P + w],
                               ps[:, q % 4, 0:4 * w].rearrange("p (t n) -> p t n", t=4))
                    ins.then_inc(*((sm("x_ready"), NCH) if q == 2 * TT + 1 else (sm("x_put"), 1)))

            def split_hi(l, n, wb=None):
                w = w_size(n)
                if wb is None:
                    act.wait_ge(sm("w_used"), l * NW + max(0, n - 1))
                    act.wait_ge(sm(f"raw_in{n % 2}"), (l * USES[n % 2] + slot_uses(n) + 1) * 16)
                else:
                    cnt, used = wb
                    act.wait_ge(sm("w_used"), used)
                    act.wait_ge(sm(f"raw_in{n % 2}"), cnt)
                copy(wh[n % 2][:, 0:w], raw[n % 2][:, 0:w]).then_inc(sm("w_hi"), 1)

            def norm_idx(l, nu, c):
                return l * 12 + nu * 3 + c

            def norm_rb(l, nu, c):
                idx, s = norm_idx(l, nu, c), (nu * 3 + c) % 2
                act.wait_ge(sm("mean_ok"), idx + 1)
                if nu * 3 + c:
                    act.wait_ge(sm("nt_ok"), idx - 1)
                else:
                    act.wait_ge(sm("nt_ok"), idx)
                act.activation(rb[s][:, :], ps[:, 4 + s, 0:CH], ACT.Ln, bias=epst[:, 0:1]).then_inc(sm("ln_ok"), 1)
                act.wait_ge(sm("ln_ok"), idx + 1)
                act.activation(rb[s][:, :], rb[s][:, :], ACT.Exp, scale=-0.5).then_inc(sm("rb_ok"), 1)

            def pre_sq(l, nu, c):
                cs = slice(c * CH, (c + 1) * CH)
                act.wait_ge(sm("x_ready"), l * 6 + 1 + (3 if nu == NPRE2 else 0) + c)
                act.activation(sq[:, :, cs], xr[:, :, cs], ACT.Square).then_inc(sm("sq_ok"), 1)

            def pre_hi(l, nu, c):
                cs = slice(c * CH, (c + 1) * CH)
                act.wait_ge(sm("h_full"), l * 6 + (3 if nu == NPRE2 else 0) + c + 1)
                copy(hh[:, :, cs], th[:, :, cs]).then_inc(sm("h_hi"), 1)

            def post_sq(l, nu, c, base):
                cs = slice(c * CH, (c + 1) * CH)
                name, per = ("y_ev", 4) if nu == NPOST1 else ("d_add", 8)
                act.wait_ge(sm(name), base + per * (c + 1))
                act.activation(sq[:, :, cs], y[:, :, cs], ACT.Square).then_inc(sm("sq_ok"), 1)

            with act.Fori(0, DEPTH) as l:
                pre_sq(l, NPRE1, 0)
                pre_sq(l, NPRE1, 1)
                for h in range(2):
                    act.wait_ge(sm("ada_mm"), l * N_ADA + 4 * (h + 1))
                    copy(mrow4[h][:, :].rearrange("p (b n) -> p b n", b=2), ps[0:2, 2 * h:2 * h + 2, :]).then_inc(sm("mrow4_ok"), 1)
                norm_rb(l, NPRE1, 0)
                pre_sq(l, NPRE1, 2)
                norm_rb(l, NPRE1, 1)
                pre_hi(l, NPRE1, 0)
                act.wait_ge(sm("ada_mm"), l * N_ADA + N_ADA1)
                split_hi(l, 0)
                norm_rb(l, NPRE1, 2)
                pre_hi(l, NPRE1, 1)
                split_hi(l, 1)
                pre_hi(l, NPRE1, 2)
                def ko_evac(i):
                    act.wait_ge(sm("ko_mm"), l * (TT + 1) + i + 1)
                    if i >= 3:
                        act.wait_ge(sm(f"ko_out{i % 3}"), (l * 3 + i // 3) * 16)
                    copy(ko[i % 3][:, :], ps[:, 6 + i % 2, :]).then_inc(sm("ko_ev"), 1)

                nr = 0
                for q, it in enumerate(PJ):
                    b = q % 4
                    if by_act(it):
                        act.wait_ge(sm("pj_mm"), l * NPJ + q + 1)
                    if it[0] == "f":
                        _, blk, j, c = it
                        dst = (qf, kf)[blk // 2]
                        copy(dst[:, 2 * (blk % 2) + j, c * CH:(c + 1) * CH], ps[:, b, 0:CH]).then_inc(sm("ev_act"), 1)
                    else:
                        _, u, i = it
                        if u == U_GATE:
                            act.wait_ge(sm("fg_a"), l * 10 + i + 1)
                        if u < U_KV:
                            copy(vf[:, i, u * 256:(u + 1) * 256], ps[:, b, 0:256]).then_inc(sm("ev_act"), 1)
                        if u == U_KV:
                            act.wait_ge(sm("rope_t"), l * NR + i + 1)
                            copy(vs[:, i, :], ps[:, b, P:256]).then_inc(sm("ev_act"), 1)
                        if u == N_TM - 1 and i == 0:
                            act.wait_ge(sm("w_lo"), l * NW + W_WO0)
                            act.wait_ge(sm("f_mm"), l + 1)
                            for h in range(2):
                                copy(frow[:, 0, h * 512:(h + 1) * 512], ps[0:NH_F, 6 + h, :]).then_inc(sm("f_hi"), 1)
                        if u == N_TM - 1 and i >= 1:
                            ko_evac(i - 1)
                        if u >= U_KV:
                            act.wait_ge(sm("rtr_mm"), l * NR + nr + 1)
                            w0, w1 = (0, P) if i < TT else (NEWP, P)
                            n_ = 1 if u == U_KV else 2
                            src = ps[:, 4 + nr % 2, 0:n_ * P].rearrange("p (t n) -> p t n", t=n_)[:, :, w0:w1]
                            t0 = 2 * (u - U_KV - 1)
                            dst = (ks[:, None, i * P:i * P + w1 - w0] if u == U_KV
                                   else qs[:, t0:t0 + 2, i * P:i * P + w1 - w0])
                            copy(dst, src).then_inc(sm("rtr_ev"), 1)
                            nr += 1
                        if u == U_KV and i == 1:
                            act.wait_ge(sm("fg_a"), l * 10 + 10)
                            act.activation(fga[:, :, :], fga[:, :, :], ACT.Exp, scale=-1.0).then_inc(sm("fg_b"), 1)
                            act.wait_ge(sm("fg_b"), 2 * l + 1)
                            act.activation(fga[:, :, :], fga[:, :, :], ACT.Ln, bias=1.0).then_inc(sm("fg_b"), 1)
                    if ends(q) and n_of(it) + 2 < W_WO0:
                        split_hi(l, n_of(it) + 2)
                ko_evac(TT)
                act.wait_ge(sm("ev_act"), (l + 1) * n_act(NPJ))
                act.wait_ge(sm("rtr_ev"), (l + 1) * NR)
                copy(qs_new[:, :, :], qs[:, :, SEQ:TOK]).then_inc(sm("new_kept"), 1)
                copy(ks_new[:, :], ks[:, SEQ:TOK]).then_inc(sm("new_kept"), 1)
                copy(vs_new[:, :], vs[:, TT, :]).then_inc(sm("new_kept"), 1)

                def k_hi(g):
                    r = slice(64 * g, 64 * g + 64)
                    copy(sk1[g][0:64, :], ks[r, 0:SEQ]).then_inc(sm("sk_hi"), 1)
                    copy(sk1[g][64:128, :], ks[r, 0:SEQ]).then_inc(sm("sk_hi"), 1)

                def v_hi(g):
                    if g == 1:
                        act.wait_ge(sm("so_mm"), l * 16 + 8)
                    dst = svh[:, :, :].rearrange("p t (a n) -> p t a n", n=64)[:, :, 0:3:2, :]
                    src = vs[:, 0:TT, None, 64 * g:64 * g + 64].broadcast_to([P, TT, 2, 64])
                    copy(dst, src).then_inc(sm("sv_hi"), 1)

                def q_hi(w):
                    g, i = w // 8, w % 8
                    if w >= 2:
                        act.wait_ge(sm("s_mm"), l * 16 + w - 1)
                    for d in range(2):
                        r = slice(64 * d, 64 * d + 64)
                        copy(sq1[w % 2][r, d:4:2, :], qs[r, 2 * g:2 * g + 2, i * P:(i + 1) * P], scale=SCALE).then_inc(sm("sq_hi"), 1)

                def expo(w):
                    W = P if w % 8 == 0 else 256
                    s4 = st[:, w % 4, :]
                    act.wait_ge(sm("s_mn"), l * 16 + w + 1)
                    if w >= 2:
                        act.wait_ge(sm("st_mm"), l * 16 + w - 1)
                    else:
                        act.wait_ge(sm("out_ks"), (l + 1) * 32)
                    for x in range(4):
                        ins = act.activation(pbuf[w % 2][:, x * W:(x + 1) * W],
                                             ps[:, 2 * (w % 2) + x // 2, (x % 2) * 256:(x % 2) * 256 + W], ACT.Exp,
                                             bias=s4[:, 4 + x:5 + x], accum_out=s4[:, 8 + x:9 + x])
                    ins.then_inc(sm("s_exp"), 1)
                    act.wait_ge(sm("s_smx"), l * 16 + w + 1)
                    act.activation(s4[:, 12:16], s4[:, 12:16], ACT.Exp).then_inc(sm("s_es"), 1)

                def pt_hi(w):
                    nk = 1 if w % 8 == 0 else 2
                    act.wait_ge(sm("st_mm"), l * 16 + w + 1)
                    if w >= 2:
                        act.wait_ge(sm("so_mm"), l * 16 + w - 1)
                    copy(spth[w % 2][:, 0:nk, :, :],
                         ps[:, 4:4 + nk, :].rearrange("p k (h n) -> p k h n", h=4)).then_inc(sm("st_hi"), 1)

                def o_hi(w):
                    g, i = w // 8, w % 8
                    act.wait_ge(sm("so_mm"), l * 16 + w + 1)
                    copy(mrow[g][:, i * 256:(i + 1) * 256], ps[0:2, 6 + w % 2, 256:512])
                    copy(hh[:, 2 * g:2 * g + 2, i * P:(i + 1) * P],
                         ps[:, 6 + w % 2, 0:256].rearrange("p (t n) -> p t n", t=2)).then_inc(sm("so_hi"), 1)

                act.wait_ge(sm("w_used"), l * NW + W_WO0)
                act.wait_ge(sm("f_kept"), (l + 1) * 16)
                k_hi(0)
                q_hi(0)
                q_hi(1)
                for w in range(-1, 18):
                    if 0 <= w + 1 < 16:
                        expo(w + 1)
                    if 0 <= w < 16:
                        pt_hi(w)
                    if 0 <= w - 2 < 16:
                        o_hi(w - 2)
                    if 2 <= w + 3 < 16:
                        q_hi(w + 3)
                    if w == -1:
                        v_hi(0)
                    if w == 0:
                        for i in range(3):
                            act.wait_ge(sm(f"ko_out{i}"), (l + 1) * 48)
                        k_hi(1)
                    if w == 8:
                        v_hi(1)

                act.wait_ge(sm("so_lo"), (l + 1) * 16)
                act.wait_ge(sm("fz_ok"), 5 * (l + 1))
                def stack_hi(t, h, part, first=False):
                    pr = l * 4 + t
                    r = slice(64 * h, 64 * h + 64)
                    t1 = bass.ds(t, 1)
                    act.wait_ge(sm("fs_mm"), pr * 16 if h or first else pr * 16 - 8)
                    if part == 0:
                        src = qf[r, t1, 0:SEQ].rearrange("p t n -> p (t n)")
                        copy(q1[h][r, :], src, scale=SCALE).then_inc(sm("fq_hi"), 1)
                        copy(q2[h][0:64, :], src, scale=SCALE).then_inc(sm("fq_hi"), 1)
                    else:
                        src = kf[r, t1, 0:SEQ].rearrange("p t n -> p (t n)")
                        copy(k1[h][0:64, :], src).then_inc(sm("fq_hi"), 1)
                        copy(k1[h][64:128, :], src).then_inc(sm("fq_hi"), 1)

                def expo(t, e, first=False):
                    pr = l * 4 + t
                    i = FOX_ORDER[e % 8]
                    n, nb = (i + 1) * P, (1 if i < 4 else 2)
                    s4 = st[:, e % 4, :]
                    act.wait_ge(sm("fs_nm"), pr * 16 + e + 1)
                    before = BT[e - 1] if e >= 1 else 0 if first else BT[15] - 24
                    act.wait_ge(sm("ft_mm"), pr * 24 + before)
                    act.activation(pbuf[e % 2][:, 0:n].rearrange("p (c n) -> p c n", c=nb),
                                   ps[:, 2 * (e % 2):2 * (e % 2) + nb, 0:n // nb], ACT.Exp,
                                   bias=s4[:, 0:1], accum_out=s4[:, 1:2]).then_inc(sm("fs_exp"), 1)

                def o_hi(t, b):
                    act.wait_ge(sm("pv_mm"), (l * 4 + t) * 8 + (6, 8)[b])
                    c0 = (512, 0)[b]
                    copy(hh[:, bass.ds(t + 4, 1), c0:c0 + 512].rearrange("p t n -> p (t n)"),
                         ps[:, 6 + b, :]).then_inc(sm("fo_hi"), 1)

                def fox_pair(t, first, last):
                    pr = act.snap(l * 4 + t)

                    def pt_hi(e):
                        i = FOX_ORDER[e % 8]
                        jb = (e // 2) % 2
                        act.wait_ge(sm("pv_mm"), pr * 8 + (max(0, e // 2 - 1) if first else e // 2 - 1))
                        for bb in range(NBT[e]):
                            g = BT[e] + bb
                            k0, k1_ = 4 * bb, min(4 * bb + 4, i + 1)
                            act.wait_ge(sm("ft_mm"), pr * 24 + g + 1)
                            copy(pth[jb][:, k0:k1_, (i % 2) * P:(i % 2 + 1) * P],
                                 ps[:, 4 + g % 2, 0:(k1_ - k0) * P].rearrange("p (k n) -> p k n", n=P)).then_inc(sm("ft_hi"), 1)

                    for e in range(16):
                        if e < 15:
                            expo(t, e + 1)
                        elif not last:
                            expo(t + 1, 0)
                        pt_hi(e)
                        if e in (2, 3):
                            stack_hi(t, 1, e - 2)
                        if e == 1:
                            act.wait_ge(sm("pv_mm"), pr * 8)
                            vdst = fvh[:, :, :].rearrange("p t (a n) -> p t a n", n=64)[:, :, 0:3:2, :]
                            vsrc = vf[:, 0:TT, bass.ds(t * P, P)].rearrange("p t (a n) -> p t a n", n=64)
                            copy(vdst, vsrc).then_inc(sm("fv_hi"), 1)
                            if not first:
                                o_hi(t - 1, 1)
                        if e in (8, 9) and not last:
                            stack_hi(t + 1, 0, e - 8)
                        if e == 13:
                            o_hi(t, 0)

                stack_hi(0, 0, 0, True)
                stack_hi(0, 0, 1, True)
                expo(0, 0, True)
                fox_pair(0, True, False)
                with act.Fori(1, 3) as t:
                    fox_pair(t, False, False)
                fox_pair(3, False, True)
                o_hi(3, 1)

                act.wait_ge(sm("ck_tr"), l + 1)
                act.wait_ge(sm("new_kept"), 3 * (l + 1))
                for c in range(2):
                    copy(kft[:, :, c * P:(c + 1) * P], ps[:, c, :].rearrange("p (t n) -> p t n", t=4))
                copy(kft[:, :, PAST:], kf[:, :, SEQ:TOK])
                copy(kst[:, :, 0:WIN], ps[:, 2, 0:256].rearrange("p (g n) -> p g n", g=2))
                for g in range(2):
                    for d in range(2):
                        copy(kst[64 * d:64 * d + 64, g, WIN:], ks_new[64 * g:64 * g + 64, :])
                copy(fs[:, :], ps[0:NH_F, 3, 0:PAST + NEW])
                copy(fsn[:, :], ps[0:NH_F, 3, 0:PAST + NEW], scale=-1.0).then_inc(sm("ck_ev"), 1)
                copy(aqs[:, 0:4, :], qs_new[:, :, :], scale=SCALE).then_inc(sm("aq_ok"), 1)
                copy(aqs[:, 4:8, :], qf[:, :, SEQ:TOK], scale=SCALE).then_inc(sm("aq_ok"), 1)
                for w in range(4):
                    W = WIN + NEW if w < 2 else PAST + NEW
                    s4 = st[:, w, :]
                    act.wait_ge(sm("a_mn"), l * 4 + w + 1)
                    if w >= 1:
                        act.wait_ge(sm("at_mm"), l * 4 + w)
                    act.activation(ap[:, 0:W], ps[:, w % 2, 0:W], ACT.Exp, bias=s4[:, 1:2], accum_out=s4[:, 2:3]).then_inc(sm("a_exp"), 1)
                    if w < 2:
                        act.wait_ge(sm("a_smx"), l * 2 + w + 1)
                        act.activation(s4[:, 3:4], s4[:, 3:4], ACT.Exp).then_inc(sm("a_es"), 1)
                    act.wait_ge(sm("at_mm"), l * 4 + w + 1)
                    if w >= 1:
                        act.wait_ge(sm("ao_mm"), l * 4 + w)
                    copy(apt[:, 0:2 if w < 2 else 3, :],
                         ps[:, 2, 0:P * (2 if w < 2 else 3)].rearrange("p (k n) -> p k n", n=P)).then_inc(sm("at_ev"), 1)
                    if w % 2:
                        act.wait_ge(sm("ao_mm"), l * 4 + w + 1)
                        t0 = 0 if w < 2 else 4
                        copy(hh[:, t0:t0 + 4, SEQ:TOK], ps[:, 3, 0:P].rearrange("p (t n) -> p t n", t=4)).then_inc(sm("ao_hi"), 1)
                    if w < 2:
                        split_hi(l, W_WO0 + w)

                for r in range(2):
                    for q in range(12):
                        if q == 6 and r == 0:
                            split_hi(l, W_WO0 + 2)
                        b, j, c = (q // 6, (q // 3) % 2, q % 3) if r == 0 else ((q // 2) % 2, q % 2, q // 4)
                        act.wait_ge(sm("y_mm"), l * 24 + r * 12 + q + 1)
                        copy(y[:, r * 4 + b * 2 + j, c * CH:(c + 1) * CH], ps[:, q % 4, 0:CH]).then_inc(sm("y_ev"), 1)
                        if r == 1 and q % 4 == 3:
                            post_sq(l, NPOST1, c, l * 24 + 12)
                        if r == 1 and q in (6, 10):
                            norm_rb(l, NPOST1, q // 4 - 1)
                    if r == 0:
                        split_hi(l, W_WO0 + 3)
                act.wait_ge(sm("w_used"), l * NW + W_MLP0)
                split_hi(l, W_MLP0)
                norm_rb(l, NPOST1, 2)
                pre_sq(l, NPRE2, 0)
                norm_rb(l, NPRE2, 0)
                pre_sq(l, NPRE2, 1)
                norm_rb(l, NPRE2, 1)
                pre_sq(l, NPRE2, 2)
                pre_hi(l, NPRE2, 0)
                norm_rb(l, NPRE2, 2)
                pre_hi(l, NPRE2, 1)
                pre_hi(l, NPRE2, 2)

                def mlp_step(m, last):
                    mm = act.snap(l * MSTEPS + m)
                    n0 = act.snap(l * NW + W_MLP0 + m * 4)
                    sl = [act.snap(l * USES[(W_MLP0 + s_) % 2] + slot_uses(W_MLP0 + s_) + m * 2) for s_ in range(2)]

                    def split(b):
                        split_hi(l, W_MLP0 + b, ((sl[b % 2] + (b // 2 + 1)) * 16, n0 + (b - 1)))

                    def u_hi(q):
                        c = q % 3
                        act.wait_ge(sm("u_sq"), mm * 12 + q + 1)
                        if q == 0:
                            act.wait_ge(sm("w_used"), n0)
                        copy(uh[:, q // 3, c * CH:(c + 1) * CH], u_t[q % 2][:, :]).then_inc(sm("u_hi"), 1)

                    split(1)
                    for q in range(12):
                        if q == 6:
                            split(2)
                        act.wait_ge(sm("u_mm"), mm * 12 + q + 1)
                        act.wait_ge(sm("u_sq"), mm * 12 + max(0, q - 1))
                        act.activation(r_t[q % 2][:, :], ps[:, q % 4, 0:CH], ACT.Relu).then_inc(sm("u_relu"), 1)
                        if q >= 1:
                            u_hi(q - 1)
                    u_hi(11)
                    split(3)
                    if not last:
                        split(4)
                        return
                    base = mm * 24
                    post_sq(l, NPOST2, 0, base)
                    norm_rb(l, NPOST2, 0)
                    post_sq(l, NPOST2, 1, base)
                    norm_rb(l, NPOST2, 1)
                    post_sq(l, NPOST2, 2, base)
                    norm_rb(l, NPOST2, 2)

                with act.Fori(0, MSTEPS - 1) as m:
                    mlp_step(m, False)
                mlp_step(MSTEPS - 1, True)

            for i in range(TT + 1):
                act.wait_ge(sm("fin_tr"), 2 * i + 1)
                if i >= 8:
                    act.wait_ge(sm("fin_out0"), 16)
                copy(orow[i % 8][:, 0:512], ps[:, (2 * i) % 4, :]).then_inc(sm("fin_ev0"), 1)

        @block.vector
        def _(dve):
            dve.wait_ge(sm("const_in"), 64)
            dve.tensor_copy(cb[:, 0:P], ident[:, :])
            dve.tensor_copy(cb[:, P:4 * P], cload[:, :]).then_inc(sm("cb_ok"), 1)
            dve.wait_ge(sm("silu_a"), 1)
            dve.tensor_scalar(sct[:, 1, :], sct[:, 0, :], 1.0, None, ALU.add).then_inc(sm("silu_b"), 1)
            dve.wait_ge(sm("silu_b"), 1)
            dve.reciprocal(sct[:, 2, :], sct[:, 1, :]).then_inc(sm("silu_b"), 1)
            dve.wait_ge(sm("silu_b"), 2)
            dve.tensor_tensor(sc[:, :, :].rearrange("p s k -> p (s k)"), ps[:, 7, 0:16], sct[:, 2, :], ALU.mult).then_inc(sm("silu_b"), 1)

            def split_lo(l, n, n0=None):
                w = w_size(n)
                dve.wait_ge(sm("w_hi"), (l * NW + n + 1) if n0 is None else n0 + 1)
                dve.tensor_tensor(wl[n % 2][:, 0:w], raw[n % 2][:, 0:w], wh[n % 2][:, 0:w].bitcast(F32), ALU.subtract).then_inc(sm("w_lo"), 1)

            def pre_scale(l, nu, c):
                pn = 0 if nu == NPRE1 else 1
                b0 = 24 * pn
                cs = slice(c * CH, (c + 1) * CH)
                idx = l * 12 + nu * 3 + c
                dve.wait_ge(sm("rb_ok"), idx + 1)
                dve.wait_ge(sm(f"x_saved{c}"), (l * 2 + pn + 1) * 16)
                dve.tensor_tensor(th[:, :, cs], xr[:, :, cs], rb[(nu * 3 + c) % 2][:, None, :].broadcast_to([P, KT, CH]), ALU.mult).then_inc(sm("nt_ok"), 1)
                dve.wait_ge(sm("nt_ok"), idx + 1)
                for k in range(KT):
                    for (c0, c1, s_) in stream_pieces(c):
                        ins = dve.tensor_scalar(th[:, k, c0:c1], th[:, k, c0:c1], coef[:, 2 * pn, k, s_:s_ + 1],
                                                mod[:, b0 + k, s_:s_ + 1], ALU.mult, ALU.add)
                ins.then_inc(sm("h_full"), 1)

            def pre_lo(l, nu, c):
                pn = 0 if nu == NPRE1 else 1
                cs = slice(c * CH, (c + 1) * CH)
                dve.wait_ge(sm("h_hi"), l * 6 + pn * 3 + c + 1)
                dve.tensor_tensor(hl[:, :, cs], th[:, :, cs], hh[:, :, cs].bitcast(F32), ALU.subtract).then_inc(sm("h_ok"), 1)

            def post_norm(l, nu, c):
                pn = 0 if nu == NPOST1 else 1
                cs = slice(c * CH, (c + 1) * CH)
                idx = l * 12 + nu * 3 + c
                x_in = xf if nu == NPOST1 else xr
                dve.wait_ge(sm("rb_ok"), idx + 1)
                dve.tensor_tensor(y[:, :, cs], y[:, :, cs], rb[(nu * 3 + c) % 2][:, None, :].broadcast_to([P, KT, CH]), ALU.mult).then_inc(sm("nt_ok"), 1)
                dve.wait_ge(sm("nt_ok"), idx + 1)
                dve.wait_ge(sm("x_loaded"), l * 32 + 16 * (pn + 1))
                for k in range(KT):
                    for (c0, c1, s_) in stream_pieces(c):
                        ins = dve.scalar_tensor_tensor(out=xr[:, k, c0:c1], in0=y[:, k, c0:c1], scalar=coef[:, 2 * pn + 1, k, s_:s_ + 1],
                                                       in1=x_in[:, k, c0:c1], op0=ALU.mult, op1=ALU.add)
                ins.then_inc(sm("x_ready"), 1)

            def coefs(which):
                for n_ in which:
                    m0, add = ((8, 1.0), (16, 0.0), (32, 1.0), (40, 0.0))[n_]
                    ins = dve.scalar_tensor_tensor(out=coef[:, n_, :, :], in0=mod[:, m0:m0 + KT, :], scalar=add,
                                                   in1=vt[:, 48 + 8 * n_:56 + 8 * n_][:, :, None].broadcast_to([P, KT, 2]), op0=ALU.add, op1=ALU.mult)
                ins.then_inc(sm("coef_ok"), 1)

            with dve.Fori(0, DEPTH) as l:
                dve.wait_ge(sm("v_tr"), l + 1)
                dve.tensor_copy(vt[:, :], ps[:, 7, 0:80]).then_inc(sm("vt_ok"), 1)
                dve.wait_ge(sm("vt_ok"), l + 1)
                dve.wait_ge(sm("small_in"), (l + 1) * 80)
                dve.tensor_scalar(nsnk[:, :], snk[:, :], -1.0, None, ALU.mult)
                dve.tensor_scalar(ssnk[:, 1, :], ssnk[:, 0, :], -1.0, None, ALU.mult).then_inc(sm("nsnk_ok"), 1)
                dve.wait_ge(sm("lcache_in"), (l + 1) * 16)
                dve.tensor_scalar(lcs[:, 0, :], lc[:, 0, :], float(D), None, ALU.mult).then_inc(sm("lcs_ok"), 1)
                dve.wait_ge(sm("lcs_ok"), 2 * l + 1)
                dve.scalar_tensor_tensor(out=lcs[:, 1, :], in0=lc[:, 1, :], scalar=float(D), in1=lcs[:, 0, :], op0=ALU.mult, op1=ALU.add).then_inc(sm("lcs_ok"), 1)
                dve.wait_ge(sm("mod_mm"), 2 * l + 1)
                dve.tensor_tensor(mod[:, 0:2 * N_ADA1, :], ps[:, 6, 0:4 * N_ADA1].rearrange("p (j s) -> p j s", s=2),
                                  vt[:, 0:2 * N_ADA1][:, :, None].broadcast_to([P, 2 * N_ADA1, 2]), ALU.add).then_inc(sm("ada_ev"), 1)
                dve.wait_ge(sm("ada_ev"), 2 * l + 1)
                coefs([0])
                dve.wait_ge(sm("coef_ok"), 2 * l + 1)
                pre_scale(l, NPRE1, 0)
                pre_scale(l, NPRE1, 1)
                pre_lo(l, NPRE1, 0)
                split_lo(l, 0)
                pre_scale(l, NPRE1, 2)
                pre_lo(l, NPRE1, 1)
                split_lo(l, 1)
                pre_lo(l, NPRE1, 2)

                nr = 0
                for q, it in enumerate(PJ):
                    b = q % 4
                    u, i = (it[1], it[2]) if it[0] == "t" else (-1, 0)
                    if u >= U_KV:
                        nh = 2 if u == U_KV else 4
                        out = rk[i - TT + 1] if u == U_KV and i >= TT - 1 else ro[nr % 2]
                        src = ps[:, b, 0:nh * HD].rearrange("p (h s f) -> p h s f", h=nh, s=2)
                        t1 = rt1[:, 0:nh * HD].rearrange("p (h s f) -> p h s f", h=nh, s=2)
                        t2 = rt2[:, 0:nh * HD].rearrange("p (h s f) -> p h s f", h=nh, s=2)
                        dst = out[:, 0:nh * HD].rearrange("p (h s f) -> p h s f", h=nh, s=2)
                        cos2 = costab[:, i, None, :].broadcast_to([P, nh * 2, 32])
                        sin1 = sintab[:, i, None, :].broadcast_to([P, nh, 32])
                        dve.wait_ge(sm("pj_mm"), l * NPJ + q + 1)
                        dve.wait_ge(sm("rope_ok"), l * NR + nr)
                        dve.tensor_tensor(rt1[:, 0:nh * HD].rearrange("p (h f) -> p h f", f=32),
                                          ps[:, b, 0:nh * HD].rearrange("p (h f) -> p h f", f=32), cos2, ALU.mult)
                        dve.tensor_tensor(t2[:, :, 0, :], src[:, :, 1, :], sin1, ALU.mult)
                        dve.tensor_tensor(t2[:, :, 1, :], src[:, :, 0, :], sin1, ALU.mult).then_inc(sm("rope_t"), 1)
                        dve.wait_ge(sm("rope_t"), l * NR + nr + 1)
                        if nr >= 2:
                            dve.wait_ge(sm("rtr_mm"), l * NR + nr - 1)
                        dve.tensor_tensor(dst[:, :, 0, :], t1[:, :, 0, :], t2[:, :, 0, :], ALU.subtract)
                        dve.tensor_tensor(dst[:, :, 1, :], t1[:, :, 1, :], t2[:, :, 1, :], ALU.add).then_inc(sm("rope_ok"), 1)
                        nr += 1
                    if u == U_GATE:
                        dve.wait_ge(sm("pj_mm"), l * NPJ + q + 1)
                        dve.tensor_tensor(fg[:, i, :], ps[:, b, 256:264], bfg[:, :], ALU.add).then_inc(sm("fg_a"), 1)
                    if ends(q) and n_of(it) + 2 < W_WO0:
                        split_lo(l, n_of(it) + 2)
                    if u == U_GATE and i == TT:
                        dve.wait_ge(sm("fg_a"), l * 10 + 9)
                        dve.scalar_tensor_tensor(out=fga[:, :, :].rearrange("p i h -> p (i h)"), in0=fg[:, :, :].rearrange("p i h -> p (i h)"),
                                                 scalar=-1.0, in1=fg[:, :, :].rearrange("p i h -> p (i h)"), op0=ALU.mult, op1=ALU.max).then_inc(sm("fg_a"), 1)
                    if u == U_KV and i == 4:
                        dve.wait_ge(sm("fg_b"), 2 * l + 2)
                        dve.scalar_tensor_tensor(out=logf[:, :, :].rearrange("p i h -> p (i h)"), in0=fg[:, :, :].rearrange("p i h -> p (i h)"),
                                                 scalar=0.0, in1=fga[:, :, :].rearrange("p i h -> p (i h)"), op0=ALU.min, op1=ALU.subtract).then_inc(sm("logf_ok"), 1)
                        dve.memset(lcum[:, 0, :], 0.0).then_inc(sm("lcum_ok"), 1)
                        dve.wait_ge(sm("logf_ok"), l + 1)
                    if u == U_KV + 1 and 1 <= i < TT:
                        dve.wait_ge(sm("lcum_ok"), l * TT + i)
                        dve.scalar_tensor_tensor(out=lcum[:, i, :], in0=logf[:, i - 1, :], scalar=float(D), in1=lcum[:, i - 1, :],
                                                 op0=ALU.mult, op1=ALU.add).then_inc(sm("lcum_ok"), 1)
                    if u == N_TM - 1 and i == 0:
                        for h in range(2):
                            dve.wait_ge(sm("f_hi"), 2 * l + h + 1)
                            dve.tensor_tensor(frow[:, 1, h * 512:(h + 1) * 512], ps[0:NH_F, 6 + h, :],
                                              frow[:, 0, h * 512:(h + 1) * 512].bitcast(F32), ALU.subtract).then_inc(sm("f_lo"), 1)
                def k_lo(g):
                    r = slice(64 * g, 64 * g + 64)
                    dve.wait_ge(sm("sk_hi"), l * 4 + 2 * g + 2)
                    for d in range(2):
                        ins = dve.tensor_tensor(sk2[g][64 * d:64 * d + 64, :], ks[r, 0:SEQ], sk1[g][r, :].bitcast(F32), ALU.subtract)
                    ins.then_inc(sm("sk_lo"), 1)

                def v_lo(g):
                    dve.wait_ge(sm("sv_hi"), l * 2 + g + 1)
                    half = lambda t: t[:, :, :].rearrange("p t (a n) -> p t a n", n=64)[:, :, 0:3:2, :]
                    dve.tensor_tensor(half(svl), vs[:, 0:TT, None, 64 * g:64 * g + 64].broadcast_to([P, TT, 2, 64]),
                                      half(svh).bitcast(F32), ALU.subtract).then_inc(sm("sv_lo"), 1)

                def q_lo(w):
                    g, i = w // 8, w % 8
                    for d in range(2):
                        r, ro_ = slice(64 * d, 64 * d + 64), slice(64 - 64 * d, 128 - 64 * d)
                        dve.wait_ge(sm("sq_hi"), l * 32 + 2 * w + d + 1)
                        ins = dve.scalar_tensor_tensor(out=sq1[w % 2][ro_, d:4:2, :], in0=qs[r, 2 * g:2 * g + 2, i * P:(i + 1) * P], scalar=SCALE,
                                                       in1=sq1[w % 2][r, d:4:2, :].bitcast(F32), op0=ALU.mult, op1=ALU.subtract)
                    ins.then_inc(sm("sq_lo"), 1)

                def row_max(w):
                    g = w // 8
                    W = P if w % 8 == 0 else 256
                    s4 = st[:, w % 4, :]
                    b = 2 * (w % 2)
                    dve.wait_ge(sm("s_mm"), l * 16 + w + 1)
                    dve.tensor_reduce(s4[:, 0:4], ps[:, b:b + 2, :].rearrange("p b (h n) -> p (b h) n", h=2)[:, :, 0:W], AX.X, ALU.max,
                                      negate=True).then_inc(sm("s_nm"), 1)
                    dve.wait_ge(sm("s_nm"), l * 16 + w + 1)
                    dve.tensor_tensor(s4[:, 4:8], s4[:, 0:4], nsnk[:, 4 * g:4 * g + 4], ALU.min).then_inc(sm("s_mn"), 1)
                    dve.wait_ge(sm("s_mn"), l * 16 + w + 1)
                    dve.tensor_tensor(s4[:, 12:16], s4[:, 4:8], snk[:, 4 * g:4 * g + 4], ALU.add).then_inc(sm("s_smx"), 1)

                def normalize(w):
                    W = P if w % 8 == 0 else 256
                    s4 = st[:, w % 4, :]
                    dve.wait_ge(sm("s_exp"), l * 16 + w + 1)
                    dve.wait_ge(sm("s_es"), l * 16 + w + 1)
                    dve.tensor_tensor(s4[:, 16:20], s4[:, 8:12], s4[:, 12:16], ALU.add).then_inc(sm("s_den"), 1)
                    dve.wait_ge(sm("s_den"), l * 16 + w + 1)
                    dve.reciprocal(s4[:, 16:20], s4[:, 16:20]).then_inc(sm("s_rd"), 1)
                    dve.wait_ge(sm("s_rd"), l * 16 + w + 1)
                    pv = pbuf[w % 2][:, 0:4 * W].rearrange("p (h n) -> p h n", h=4)
                    dve.tensor_tensor(pv, pv, s4[:, 16:20][:, :, None].broadcast_to([P, 4, W]), ALU.mult).then_inc(sm("s_norm"), 1)

                def pt_lo(w):
                    nk = 1 if w % 8 == 0 else 2
                    dve.wait_ge(sm("st_hi"), l * 16 + w + 1)
                    dve.tensor_tensor(sptl[w % 2][:, 0:nk, :, :].rearrange("p k h n -> p k (h n)"), ps[:, 4:4 + nk, :],
                                      spth[w % 2][:, 0:nk, :, :].rearrange("p k h n -> p k (h n)").bitcast(F32), ALU.subtract).then_inc(sm("st_lo"), 1)

                def o_lo(w):
                    g, i = w // 8, w % 8
                    dve.wait_ge(sm("so_hi"), l * 16 + w + 1)
                    dve.tensor_tensor(hl[:, 2 * g:2 * g + 2, i * P:(i + 1) * P], ps[:, 6 + w % 2, 0:256].rearrange("p (t n) -> p t n", t=2),
                                      hh[:, 2 * g:2 * g + 2, i * P:(i + 1) * P].bitcast(F32), ALU.subtract).then_inc(sm("so_lo"), 1)

                dve.wait_ge(sm("nsnk_ok"), l + 1)
                k_lo(0)
                q_lo(0)
                q_lo(1)
                for w in range(-1, 18):
                    if 0 <= w + 1 < 16:
                        row_max(w + 1)
                    if 0 <= w - 1 < 16:
                        pt_lo(w - 1)
                    if 0 <= w + 1 < 16:
                        normalize(w + 1)
                    if 0 <= w - 2 < 16:
                        o_lo(w - 2)
                    if 2 <= w + 3 < 16:
                        q_lo(w + 3)
                    if w == -1:
                        v_lo(0)
                    if w == 0:
                        k_lo(1)
                    if w == 8:
                        v_lo(1)

                def stack_lo(t, h, part):
                    pr = l * 4 + t
                    r, ro_ = slice(64 * h, 64 * h + 64), slice(64 - 64 * h, 128 - 64 * h)
                    t1 = bass.ds(t, 1)
                    dve.wait_ge(sm("fq_hi"), pr * 8 + 4 * h + 2 * part + 2)
                    if part == 0:
                        dve.scalar_tensor_tensor(out=q1[h][ro_, :], in0=qf[r, t1, 0:SEQ].rearrange("p t n -> p (t n)"), scalar=SCALE,
                                                 in1=q1[h][r, :].bitcast(F32), op0=ALU.mult, op1=ALU.subtract).then_inc(sm("fq_lo"), 1)
                    else:
                        dve.tensor_tensor(k2[h][0:64, :], kf[r, t1, 0:SEQ].rearrange("p t n -> p (t n)"), k1[h][r, :].bitcast(F32),
                                          ALU.subtract).then_inc(sm("fq_lo"), 1)

                def row_max(t, e):
                    pr = l * 4 + t
                    i = FOX_ORDER[e % 8]
                    n, nb = (i + 1) * P, (1 if i < 4 else 2)
                    b = 2 * (e % 2)
                    dve.wait_ge(sm("fs_mm"), pr * 16 + e + 1)
                    dve.tensor_reduce(st[:, e % 4, 0:1], ps[:, b:b + nb, 0:n // nb], AX.XY, ALU.max, negate=True).then_inc(sm("fs_nm"), 1)

                def normalize(t, e):
                    pr = l * 4 + t
                    i = FOX_ORDER[e % 8]
                    n = (i + 1) * P
                    s4 = st[:, e % 4, :]
                    dve.wait_ge(sm("fs_exp"), pr * 16 + e + 1)
                    dve.reciprocal(s4[:, 2:3], s4[:, 1:2]).then_inc(sm("fs_rd"), 1)
                    dve.wait_ge(sm("fs_rd"), pr * 16 + e + 1)
                    dve.tensor_scalar(pbuf[e % 2][:, 0:n], pbuf[e % 2][:, 0:n], s4[:, 2:3], None, ALU.mult).then_inc(sm("fs_norm"), 1)

                def pt_lo(t, e):
                    pr = l * 4 + t
                    i = FOX_ORDER[e % 8]
                    jb = (e // 2) % 2
                    for bb in range(NBT[e]):
                        g = BT[e] + bb
                        k0, k1_ = 4 * bb, min(4 * bb + 4, i + 1)
                        dve.wait_ge(sm("ft_hi"), pr * 24 + g + 1)
                        dve.tensor_tensor(ptl[jb][:, k0:k1_, (i % 2) * P:(i % 2 + 1) * P],
                                          ps[:, 4 + g % 2, 0:(k1_ - k0) * P].rearrange("p (k n) -> p k n", n=P),
                                          pth[jb][:, k0:k1_, (i % 2) * P:(i % 2 + 1) * P].bitcast(F32), ALU.subtract).then_inc(sm("ft_lo"), 1)

                def o_lo(t, b):
                    dve.wait_ge(sm("fo_hi"), (l * 4 + t) * 2 + b + 1)
                    c0 = (512, 0)[b]
                    t4 = bass.ds(t + 4, 1)
                    dve.tensor_tensor(hl[:, t4, c0:c0 + 512].rearrange("p t n -> p (t n)"), ps[:, 6 + b, :],
                                      hh[:, t4, c0:c0 + 512].rearrange("p t n -> p (t n)").bitcast(F32), ALU.subtract).then_inc(sm("fo_lo"), 1)

                def fox_pair(t, first, last):
                    for e in range(16):
                        if e < 15:
                            row_max(t, e + 1)
                        elif not last:
                            row_max(t + 1, 0)
                        if e >= 1:
                            pt_lo(t, e - 1)
                        elif not first:
                            pt_lo(t - 1, 15)
                        if e < 15:
                            normalize(t, e + 1)
                        elif not last:
                            normalize(t + 1, 0)
                        if e in (3, 4):
                            stack_lo(t, 1, e - 3)
                        if e == 1:
                            dve.wait_ge(sm("fv_hi"), l * 4 + t + 1)
                            half = lambda t_: t_[:, :, :].rearrange("p t (a n) -> p t a n", n=64)[:, :, 0:3:2, :]
                            dve.tensor_tensor(half(fvl), vf[:, 0:TT, bass.ds(t * P, P)].rearrange("p t (a n) -> p t a n", n=64),
                                              half(fvh).bitcast(F32), ALU.subtract).then_inc(sm("fv_lo"), 1)
                            if not first:
                                o_lo(t - 1, 1)
                        if e in (9, 10) and not last:
                            stack_lo(t + 1, 0, e - 9)
                        if e == 13:
                            o_lo(t, 0)

                stack_lo(0, 0, 0)
                stack_lo(0, 0, 1)
                row_max(0, 0)
                normalize(0, 0)
                dve.wait_ge(sm("mod_mm"), 2 * (l + 1))
                dve.tensor_tensor(mod[:, 2 * N_ADA1:48, :], ps[:, 7, 0:96 - 4 * N_ADA1].rearrange("p (j s) -> p j s", s=2),
                                  vt[:, 2 * N_ADA1:48][:, :, None].broadcast_to([P, 48 - 2 * N_ADA1, 2]), ALU.add).then_inc(sm("ada_ev"), 1)
                dve.wait_ge(sm("ada_ev"), 2 * (l + 1))
                coefs([1, 2, 3])
                fox_pair(0, True, False)
                with dve.Fori(1, 3) as t:
                    fox_pair(t, False, False)
                fox_pair(3, False, True)
                pt_lo(3, 15)
                o_lo(3, 1)

                for w in range(4):
                    W = WIN + NEW if w < 2 else PAST + NEW
                    s4 = st[:, w, :]
                    dve.wait_ge(sm("a_mm"), l * 4 + w + 1)
                    if w < 2:
                        dve.tensor_reduce(s4[:, 0:1], ps[:, w % 2, 0:W], AX.X, ALU.max, negate=True).then_inc(sm("a_nm"), 1)
                        dve.wait_ge(sm("a_nm"), l * 2 + w + 1)
                        dve.tensor_tensor(s4[:, 1:2], s4[:, 0:1], ssnk[:, 1, w:w + 1], ALU.min).then_inc(sm("a_mn"), 1)
                        dve.wait_ge(sm("a_mn"), l * 4 + w + 1)
                        dve.tensor_tensor(s4[:, 3:4], s4[:, 1:2], ssnk[:, 0, w:w + 1], ALU.add).then_inc(sm("a_smx"), 1)
                        dve.wait_ge(sm("a_es"), l * 2 + w + 1)
                        dve.wait_ge(sm("a_exp"), l * 4 + w + 1)
                        dve.tensor_tensor(s4[:, 4:5], s4[:, 2:3], s4[:, 3:4], ALU.add).then_inc(sm("a_den"), 1)
                        dve.wait_ge(sm("a_den"), l * 2 + w + 1)
                        dve.reciprocal(s4[:, 5:6], s4[:, 4:5]).then_inc(sm("a_rd"), 1)
                    else:
                        dve.tensor_reduce(s4[:, 1:2], ps[:, w % 2, 0:W], AX.X, ALU.max, negate=True).then_inc(sm("a_mn"), 1)
                        dve.wait_ge(sm("a_exp"), l * 4 + w + 1)
                        dve.reciprocal(s4[:, 5:6], s4[:, 2:3]).then_inc(sm("a_rd"), 1)
                    dve.wait_ge(sm("a_rd"), l * 4 + w + 1)
                    dve.tensor_scalar(ap[:, 0:W], ap[:, 0:W], s4[:, 5:6], None, ALU.mult).then_inc(sm("a_norm"), 1)
                    if w in (1, 2):
                        split_lo(l, W_WO0 + w - 1)
                    if w % 2:
                        t0 = 0 if w < 2 else 4
                        dve.wait_ge(sm("ao_hi"), 2 * l + w // 2 + 1)
                        dve.tensor_tensor(hl[:, t0:t0 + 4, SEQ:TOK], ps[:, 3, 0:P].rearrange("p (t n) -> p t n", t=4),
                                          hh[:, t0:t0 + 4, SEQ:TOK].bitcast(F32), ALU.subtract).then_inc(sm("ao_lo"), 1)

                split_lo(l, W_WO0 + 2)
                split_lo(l, W_WO0 + 3)
                post_norm(l, NPOST1, 0)
                post_norm(l, NPOST1, 1)
                split_lo(l, W_MLP0)
                post_norm(l, NPOST1, 2)
                pre_scale(l, NPRE2, 0)
                pre_scale(l, NPRE2, 1)
                pre_lo(l, NPRE2, 0)
                pre_scale(l, NPRE2, 2)
                pre_lo(l, NPRE2, 1)
                pre_lo(l, NPRE2, 2)

                wait_apart(dve, ("const_in", 64), ("y_zero", l + 1))

                def mlp_step(m, last):
                    mm = dve.snap(l * MSTEPS + m)
                    n0 = dve.snap(l * NW + W_MLP0 + m * 4)

                    def u_square(q):
                        dve.wait_ge(sm("u_relu"), mm * 12 + q + 1)
                        dve.wait_ge(sm("u_ok"), mm * 12 + max(0, q - 1))
                        dve.tensor_tensor(u_t[q % 2][:, :], r_t[q % 2][:, :], r_t[q % 2][:, :], ALU.mult).then_inc(sm("u_sq"), 1)

                    def u_lo(q):
                        c = q % 3
                        cs = slice(c * CH, (c + 1) * CH)
                        dve.wait_ge(sm("u_hi"), mm * 12 + q + 1)
                        dve.tensor_tensor(ul[:, q // 3, cs], u_t[q % 2][:, :], uh[:, q // 3, cs].bitcast(F32), ALU.subtract).then_inc(sm("u_ok"), 1)

                    split_lo(l, W_MLP0 + 1, n0 + 1)
                    for q in range(12):
                        if q == 6:
                            split_lo(l, W_MLP0 + 2, n0 + 2)
                        u_square(q)
                        if q >= 1:
                            u_lo(q - 1)
                    u_lo(11)
                    dve.wait_ge(sm("d_add"), mm * 24)
                    for q in range(24):
                        if q == 0:
                            split_lo(l, W_MLP0 + 3, n0 + 3)
                        if q == 14 and not last:
                            split_lo(l, W_MLP0 + 4, n0 + 4)
                        kt, c = (q % 8, q // 8) if last else (q // 3, q % 3)
                        cs = slice(c * CH, (c + 1) * CH)
                        dve.wait_ge(sm("d_mm"), mm * 24 + q + 1)
                        dve.tensor_tensor(y[:, kt, cs], ps[:, DB[last][q], 0:CH], y[:, kt, cs], ALU.add).then_inc(sm("d_add"), 1)
                        if last and q == 20:
                            post_norm(l, NPOST2, 0)

                with dve.Fori(0, MSTEPS - 1) as m:
                    mlp_step(m, False)
                mlp_step(MSTEPS - 1, True)
                post_norm(l, NPOST2, 1)
                post_norm(l, NPOST2, 2)

            for i in range(TT + 1):
                dve.wait_ge(sm("fin_tr"), 2 * i + 2)
                if i >= 8:
                    dve.wait_ge(sm("fin_out0"), 16)
                dve.tensor_copy(orow[i % 8][:, 512:1024], ps[:, (2 * i + 1) % 4, :]).then_inc(sm("fin_ev1"), 1)

        @block.tensor
        def _(pe):
            def three(out, w_hi, w_lo, m_hi, m_lo, k, nk, start=True, stop=True):
                pe.matmul(out, w_hi, m_hi, start=start and k == 0, stop=False)
                pe.matmul(out, w_hi, m_lo, start=False, stop=False)
                return pe.matmul(out, w_lo, m_hi, start=False, stop=stop and k == nk - 1)

            pe.wait_ge(sm("const_in"), 64)
            pe.wait_ge(sm("c_in"), 16)
            pe.transpose(ps[:, 7, 0:16], crow[:, :], ident[0:16, 0:16]).then_inc(sm("c_tr"), 1)
            for i in range(TT + 1):
                pe.wait_ge(sm(f"xrow_in{i % 8}"), 16 * (i // 8 + 1))
                w = P if i < TT else NEW
                for hf in range(2):
                    q = 2 * i + hf
                    if q >= 4:
                        pe.wait_ge(sm("x_put"), q - 3)
                    for k in range(4):
                        ins = pe.transpose(ps[:, q % 4, k * w:(k + 1) * w], xrow[i % 8][0:w, (4 * hf + k) * P:(4 * hf + k + 1) * P], ident[0:w, 0:w])
                    ins.then_inc(sm("x_tr"), 1)
            pe.wait_ge(sm("zero_ok"), 1)
            pe.wait_ge(sm("cb_ok"), 1)
            pe.wait_ge(sm("silu_b"), 3)
            pe.wait_ge(sm("x_ready"), NCH)

            def mean(l, nu, c):
                idx, s = l * 12 + nu * 3 + c, (nu * 3 + c) % 2
                pe.wait_ge(sm("sq_ok"), idx + 1)
                pe.wait_ge(sm("ln_ok"), idx - 1 if nu * 3 + c else idx)
                for k in range(KT):
                    ins = pe.matmul(ps[:, 4 + s, 0:CH], onesd[:, :], sq[:, k, c * CH:(c + 1) * CH], start=(k == 0), stop=(k == KT - 1))
                ins.then_inc(sm("mean_ok"), 1)

            def modulate(out, w):
                for k in range(KT):
                    ins = pe.matmul(out, sc[:, :, k], w[:, k * 256:(k + 1) * 256], start=(k == 0), stop=(k == KT - 1), skip_group_check=True)
                ins.then_inc(sm("ada_mm"), 1)

            def mod_columns(out, rows):
                for j in range(2):
                    ins = pe.matmul(out[:, 2 * j:2 * j + 2], rows[:, j * P:(j + 1) * P], ident[0:2, 0:2], start=(j == 0), stop=(j == 1),
                                    skip_group_check=True)
                return ins

            with pe.Fori(0, DEPTH) as l:
                wait_apart(pe, ("zero_ok", 1), ("ln_ok", l * 12), ("d_add", l * MSTEPS * 24))
                seen = {}
                for b in range(N_ADA1):
                    slot = ADA_SLOT[b]
                    seen[slot] = seen.get(slot, 0) + 1
                    pe.wait_ge(sm(f"ada_in{slot}"), (l * ADA_SLOT.count(slot) + seen[slot]) * 16)
                    modulate(ps[0:2, b // 2, (b % 2) * 256:(b % 2) * 256 + 256], ada_w[slot])
                pe.wait_ge(sm("vrow_in"), (l + 1) * 32)
                pe.transpose(ps[:, 7, 0:80], vrow[:, :], ident[0:80, 0:80]).then_inc(sm("v_tr"), 1)
                mean(l, NPRE1, 0)
                for b in range(N_ADA1):
                    pe.wait_ge(sm("mrow4_ok"), l * 2 + b // 4 + 1)
                    ins = mod_columns(ps[:, 6, 4 * b:4 * b + 4], mrow4[b // 4][:, (b % 4) * 256:(b % 4 + 1) * 256])
                ins.then_inc(sm("mod_mm"), 1)
                mean(l, NPRE1, 1)
                mean(l, NPRE1, 2)


                def transposes(nr):
                    u, i = ROPES[nr]
                    src = rk[i - TT + 1] if u == U_KV and i >= TT - 1 else ro[nr % 2]
                    pe.wait_ge(sm("rope_ok"), l * NR + nr + 1)
                    if nr >= 2:
                        pe.wait_ge(sm("rtr_ev"), l * NR + nr - 1)
                    for j in range(1 if u == U_KV else 2):
                        ins = pe.transpose(ps[:, 4 + nr % 2, j * P:(j + 1) * P], src[:, j * P:(j + 1) * P], ident[:, :])
                    ins.then_inc(sm("rtr_mm"), 1)

                def ko_transposes(i):
                    if i >= 2:
                        pe.wait_ge(sm("ko_ev"), l * (TT + 1) + i - 1)
                    else:
                        pe.wait_ge(sm("f_lo"), 2 * l + i + 1)
                    t0 = i * P if i < TT else TAIL
                    for t in range(4):
                        ins = pe.transpose(ps[:, 6 + i % 2, t * P:(t + 1) * P], kf[:, t, t0:t0 + P], ident[:, :])
                    ins.then_inc(sm("ko_mm"), 1)

                def cumulate():
                    pe.wait_ge(sm("logf_ok"), l + 1)
                    pe.wait_ge(sm("lcum_ok"), (l + 1) * TT)
                    for i in range(TT):
                        out = ps[0:NH_F, 6 + i // 4, (i % 4) * P:(i % 4 + 1) * P]
                        pe.matmul(out, logf[:, i, :], tri[:, :], start=(i % 4 == 0), stop=False, skip_group_check=True)
                        ins = pe.matmul(out, lcum[:, i, :], onesd[:, :], start=False, stop=(i % 4 == 3), skip_group_check=True)
                    ins.then_inc(sm("f_mm"), 1)

                pending = None
                for q, it in enumerate(PJ):
                    b, n = q % 4, n_of(it)
                    if q >= 4:
                        pe.wait_ge(sm("ev_act"), l * n_act(NPJ) + n_act(q - 3))
                        if by_dve(PJ[q - 4]):
                            _, u4, i4 = PJ[q - 4]
                            if u4 >= U_KV:
                                pe.wait_ge(sm("rope_t"), l * NR + (u4 - U_KV) * (TT + 1) + i4 + 1)
                            else:
                                pe.wait_ge(sm("fg_a"), l * 10 + i4 + 1)
                    pe.wait_ge(sm("w_lo"), l * NW + n + 1)
                    whv, wlv = w_view(wh[n % 2], n), w_view(wl[n % 2], n)
                    if it[0] == "t":
                        _, u, i = it
                        w = TM_COLS[u][1]
                        t0 = i * P if i < TT else TAIL
                        ts = slice(t0, t0 + P)
                        for k in range(KT):
                            ins = three(ps[:, b, 0:w], hh[:, k, ts], hl[:, k, ts], whv[:, k, :], wlv[:, k, :], k, KT)
                    else:
                        _, blk, j, c = it
                        cs = slice(c * CH, (c + 1) * CH)
                        if blk == 0:
                            pe.wait_ge(sm("h_ok"), l * 6 + c + 1)
                        for k in range(KT):
                            ins = three(ps[:, b, 0:CH], whv[:, k, j * P:(j + 1) * P], wlv[:, k, j * P:(j + 1) * P],
                                        hh[:, k, cs], hl[:, k, cs], k, KT)
                    ins.then_inc(sm("pj_mm"), 1)
                    if ends(q):
                        if q == NPJ - 1:
                            pe.wait_ge(sm("ko_ev"), l * (TT + 1) + 6)
                        pe.matmul(ps[:, 7, 0:32], zerob[:, :], identb[:, 0:32], start=True, stop=True).then_inc(sm("w_used"), 1)
                    if pending is not None:
                        transposes(pending)
                        pending = None
                    if it[0] == "t" and it[1] == N_TM - 1:
                        if it[2] == 0:
                            cumulate()
                        else:
                            ko_transposes(it[2] - 1)
                    if it[0] == "t" and it[1] >= U_KV:
                        pending = (it[1] - U_KV) * (TT + 1) + it[2]
                transposes(pending)
                ko_transposes(TT)

                def scores(w):
                    g, i = w // 8, w % 8
                    W = P if i == 0 else 256
                    k0 = 0 if i == 0 else (i - 1) * P
                    pe.wait_ge(sm("sq_lo"), l * 16 + w + 1)
                    pe.wait_ge(sm("sk_lo"), l * 2 + g + 1)
                    if w >= 2:
                        pe.wait_ge(sm("s_exp"), l * 16 + w - 1)
                    for bb in range(2):
                        bank = 2 * (w % 2) + bb
                        view = ps[:, bank, :].rearrange("p (h n) -> p h n", h=2)
                        msk = winb[:, 256 - W:256]
                        for h in range(2):
                            pe.matmul(view[:, h, 0:W], identb, msk, start=(h == 0), stop=False, skip_group_check=True)
                        for h in range(2):
                            hd = 2 * h + bb
                            r = slice(64 * bb, 64 * bb + 64)
                            pe.matmul(view[:, h, 0:W], sq1[w % 2][:, hd, :], sk1[g][:, k0:k0 + W], start=False, stop=False, skip_group_check=True)
                            ins = pe.matmul(view[:, h, 0:W], sq1[w % 2][r, hd, :], sk2[g][r, k0:k0 + W], start=False, stop=(h == 1), skip_group_check=True)
                    ins.then_inc(sm("s_mm"), 1)

                def p_transposes(w):
                    W = P if w % 8 == 0 else 256
                    pe.wait_ge(sm("s_norm"), l * 16 + w + 1)
                    pe.wait_ge(sm("st_lo"), l * 16 + w)
                    for kb in range(W // P):
                        for hd in range(4):
                            ins = pe.transpose(ps[:, 4 + kb, hd * P:(hd + 1) * P], pbuf[w % 2][:, hd * W + kb * P:hd * W + (kb + 1) * P], ident[:, :])
                    ins.then_inc(sm("st_mm"), 1)

                def products(w):
                    g, i = w // 8, w % 8
                    if w >= 2:
                        pe.wait_ge(sm("so_lo"), l * 16 + w - 1)
                    pe.wait_ge(sm(f"ada_v_in{w % 2}"), (l * 8 + w // 2 + 1) * 16)
                    modulate(ps[0:2, 6 + w % 2, 256:512], ada_v[w % 2])
                    pe.wait_ge(sm("st_lo"), l * 16 + w + 1)
                    pe.wait_ge(sm("sv_lo"), l * 2 + g + 1)
                    kbs = [0] if i == 0 else [i - 1, i]
                    todo = [(kb, d) for kb in range(len(kbs)) for d in range(2)]
                    for x, (kb, d) in enumerate(todo):
                        vsl = slice(64 * d, 64 * d + P)
                        out = ps[:, 6 + w % 2, 0:256]
                        ins = three(out, svh[:, kbs[kb], vsl], svl[:, kbs[kb], vsl],
                                    spth[w % 2][:, kb, 2 * d:2 * d + 2, :], sptl[w % 2][:, kb, 2 * d:2 * d + 2, :], x, len(todo))
                    ins.then_inc(sm("so_mm"), 1)

                pe.wait_ge(sm("sz_ok"), 2 * (l + 1))
                pe.wait_ge(sm("f_lo"), 2 * (l + 1))
                pe.wait_ge(sm("ko_ev"), (l + 1) * (TT + 1))
                pe.wait_ge(sm("rtr_ev"), (l + 1) * NR)
                for w in range(-2, 17):
                    if 0 <= w + 2 < 16:
                        scores(w + 2)
                    if 0 <= w < 16:
                        p_transposes(w)
                    if 0 <= w - 1 < 16:
                        products(w - 1)

                wait_apart(pe, ("zero_ok", 1), ("so_lo", (l + 1) * 16), ("fz_ok", 5 * (l + 1)))

                def scores(t, e, first=False):
                    pr = l * 4 + t
                    h, i = e // 8, FOX_ORDER[e % 8]
                    n, nb = (i + 1) * P, (1 if i < 4 else 2)
                    w = n // nb
                    if e % 8 == 0:
                        pe.wait_ge(sm("fq_lo"), pr * 4 + 2 * h + 2)
                        pe.wait_ge(sm(f"frow_in{h}"), (pr + 1) * 32)
                    pe.wait_ge(sm("fs_exp"), pr * 16 + (max(0, e - 1) if first else e - 1))
                    qb = slice(i * P, (i + 1) * P)
                    for c in range(nb):
                        out = ps[:, 2 * (e % 2) + c, 0:w]
                        pe.matmul(out, q1[h][:, qb], k1[h][:, c * w:(c + 1) * w], start=True, stop=False)
                        pe.matmul(out, q2[h][0:68, qb], k2[h][0:68, c * w:(c + 1) * w], start=False, stop=(c < nb - 1))
                    pe.matmul(ps[:, 2 * (e % 2) + nb - 1, w - P:w], identb, causb, start=False, stop=True).then_inc(sm("fs_mm"), 1)

                def p_transposes(t, e, first):
                    pr = l * 4 + t
                    i = FOX_ORDER[e % 8]
                    pe.wait_ge(sm("fs_norm"), pr * 16 + e + 1)
                    for bb in range(NBT[e]):
                        g = BT[e] + bb
                        pe.wait_ge(sm("ft_lo"), pr * 24 + (max(0, g - 1) if first else g - 1))
                        k0, k1_ = 4 * bb, min(4 * bb + 4, i + 1)
                        for kb in range(k0, k1_):
                            ins = pe.transpose(ps[:, 4 + g % 2, (kb - k0) * P:(kb - k0 + 1) * P], pbuf[e % 2][:, kb * P:(kb + 1) * P], ident[:, :])
                        ins.then_inc(sm("ft_mm"), 1)

                def products(t, jj):
                    pr = l * 4 + t
                    h, J, jb = jj // 4, 3 - jj % 4, jj % 2
                    bank, half = (6, J - 2) if J >= 2 else (7, J)
                    if h == 0 and J in (3, 1):
                        pe.wait_ge(sm("fo_lo"), pr * 2)
                        pe.wait_ge(sm("ada_ev"), 2 * (l + 1))
                        pe.matmul(ps[:, bank, :], zerob[:, :], cb[:, :], start=True, stop=False, skip_group_check=True)
                    pe.wait_ge(sm("ft_lo"), pr * 24 + BT[2 * jj + 2])
                    if jj == 0:
                        pe.wait_ge(sm("fv_lo"), pr + 1)
                    vsl = slice(64 * h, 64 * h + P)
                    for kb in range(2 * J + 2):
                        q0 = P if kb == 2 * J + 1 else 0
                        out = ps[:, bank, half * 256 + q0:half * 256 + 256]
                        mh, ml = pth[jb][:, kb, q0:256], ptl[jb][:, kb, q0:256]
                        for wv, mv in ((fvh, mh), (fvh, ml), (fvl, mh)):
                            ins = pe.matmul(out, wv[:, kb, vsl], mv, start=False, stop=(kb == 2 * J + 1 and wv is fvl), skip_group_check=True)
                    ins.then_inc(sm("pv_mm"), 1)

                def fox_pair(t, first, last):
                    for e in range(16):
                        if e < 14:
                            scores(t, e + 2)
                        elif not last:
                            scores(t + 1, e - 14)
                        p_transposes(t, e, first)
                        if e % 2 == 0 and e >= 2:
                            products(t, e // 2 - 1)
                        elif e == 0 and not first:
                            products(t - 1, 7)

                scores(0, 0, True)
                scores(0, 1, True)
                for b in range(16):
                    ins = mod_columns(ps[:, 7, 4 * b:4 * b + 4], mrow[b // 8][:, (b % 8) * 256:(b % 8 + 1) * 256])
                ins.then_inc(sm("mod_mm"), 1)
                fox_pair(0, True, False)
                with pe.Fori(1, 3) as t:
                    fox_pair(t, False, False)
                fox_pair(3, False, True)
                products(3, 7)

                pe.wait_ge(sm("cache_in"), (l + 1) * 80)
                pe.wait_ge(sm("lcs_ok"), 2 * (l + 1))
                pe.wait_ge(sm("ft_lo"), (l + 1) * 96)
                pe.wait_ge(sm("fo_lo"), (l + 1) * 8)
                for c in range(2):
                    for t in range(4):
                        pe.transpose(ps[:, c, t * P:(t + 1) * P], ckf[:, c, t * P:(t + 1) * P], ident[:, :])
                for g in range(2):
                    pe.transpose(ps[:, 2, g * P:(g + 1) * P], cks[:, g, :, :].rearrange("p d e -> p (d e)"), ident[:, :])
                pe.matmul(ps[0:NH_F, 3, 0:P], lc[:, 0, :], tri[:, :], start=True, stop=False, skip_group_check=True)
                pe.matmul(ps[0:NH_F, 3, P:2 * P], lc[:, 1, :], tri[:, :], start=False, stop=False, skip_group_check=True)
                pe.matmul(ps[0:NH_F, 3, P:2 * P], lcs[:, 0, :], onesd[:, :], start=False, stop=False, skip_group_check=True)
                pe.matmul(ps[0:NH_F, 3, 2 * P:2 * P + NEW], logf[NEWP:P, TT, :], tri[NEWP:P, NEWP:P], start=False, stop=False, skip_group_check=True)
                pe.matmul(ps[0:NH_F, 3, 2 * P:2 * P + NEW], lcs[:, 1, :], onesd[:, 0:NEW], start=False, stop=True,
                          skip_group_check=True).then_inc(sm("ck_tr"), 1)
                for w in range(4):
                    pe.wait_ge(sm("zero_ok"), 1)
                    pe.wait_ge(sm("ck_ev"), l + 1)
                    pe.wait_ge(sm("aq_ok"), 2 * (l + 1))
                    W = WIN + NEW if w < 2 else PAST + NEW
                    if w >= 2:
                        pe.wait_ge(sm("a_exp"), l * 4 + w - 1)
                    for hd in range(4):
                        h = 4 * (w % 2) + hd
                        r = slice(64 * (h % 2), 64 * (h % 2) + 64)
                        out = ps[32 * hd:32 * hd + 32, w % 2, 0:W]
                        qn = aqs[r, (0 if w < 2 else 4) + h // 2, :]
                        if w < 2:
                            ins = pe.matmul(out, qn, kst[r, w, :], start=True, stop=True)
                            continue
                        pe.matmul(out, qn, kft[r, h // 2, :], start=True, stop=False)
                        pe.matmul(out, ident[0:NH_F, h:h + 1].broadcast_to([NH_F, NEW]), fsn[:, :], start=False, stop=False)
                        pe.matmul(out, fs[:, PAST:], ident[0:NH_F, h:h + 1].broadcast_to([NH_F, W]), start=False, stop=False)
                        ins = pe.matmul(out[:, PAST:W], identb[0:NEW, 0:NEW], causb[0:NEW, 0:NEW], start=False, stop=True)
                    ins.then_inc(sm("a_mm"), 1)
                    pe.wait_ge(sm("a_norm"), l * 4 + w + 1)
                    if w >= 1:
                        pe.wait_ge(sm("at_ev"), l * 4 + w)
                    starts = [0, NEW] if w < 2 else [0, P, PAST + NEW - P]
                    for kb, c0 in enumerate(starts):
                        ins = pe.transpose(ps[:, 2, kb * P:(kb + 1) * P], ap[:, c0:c0 + P], ident[:, :])
                    ins.then_inc(sm("at_mm"), 1)
                    pe.wait_ge(sm("at_ev"), l * 4 + w + 1)
                    if w == 2:
                        pe.wait_ge(sm("ao_lo"), 2 * l + 1)
                    for hd in range(4):
                        h = 4 * (w % 2) + hd
                        out = ps[64 * (h % 2):64 * (h % 2) + 64, 3, (h // 2) * NEW:(h // 2 + 1) * NEW]
                        pc = slice(hd * NEW, (hd + 1) * NEW)
                        if w < 2:
                            pe.matmul(out, cvs[:, 64 * w:64 * w + 64], apt[:, 0, pc], start=True, stop=False)
                            ins = pe.matmul(out, vs_new[NEWP:P, 64 * w:64 * w + 64], apt[NEWP:P, 1, pc], start=False, stop=True)
                        else:
                            for kb in range(2):
                                pe.matmul(out, cvf[:, kb, h * HD:(h + 1) * HD], apt[:, kb, pc], start=(kb == 0), stop=False)
                            ins = pe.matmul(out, vf[NEWP:P, TT, h * HD:(h + 1) * HD], apt[NEWP:P, 2, pc], start=False, stop=True)
                    ins.then_inc(sm("ao_mm"), 1)

                def step(n, out, b, j, cs, k, nk, m_hi, m_lo):
                    whv, wlv = w_view(wh[n % 2], n), w_view(wl[n % 2], n)
                    js = slice(j * P, (j + 1) * P)
                    return three(out, whv[:, k, js], wlv[:, k, js], m_hi[:, k, cs], m_lo[:, k, cs], k, nk)

                def free_slots(bank, n=1):
                    pe.matmul(ps[:, bank, 0:32], zerob[:, :], identb[:, 0:32], start=True, stop=True).then_inc(sm("w_used"), n)

                pe.wait_ge(sm("ao_lo"), 2 * (l + 1))
                for r in range(2):
                    n0 = l * NW + W_WO0 + r * 2
                    for q in range(12):
                        b, j, c = (q // 6, (q // 3) % 2, q % 3) if r == 0 else ((q // 2) % 2, q % 2, q // 4)
                        pe.wait_ge(sm("w_lo"), n0 + b + 1)
                        if r * 12 + q >= 4:
                            pe.wait_ge(sm("y_ev"), l * 24 + r * 12 + q - 3)
                        for k in range(KT):
                            ins = step(W_WO0 + b, ps[:, q % 4, 0:CH], b, j, slice(c * CH, (c + 1) * CH), k, KT, hh, hl)
                        ins.then_inc(sm("y_mm"), 1)
                        if r == 0 and q % 6 == 5:
                            free_slots(7)
                        if r == 1 and q in (5, 9):
                            mean(l, NPOST1, q // 4 - 1)
                free_slots(7, 2)
                mean(l, NPOST1, 2)
                for c in range(NCH):
                    mean(l, NPRE2, c)

                def mlp_step(m, last):
                    mm = pe.snap(l * MSTEPS + m)
                    n0 = pe.snap(l * NW + W_MLP0 + m * 4)
                    for q in range(12):
                        b, j, c = q // 6, (q // 3) % 2, q % 3
                        if q % 6 == 0:
                            pe.wait_ge(sm("w_lo"), n0 + b + 1)
                        if q < 3:
                            pe.wait_ge(sm("h_ok"), l * 6 + 4 + c)
                        pe.wait_ge(sm("u_relu"), mm * 12 + max(0, q - 3))
                        for k in range(KT):
                            ins = step(W_MLP0 + b, ps[:, q % 4, 0:CH], b, j, slice(c * CH, (c + 1) * CH), k, KT, hh, hl)
                        ins.then_inc(sm("u_mm"), 1)
                        if q % 6 == 5:
                            pe.wait_ge(sm("d_add"), mm * 24)
                            free_slots(7)
                    for q in range(24):
                        b, j, c = ((q // 4) % 2, q % 4, q // 8) if last else (q // 12, (q // 3) % 4, q % 3)
                        if q % 12 == 0 or last:
                            pe.wait_ge(sm("w_lo"), n0 + b + 3)
                        if q < 3 or last:
                            pe.wait_ge(sm("u_ok"), mm * 12 + 10 + c)
                        if last:
                            pe.wait_ge(sm("u_relu"), mm * 12 + 12)
                        pe.wait_ge(sm("d_add"), mm * 24 + max(0, q - 3))
                        for k in range(HG):
                            ins = step(W_MLP0 + 2 + b, ps[:, DB[last][q], 0:CH], b, j, slice(c * CH, (c + 1) * CH), k, HG, uh, ul)
                        ins.then_inc(sm("d_mm"), 1)
                        if q % 12 == 11 and not last:
                            free_slots(0)
                        if last and q in (13, 21):
                            mean(l, NPOST2, q // 8 - 1)

                with pe.Fori(0, MSTEPS - 1) as m:
                    mlp_step(m, False)
                mlp_step(MSTEPS - 1, True)
                free_slots(0, 2)
                mean(l, NPOST2, 2)

            pe.wait_ge(sm("x_ready"), DEPTH * 6 + 3)
            for i in range(TT + 1):
                t0 = i * P if i < TT else TAIL
                for hf in range(2):
                    q = 2 * i + hf
                    if q >= 4:
                        pe.wait_ge(sm(f"fin_ev{hf}"), i - 1)
                    for k in range(4):
                        ins = pe.transpose(ps[:, q % 4, k * P:(k + 1) * P], xr[:, 4 * hf + k, t0:t0 + P], ident[:, :])
                    ins.then_inc(sm("fin_tr"), 1)


def constants():
    k, q = np.arange(P)[:, None], np.arange(P)[None, :]
    caus = np.where(q > k, NEG, 0.0)
    w = np.arange(256)[None, :]
    win = np.where(((k < 64) & (w >= 192)) | ((k >= 64) & (w < 64)), NEG, 0.0)
    consts = np.concatenate([np.eye(P), np.full((P, P), 1.0 / D), (k <= q) * 1.0, caus, win], 1).astype(np.float32)
    half = HD // 2
    inv = np.float32(10000.0) ** (-np.arange(half, dtype=np.float32) / np.float32(half))
    pos = np.zeros((P, TT + 1), np.float32)
    pos[:, :TT] = np.arange(SEQ).reshape(TT, P).T
    pos[NEWP:, TT] = PAST + np.arange(NEW)
    ang = pos[:, :, None] * inv[None, None, :]
    return consts, np.cos(ang).astype(np.float32).reshape(P, -1), np.sin(ang).astype(np.float32).reshape(P, -1)


def kernel(x_prompt, x_sample, c_prompt, c_sample, cache_swa_k, cache_swa_v, cache_fox_k, cache_fox_v,
           cache_fox_logf, w_in, b_forget, sinks, w_out, w_up, w_down, w_ada, b_ada,
           g_pre_mix, g_post_mix, g_pre_mlp, g_post_mlp):
    import concourse.bacc as bacc
    from concourse.bass_utils import run_bass_kernel_spmd as run

    consts, cos, sin = constants()
    A = lambda x: np.ascontiguousarray(np.asarray(x))
    rows = lambda g: A(g).reshape(DEPTH, KT, P)
    sk = A(sinks)
    ins = {
        "x_prompt": A(x_prompt).reshape(SEQ, D), "x_sample": A(x_sample).reshape(NEW, D),
        "c_rows": np.concatenate([A(c_prompt).reshape(KT, P), A(c_sample).reshape(KT, P)]),
        "cache_swa_k": A(cache_swa_k).reshape(DEPTH, WIN, P), "cache_swa_v": A(cache_swa_v).reshape(DEPTH, WIN, P),
        "cache_fox_k": A(cache_fox_k).reshape(DEPTH, PAST, 512), "cache_fox_v": A(cache_fox_v).reshape(DEPTH, PAST, 512),
        "cache_fox_logf": A(cache_fox_logf).reshape(DEPTH, PAST, NH_F),
        "w_in": A(w_in), "w_out": A(w_out), "w_up": A(w_up), "w_down": A(w_down), "w_ada": A(w_ada),
        "b_ada": A(b_ada).reshape(DEPTH, 48, P),
        "gains": np.concatenate([rows(g_pre_mix), rows(g_post_mix), rows(g_pre_mlp), rows(g_post_mlp)], 1),
        "sinks_rows": np.repeat(sk[:, None, [0, 2, 1, 3, 4, 6, 5, 7]], P, 1), "bf_rows": np.repeat(A(b_forget)[:, None, :], P, 1),
        "sinks_sample": np.repeat(sk.reshape(DEPTH, 2, 4).transpose(0, 2, 1), NEW, 1),
        "consts": consts, "cos": cos, "sin": sin,
    }
    outs = {
        "y_prompt": (SEQ, D), "y_sample": (NEW, D),
        "p_swa_k": (DEPTH, WIN, P), "p_swa_v": (DEPTH, WIN, P),
        "p_fox_k": (DEPTH, SEQ, 512), "p_fox_v": (DEPTH, SEQ, 512), "p_fox_logf": (DEPTH, SEQ, NH_F),
        "s_swa_k": (DEPTH, WIN, P), "s_swa_v": (DEPTH, WIN, P),
        "s_fox_k": (DEPTH, NEW, 512), "s_fox_v": (DEPTH, NEW, 512), "s_fox_logf": (DEPTH, NEW, NH_F),
    }
    nc = bacc.Bacc("TRN2", target_bir_lowering=False, num_devices=1)
    a = {n: nc.dram_tensor(n, v.shape, mybir.dt.from_np(v.dtype), kind="ExternalInput").ap() for n, v in ins.items()}
    a |= {n: nc.dram_tensor(n, s, F32, kind="ExternalOutput").ap() for n, s in outs.items()}
    build(nc, a)
    r = run(nc, [ins], core_ids=[0]).results[0]
    kv = lambda n, s, h: r[n].reshape(DEPTH, 1, s, h, HD)
    return (r["y_prompt"].reshape(1, SEQ, D), r["y_sample"].reshape(1, NEW, D),
            kv("p_swa_k", WIN, NKV), kv("p_swa_v", WIN, NKV), kv("p_fox_k", SEQ, NH_F), kv("p_fox_v", SEQ, NH_F),
            r["p_fox_logf"].reshape(DEPTH, 1, SEQ, NH_F),
            kv("s_swa_k", WIN, NKV), kv("s_swa_v", WIN, NKV), kv("s_fox_k", NEW, NH_F), kv("s_fox_v", NEW, NH_F),
            r["s_fox_logf"].reshape(DEPTH, 1, NEW, NH_F))
```
